# Optimizing a Trainium2 kernel written in Bass

```python
import math
import jax, jax.numpy as jnp
from jax import lax
import numpy as np

D_MODEL = 1024
BATCH = 1
SEQ = 1024
DEPTH = 1
DEC_BATCH = 8
DEC_SEQ = 8
PAST_LEN = 256
PAGE_SIZE = 128

N_MEM = 256
A_HEADS = 4
A_QK_DIM = 64
A_V_DIM = 128
A_WIDTH = A_HEADS * A_V_DIM
G_HEADS = 4
G_K_DIM = 64
G_V_DIM = 128
G_WIDTH = G_HEADS * G_V_DIM
G_GATE_RANK = 16
G_GATE_TAU = 16.0
M_HEADS = 4
M_DIM = 128
M_WIDTH = M_HEADS * M_DIM
BRANCH_WIDTH = 512
N_BRANCH = 3
Q_BLOCK = 128
GLA_CHUNK = 64
EPS = 1e-6
IN_SIZES = (A_HEADS * 2 * A_QK_DIM, A_HEADS * 2 * A_QK_DIM, A_WIDTH, A_WIDTH,
            G_HEADS * G_K_DIM, G_HEADS * G_K_DIM, G_WIDTH, G_WIDTH, G_GATE_RANK,
            M_WIDTH, M_WIDTH, N_BRANCH * D_MODEL)
IN_COLS = sum(IN_SIZES)

kernel_name = "hybrid_diffattn_gla_memory_decode_step"

def rmsnorm(x, g):
    xf = x.astype(jnp.float32)
    y = xf * lax.rsqrt(jnp.mean(xf * xf, axis=-1, keepdims=True) + EPS) * g.astype(jnp.float32)
    return y.astype(x.dtype)

def alibi_slopes(n_heads):
    return jnp.exp2(-8.0 * jnp.arange(1, n_heads + 1, dtype=jnp.float32) / n_heads)

def diff_attention(q, k, v, q_pos, k_pos, lam, block):
    B, Tq, H, _, dk = q.shape
    nb = Tq // block
    scale = dk ** -0.5
    slopes = alibi_slopes(H)
    kf = k.astype(jnp.float32)
    vf = v.astype(jnp.float32)
    qb = q.reshape(B, nb, block, H, 2, dk).transpose(1, 0, 2, 3, 4, 5)
    pb = q_pos.reshape(nb, block)

    def one_block(args):
        qi, pi = args
        s = jnp.einsum('bqhcd,bkhcd->bhcqk', qi.astype(jnp.float32), kf) * scale
        dist = pi[:, None] - k_pos[None, :]
        bias = -slopes[:, None, None] * dist.astype(jnp.float32)[None]
        s = jnp.where((dist >= 0)[None, None, None], s + bias[None, :, None], -jnp.inf)
        p = jax.nn.softmax(s, axis=-1)
        a = p[:, :, 0] - lam * p[:, :, 1]
        return jnp.einsum('bhqk,bkhd->bqhd', a, vf)

    out = lax.map(one_block, (qb, pb))
    return out.transpose(1, 0, 2, 3, 4).reshape(B, Tq, H, v.shape[-1]).astype(v.dtype)

def gla_chunked(q, k, v, log_a, S0, chunk):
    B, T, H, dk = q.shape
    dv = v.shape[-1]
    nc = T // chunk

    def to_chunks(t):
        return t.astype(jnp.float32).reshape(B, nc, chunk, H, t.shape[-1]).transpose(1, 0, 3, 2, 4)

    tril = jnp.tril(jnp.ones((chunk, chunk), dtype=bool))

    def step(S, inp):
        qc, kc, vc, lc = inp
        b = jnp.cumsum(lc, axis=2)
        diff = b[:, :, :, None, :] - b[:, :, None, :, :]
        dec = jnp.exp(jnp.where(tril[:, :, None], diff, -jnp.inf))
        att = jnp.einsum('bhtd,bhtsd,bhsd->bhts', qc, dec, kc)
        o = jnp.einsum('bhts,bhsv->bhtv', att, vc) + jnp.einsum('bhtd,bhdv->bhtv', qc * jnp.exp(b), S)
        b_last = b[:, :, -1, :]
        S = jnp.exp(b_last)[..., None] * S + jnp.einsum(
            'bhsd,bhsv->bhdv', kc * jnp.exp(b_last[:, :, None, :] - b), vc)
        return S, o

    S, o = lax.scan(step, S0.astype(jnp.float32),
                    (to_chunks(q), to_chunks(k), to_chunks(v), to_chunks(log_a)))
    o = o.transpose(1, 0, 3, 2, 4).reshape(B, T, H, dv)
    return o.astype(v.dtype), S

def memory_kv(mem, norm_mem, w_mkv, g_km):
    B, N, _ = mem.shape
    hm = rmsnorm(mem, norm_mem)
    mk, mv = jnp.split(hm @ w_mkv, 2, axis=-1)
    mk = rmsnorm(mk.reshape(B, N, M_HEADS, M_DIM), g_km)
    return mk, mv.reshape(B, N, M_HEADS, M_DIM)

def layer(x, mem_k, mem_v, past_k, past_v, S0, pos0, l,
          norm_x, w_in, g_qa, g_ka, lam, g_oa, w_a2, b_a, g_ob, g_qm, w_branch, w_o):
    B, T, _ = x.shape
    h = rmsnorm(x, norm_x)
    proj = h @ w_in
    (aq, ak, av, az, gq, gk, gv, gz, gr, mq, mz, gl) = jnp.split(
        proj, np.cumsum(IN_SIZES)[:-1].tolist(), axis=-1)

    aq = rmsnorm(aq.reshape(B, T, A_HEADS, 2, A_QK_DIM), g_qa)
    ak = rmsnorm(ak.reshape(B, T, A_HEADS, 2, A_QK_DIM), g_ka)
    av = av.reshape(B, T, A_HEADS, A_V_DIM)
    new_k = ak.reshape(B, T, A_HEADS, 2 * A_QK_DIM)
    new_v = av
    if past_k is None:
        k_all, v_all = new_k, new_v
    else:
        k_all = jnp.concatenate([past_k.astype(new_k.dtype), new_k], axis=1)
        v_all = jnp.concatenate([past_v.astype(new_v.dtype), new_v], axis=1)
    Tk = k_all.shape[1]
    lam_init = 0.8 - 0.6 * math.exp(-0.3 * l)
    lf = lam.astype(jnp.float32)
    lam_val = jnp.exp(jnp.sum(lf[0] * lf[1])) - jnp.exp(jnp.sum(lf[2] * lf[3])) + lam_init
    q_pos = pos0 + jnp.arange(T, dtype=jnp.int32)
    k_pos = jnp.arange(Tk, dtype=jnp.int32)
    block = Q_BLOCK if T % Q_BLOCK == 0 else T
    oa = diff_attention(aq, k_all.reshape(B, Tk, A_HEADS, 2, A_QK_DIM), v_all,
                        q_pos, k_pos, lam_val, block)
    oa = rmsnorm(oa, g_oa) * (1.0 - lam_init)
    ua = (oa.reshape(B, T, A_WIDTH) * jax.nn.silu(az)) @ w_branch[0]

    log_a = jax.nn.log_sigmoid((gr @ w_a2 + b_a).astype(jnp.float32)) / G_GATE_TAU
    log_a = log_a.reshape(B, T, G_HEADS, G_K_DIM)
    gq = gq.reshape(B, T, G_HEADS, G_K_DIM) * (G_K_DIM ** -0.5)
    gk = gk.reshape(B, T, G_HEADS, G_K_DIM)
    gv = gv.reshape(B, T, G_HEADS, G_V_DIM)
    chunk = GLA_CHUNK if T % GLA_CHUNK == 0 else T
    ob, S = gla_chunked(gq, gk, gv, log_a, S0, chunk)
    ob = rmsnorm(ob, g_ob)
    ub = (ob.reshape(B, T, G_WIDTH) * jax.nn.silu(gz)) @ w_branch[1]

    mq = rmsnorm(mq.reshape(B, T, M_HEADS, M_DIM), g_qm)
    s = jnp.einsum('bthd,bmhd->bhtm', mq.astype(jnp.float32),
                   mem_k.astype(jnp.float32)) * (M_DIM ** -0.5)
    p = jax.nn.softmax(s, axis=-1)
    om = jnp.einsum('bhtm,bmhd->bthd', p, mem_v.astype(jnp.float32)).astype(x.dtype)
    um = (om.reshape(B, T, M_WIDTH) * jax.nn.silu(mz)) @ w_branch[2]

    g_a, g_b, g_m = jnp.split(gl, N_BRANCH, axis=-1)
    merged = jax.nn.sigmoid(g_a) * ua + jax.nn.sigmoid(g_b) * ub + jax.nn.sigmoid(g_m) * um
    y = x + merged @ w_o
    return y, new_k, new_v, S.astype(x.dtype)

def setup_inputs(seed: int = 0) -> dict:
    key = jax.random.key(seed)
    ks = jax.random.split(key, 32)
    f32 = jnp.float32
    n_pages = PAST_LEN // PAGE_SIZE
    used = DEC_BATCH * n_pages
    n_pool = used + max(1, used // 4)
    nrm = lambda k, shape, s: jax.random.normal(k, shape, f32) * s
    gain = lambda k, shape: 1.0 + 0.02 * jax.random.normal(k, shape, f32)
    page_table = jax.random.permutation(ks[0], n_pool)[:used].reshape(DEC_BATCH, n_pages).astype(jnp.int32)
    return {
        "x_prompt": nrm(ks[1], (BATCH, SEQ, D_MODEL), 1.0),
        "x_sample": nrm(ks[2], (DEC_BATCH, DEC_SEQ, D_MODEL), 1.0),
        "cache_k_a": nrm(ks[3], (DEPTH, n_pool, PAGE_SIZE, A_HEADS, 2 * A_QK_DIM), 1.0),
        "cache_v_a": nrm(ks[4], (DEPTH, n_pool, PAGE_SIZE, A_HEADS, A_V_DIM), 1.0),
        "page_table": page_table,
        "state_gla": nrm(ks[5], (DEPTH, DEC_BATCH, G_HEADS, G_K_DIM, G_V_DIM), 0.3),
        "cache_mem_k": nrm(ks[6], (DEPTH, DEC_BATCH, N_MEM, M_HEADS, M_DIM), 1.0),
        "cache_mem_v": nrm(ks[7], (DEPTH, DEC_BATCH, N_MEM, M_HEADS, M_DIM), 1.0),
        "mem_prompt": nrm(ks[8], (BATCH, N_MEM, D_MODEL), 1.0),
        "norm_x": gain(ks[9], (DEPTH, D_MODEL)),
        "w_in": nrm(ks[10], (DEPTH, D_MODEL, IN_COLS), D_MODEL ** -0.5),
        "g_qa": gain(ks[11], (DEPTH, A_QK_DIM)),
        "g_ka": gain(ks[12], (DEPTH, A_QK_DIM)),
        "lam": nrm(ks[13], (DEPTH, 4, A_QK_DIM), 0.1),
        "g_oa": gain(ks[14], (DEPTH, A_V_DIM)),
        "w_a2": nrm(ks[15], (DEPTH, G_GATE_RANK, G_HEADS * G_K_DIM), G_GATE_RANK ** -0.5),
        "b_a": nrm(ks[16], (DEPTH, G_HEADS * G_K_DIM), 0.1),
        "g_ob": gain(ks[17], (DEPTH, G_V_DIM)),
        "g_qm": gain(ks[18], (DEPTH, M_DIM)),
        "g_km": gain(ks[19], (DEPTH, M_DIM)),
        "norm_mem": gain(ks[20], (DEPTH, D_MODEL)),
        "w_mkv": nrm(ks[21], (DEPTH, D_MODEL, 2 * M_WIDTH), D_MODEL ** -0.5),
        "w_branch": nrm(ks[22], (DEPTH, N_BRANCH, BRANCH_WIDTH, D_MODEL), BRANCH_WIDTH ** -0.5),
        "w_o": nrm(ks[23], (DEPTH, D_MODEL, D_MODEL), D_MODEL ** -0.5),
    }

def reference(x_prompt, x_sample, cache_k_a, cache_v_a, page_table, state_gla,
              cache_mem_k, cache_mem_v, mem_prompt, norm_x, w_in, g_qa, g_ka, lam, g_oa,
              w_a2, b_a, g_ob, g_qm, g_km, norm_mem, w_mkv, w_branch, w_o):
    Bp = x_prompt.shape[0]
    Bs = x_sample.shape[0]
    n_pages = page_table.shape[1]
    page = cache_k_a.shape[2]
    past_len = n_pages * page

    x = x_prompt
    kp, vp, sp, mkp, mvp = [], [], [], [], []
    for l in range(DEPTH):
        mk, mv = memory_kv(mem_prompt, norm_mem[l], w_mkv[l], g_km[l])
        S0 = jnp.zeros((Bp, G_HEADS, G_K_DIM, G_V_DIM), jnp.float32)
        x, nk, nv, S = layer(x, mk, mv, None, None, S0, 0, l,
                             norm_x[l], w_in[l], g_qa[l], g_ka[l], lam[l], g_oa[l],
                             w_a2[l], b_a[l], g_ob[l], g_qm[l], w_branch[l], w_o[l])
        kp.append(nk); vp.append(nv); sp.append(S); mkp.append(mk); mvp.append(mv)
    y_prompt = x

    x = x_sample
    ks_, vs_, ss_ = [], [], []
    for l in range(DEPTH):
        past_k = cache_k_a[l][page_table].reshape(Bs, past_len, A_HEADS, 2 * A_QK_DIM)
        past_v = cache_v_a[l][page_table].reshape(Bs, past_len, A_HEADS, A_V_DIM)
        x, nk, nv, S = layer(x, cache_mem_k[l], cache_mem_v[l], past_k, past_v,
                             state_gla[l], past_len, l,
                             norm_x[l], w_in[l], g_qa[l], g_ka[l], lam[l], g_oa[l],
                             w_a2[l], b_a[l], g_ob[l], g_qm[l], w_branch[l], w_o[l])
        ks_.append(nk); vs_.append(nv); ss_.append(S)
    y_sample = x

    return (y_prompt, y_sample,
            jnp.stack(kp), jnp.stack(vp), jnp.stack(ks_), jnp.stack(vs_),
            jnp.stack(sp), jnp.stack(ss_), jnp.stack(mkp), jnp.stack(mvp))


_drawn_inputs = setup_inputs


def setup_inputs(seed=0):
    import zlib

    import numpy as np

    out = dict(_drawn_inputs(seed))
    spreads = {}
    factors = {'g_qa': 8.0,
     'g_ka': 3.108,
     'lam': 8.0,
     'g_oa': 8.0,
     'g_ob': 8.0,
     'g_qm': 8.0,
     'g_km': 2.905,
     'norm_mem': 2.928}
    for name, (base, spread) in spreads.items():
        noise = np.random.default_rng([zlib.crc32(name.encode()), seed]).standard_normal(out[name].shape)
        drawn = base * np.exp(spread * noise) if base else spread * noise
        out[name] = __import__('jax').numpy.asarray(drawn.astype(out[name].dtype))
    for name, factor in factors.items():
        out[name] = (out[name] * factor).astype(out[name].dtype)
    return out
```

```python
import math
from contextlib import ExitStack

import numpy as np
import concourse.bass as bass
from concourse import mybir

F32 = mybir.dt.float32
I32 = mybir.dt.int32
ALU = mybir.AluOpType
ACT = mybir.ActivationFunctionType
AX = mybir.AxisListType

P = 128
D = 1024
KD = D // P
NP_TOK, NS_TOK = 1024, 64
T = NP_TOK + NS_TOK
NMEM = 256
H = 4
W = 512
KW = W // P
NB = 8
QB = 8
PAST, PAGE = 256, 128
NPG = PAST // PAGE
GC = 64
EPS = 1e-6
LAM_INIT = 0.8 - 0.6 * math.exp(-0.3 * 0)
NEG = -1e30
CLIP = 43.0 * 16.0

C_AQ, C_AK, C_AV, C_AZ = 0, 512, 1024, 1536
C_GQ, C_GK, C_GV, C_GZ, C_GR = 2048, 2304, 2560, 3072, 3584
C_MQ, C_MZ, C_GL = 3600, 4112, 4624

PT = NP_TOK // P
CH = [(0, 364), (364, 364), (728, 360)]
CHW = 364

def shape_tables():
    p = np.arange(P)[:, None]
    tabs = {}
    tabs["ident"] = np.eye(P)
    tabs["mean"] = np.full((P, P), 1.0 / P)
    j = np.arange(NP_TOK)[None, :] - (NP_TOK - P) - p
    tabs["alibi"] = np.where(j <= 0, j, NEG)
    r = np.arange(P)
    half = np.stack([(r < 64), (r >= 64)], 1)
    tabs["half"] = half
    tabs["batch"] = (np.minimum(r, 63)[:, None] // QB == np.arange(NB)[None, :]) & (r < 64)[:, None]
    row = np.arange(P)
    hh, cc, qq = (row // 16) % 4, (row // 8) % 2, row % 8
    slope = 2.0 ** (-8.0 * (hh + 1) / H)
    tabs["past"] = -slope[:, None] * (PAST + qq[:, None] - np.arange(PAST)[None, :])
    new = np.zeros((P, NB, NS_TOK))
    for b in range(NB):
        u = np.arange(NS_TOK)[None, :] - QB * b
        new[:, b] = np.where((u >= 0) & (u <= qq[:, None]), -slope[:, None] * (qq[:, None] - u), NEG)
    tabs["new"] = new.reshape(P, -1)
    tabs["map"] = np.stack([cc == 0, cc == 1], 1)
    comb = np.zeros((P, 32))
    for x in range(64):
        comb[x, hh[x] * 8 + qq[x]] = 1.0
    tabs["comb"] = comb
    s, t = np.arange(P)[:, None], np.arange(P)[None, :]
    tabs["gmask"] = np.concatenate([
        (s // 16 == t // 16) & (s <= t),
        (s // 32 == t // 32) & (s % 32 < 16) & (t % 32 >= 16),
        (s // 64 == t // 64) & (s % 64 < 32) & (t % 64 >= 32),
        (s // 8 == t // 8) & (s <= t)], 1)
    keep = np.ones((P, T))
    keep[:, 0:NP_TOK:GC] = 0
    keep[:, NP_TOK::QB] = 0
    tabs["keep"] = keep
    return {k: np.ascontiguousarray(v, dtype=np.float32) for k, v in tabs.items()}


SMALL = ["ident", "mean", "half", "batch", "map", "comb", "gmask"]


def heavy_jobs():
    jobs, stage = [], {}

    def add(name, some):
        stage[name] = range(len(jobs), len(jobs) + len(some))
        jobs.extend(some)

    add("X", [("rows", k, t) for t in range(NMEM // P) for k in ("mk", "mv")]
        + [("rows", k, r) for r in range(PT + 1) for k in ("q", "k", "v")])
    add("A", [("cols", "az", f, c) for c in range(3) for f in range(KW)]
        + [("cols", k, f, c) for k in ("gq", "gk") for f in range(2) for c in range(3)])
    add("R", [("cols", "gr", 0, c) for c in range(3)])
    add("V", [("rows", "gv", r) for r in range(PT + 1)])
    add("Z", [("cols", "gz", f, c) for f in range(KW) for c in range(3)])
    pairs = lambda br: [(k, br, f, c) for f in range(KD) for c in range(3) for k in ("gate", "up")]
    add("PA", pairs(0))
    add("MZ", [("cols", "mz", f, c) for f in range(KW) for c in range(3)])
    add("Q", [("rows", "mq", r) for r in range(PT + 1)])
    add("PB", pairs(1))
    add("PM", pairs(2))
    add("O", [("out", r, j) for r in range(PT + 1) for j in range(2)])
    return jobs, stage


JOBS, STAGE = heavy_jobs()
NORMED = {"mk": 128, "q": 64, "k": 64, "mq": 128}
NJ = [n for n, j in enumerate(JOBS) if j[0] == "rows" and j[1] in NORMED]
KJ = [n for n in NJ if JOBS[n][1] in ("k", "mk")]
ZJ = [n for n, j in enumerate(JOBS) if j[0] == "gate" or (j[0] == "cols" and j[1] in ("az", "gz", "mz"))]


def ring_loads():
    first, last = {}, {}
    for n, j in enumerate(JOBS):
        if j[0] == "cols":
            key = (j[1], j[2] // 2)
        elif j[0] in ("gate", "up"):
            key = ("pair", j[1], j[2])
        else:
            continue
        first.setdefault(key, n)
        last[key] = n
    return [(key, last[key]) for key in first]


LOADS = ring_loads()
LOAD_OF = {key: i for i, (key, _) in enumerate(LOADS)}
STEPS_A = H * PT + NB


def heavy_A(u):
    js = STAGE["A"]
    return [js[u]] if u < 12 else [js[12 + x] for x in range(12 * (u - 12) // 28, 12 * (u - 11) // 28)]


def groups_A(u):
    nb = u // H + 1
    return [(g, min(g + 4, nb)) for g in range(0, nb, 4)]


def transposed_uses():
    uses = [("norm", n) for n in NJ if n in STAGE["X"]]
    for u in range(1, STEPS_A + 1):
        if u <= H * PT:
            uses += [("a", u - 1, g) for g, _ in groups_A(u - 1)]
        else:
            uses.append(("s", u - 1 - H * PT))
        if u % 4 == 1 and 5 <= u <= 33:
            uses.append(("mean", (u - 5) // 4))
    uses.append(("mean", PT))
    for r in range(PT + 1):
        uses += [("kd", r), ("mean", PT + 1 + r)]
    uses += [("norm", n) for n in NJ if n not in STAGE["X"]]
    for i in range(PT):
        uses += [("m", i, 0), ("m", i, 1)]
    uses += [("ms", b) for b in range(NB)]
    return {key: i for i, key in enumerate(uses)}


TRN = transposed_uses()
LEVELS = [(16, 7, 0), (32, 15, 1), (64, 31, 2)]
LEVELS_S = [(QB, 3, 3)]
N_CONSTS = len(SMALL) + 11
ROWS_TILE = lambda r: P if r < PT else NS_TOK


def parts_before(seq, n):
    return sum(1 for x in seq if x < n)


def hybrid_step(nc, x_prompt, x_sample, cache_k, cache_v, page_table, state_gla, mem_k, mem_v,
                mem_prompt, norm_x, w_in, g_qa, g_ka, lam, g_oa, w_a2, b_a, g_ob, g_qm, g_km,
                norm_mem, w_mkv, w_branch, w_o, tab,
                y_prompt, y_sample, ka_prompt, va_prompt, ka_sample, va_sample,
                gla_prompt, gla_sample, mk_prompt, mv_prompt):
    ctx = ExitStack()

    def sb(name, shape, dt=F32):
        return ctx.enter_context(nc.sbuf_tensor(name, shape, dt))

    def sem(name):
        return ctx.enter_context(nc.semaphore(name))

    xs = x_sample.rearrange("b q d -> (b q) d")
    NMT = NMEM // P
    TILES = [(mem_prompt[0, t * P:(t + 1) * P, :], P) for t in range(NMT)] + \
            [(x_prompt[0, t * P:(t + 1) * P, :], P) for t in range(PT)] + [(xs, NS_TOK)]
    NT = len(TILES)

    with ctx:
        arena = sb("arena", [P, 51672])

        def at(off, shape):
            n = int(np.prod(shape))
            v = arena[:, off:off + n]
            if len(shape) == 1:
                return v
            names = "abcd"[:len(shape)]
            return v.rearrange(f"p ({' '.join(names)}) -> p {' '.join(names)}",
                               **{c: s for c, s in zip(names, shape)})

        hT = at(0, [KD, T])
        qT, kT, vA = at(8704, [H, T]), at(13056, [H, T]), at(17408, [9, W])
        w_mem, hT_mem = at(8704, [KD, 2 * W]), at(17408, [KD, NMEM])
        wX = [at(22016 + 4096 * i, [KD, W]) for i in range(3)]
        merged = at(8704, [KD, T])
        w_gv = at(8704, [KD, W])
        azT, gzT = at(22016, [KW, T]), at(26368, [KW, T])
        alibi = at(26368, [H, NP_TOK])
        gqT, gkT = at(30720, [2, T]), at(30720 + 2176, [2, T])
        mqT, mzT = at(30720, [H, T]), at(17408, [KW, T])
        gv = at(17408, [9, W])
        ring = [at(35072 + 2048 * i, [2048]) for i in range(2)]
        mkT, mv = at(39168, [H, NMEM]), at(39168 + 1024, [2, W])
        SCR = 41216
        x_in = [at(SCR + 1024 * i, [D]) for i in range(2)]
        xn = at(SCR + 2048, [D])
        junk = at(SCR + 3072, [D])
        nrm = [at(SCR + 4096 + 512 * i, [W]) for i in range(2)]
        S = [at(SCR + 2048 * i, [2, NP_TOK]) for i in range(2)]
        aT = [at(SCR + 4096 + 1024 * i, [NP_TOK]) for i in range(2)]
        qpadA = at(SCR + 6144, [H, NB, NS_TOK])
        NSK = PAST + NS_TOK
        kpage = [at(SCR + 1024 * i, [NPG, W]) for i in range(2)]
        vpage = [at(SCR + 2048 + 1024 * i, [NPG, W]) for i in range(2)]
        Ps = [at(SCR + 4096 + 320 * i, [NSK]) for i in range(2)]
        aTs = [at(SCR + 4736 + 96 * i, [3, 32]) for i in range(2)]
        kTsA = [at(26368 + 1280 * i, [H, NSK]) for i in range(2)]
        past_t, new_t = at(26368 + 2560, [PAST]), at(26368 + 2816, [NB, NS_TOK])
        bb = at(SCR, [2, T])
        GT = SCR + 2176
        lsig = at(GT, [2, T])
        gr = at(GT + 2176, [T])
        keep = at(GT + 3264, [T])
        wa2 = at(GT + 4352, [256])
        edel, dlt, dq, dk = (at(GT + 256 * i, [2, P]) for i in range(4))
        qz = [at(GT + 1024 + 512 * i, [2, 2, P]) for i in range(2)]
        kz = [at(GT + 2048 + 256 * i, [2, P]) for i in range(2)]
        qe = at(GT + 2560, [2, 2, P])
        kd = at(GT + 3072, [2, P])
        kdt = at(GT + 3328, [256])
        kdz = [at(GT + 3584 + 256 * i, [2, P]) for i in range(2)]
        att = at(GT + 4096, [H, P])
        atm = at(GT + 4608, [H, P])
        St = [at(GT + 5120 + 256 * i, [2, P]) for i in range(3)]
        Pm = at(SCR, [H, NMEM])
        PmT = at(SCR + 1024, [8, P])
        qpadM = at(SCR + 2048, [H, NB, 32])
        w_mq = at(SCR + 4096, [KD, W])
        kpageM = [at(SCR + 4096 + 1024 * i, [2, W]) for i in range(2)]
        vpageM = [at(SCR + 6144 + 1024 * i, [2, W]) for i in range(2)]
        kTsM = at(SCR + 3072, [H, NMEM])
        PsM, aTsM = at(SCR, [NMEM]), at(SCR + 1024, [2, 32])
        nrmM = [at(SCR + 512 * i, [W]) for i in range(2)]
        w_out = at(SCR, [KD, D])
        x_res = [at(22016 + 1024 * i, [D]) for i in range(2)]
        y_row = [at(22016 + 2048 + 1024 * i, [D]) for i in range(2)]
        TAIL = SCR + 8192
        tanh = [at(TAIL + CHW * i, [CHW]) for i in range(2)]
        sq = at(TAIL + 728, [W])
        rs_t = at(TAIL + 728 + 512, [W])
        og = at(TAIL + 728 + 1024, [W])

        small = {k: sb("t_" + k, [P, tab[k].shape[1]]) for k in SMALL}
        ident, meanm = small["ident"], small["mean"]
        half_t, batch_t, comb_t = small["half"], small["batch"], small["comb"]
        gmask = small["gmask"][:, :].rearrange("p (l t) -> p l t", l=4)
        gx, gmem = sb("gx", [P, KD]), sb("gmem", [P, KD])
        gka_row, gkm_row = sb("gka_row", [P, 64]), sb("gkm_row", [P, P])
        ba_col = sb("ba_col", [P, 2])
        gcol = sb("gcol", [P, 4])
        GQA, GQM, GOA, GOB = range(4)
        eps = sb("eps", [P, 1])
        rstat = sb("rstat", [P, 3])
        gstat = sb("gstat", [P, 3, 8])
        lam_sum = sb("lam_sum", [P, 4])
        neg_lam, wrow = sb("neg_lam", [P, 1]), sb("wrow", [P, 1])
        mx, nmx, psum_r, coef = (sb(k, [P, 4]) for k in ("mx", "nmx", "psum_r", "coef"))
        dec = sb("dec", [P, 2, NB])
        pt_sb = sb("pt_sb", [1, NB * NPG], I32)

        sc_all = ctx.enter_context(nc.psum_tensor("scores", [P, 4, W], F32))
        HV = [ctx.enter_context(nc.psum_tensor(f"heavy{i}", [P, W], F32)) for i in range(2)]
        TR = ctx.enter_context(nc.psum_tensor("transposed", [P, W], F32))
        OB = ctx.enter_context(nc.psum_tensor("attended", [P, W], F32))

        tmp = [at(TAIL + 728 + 512 + CHW * i, [CHW]) for i in range(2)]

        hv_full = [sem("hv_full0"), sem("hv_full1")]
        hv_free = [sem("hv_free0"), sem("hv_free1")]
        ring_in = [sem("ring_in0"), sem("ring_in1")]
        tm_w = [sem(f"tm_w{i}") for i in range(6)]
        wo_in = sem("wo_in")
        consts_in, consts_ready = sem("consts_in"), sem("consts_ready")
        x_loaded = [sem("x_loaded0"), sem("x_loaded1")]
        root_done, xn_done, xt_full, xt_done = (sem(k) for k in ("root_done", "xn_done", "xt_full", "xt_done"))
        sq_done, gsum_done, groot_done, nrm_done = (sem(k) for k in ("sq_done", "gsum_done", "groot_done", "nrm_done"))
        tr_full, tr_free = sem("tr_full"), sem("tr_free")
        rows_out = [sem("rows_out0"), sem("rows_out1")]
        out_done = sem("out_done")
        tanh_done = sem("tanh_done")
        dve_step, act_step = sem("dve_step"), sem("act_step")
        alibi_in, alibi_ready = sem("alibi_in"), sem("alibi_ready")
        sc_full, sc_read, nmx_ready, p_ready, a_ready = (sem(k) for k in ("sc_full", "sc_read", "nmx_ready", "p_ready", "a_ready"))
        pv_done = sem("pv_done")
        qpad_zero, qpad_ready, new_keys = sem("qpad_zero"), sem("qpad_ready"), sem("new_keys")
        tabs_in, pt_in = sem("tabs_in"), sem("pt_in")
        k_in, v_in = [sem("k_in0"), sem("k_in1")], [sem("v_in0"), sem("v_in1")]
        ktr_full, kts_copied = [sem("ktr_full0"), sem("ktr_full1")], [sem("kts_copied0"), sem("kts_copied1")]
        ss_full, ss_read = sem("ss_full"), sem("ss_read")
        gw_in, lg_full, lg_read, lsig_done, bb_ready = (sem(k) for k in ("gw_in", "lg_full", "lg_read", "lsig_done", "bb_ready"))
        gd_in, gd_exp, kd_ready, kdz_ready, u_full, st_ready = (sem(k) for k in ("gd_in", "gd_exp", "kd_ready", "kdz_ready", "u_full", "st_ready"))
        lv_in, lv_exp, lv_ready, at_full, masked, att_ready = (sem(k) for k in ("lv_in", "lv_exp", "lv_ready", "at_full", "masked", "att_ready"))
        st_in, st_out = [sem(f"st_in{i}") for i in range(3)], [sem(f"st_out{i}") for i in range(3)]
        vb_done, st_zero, bst_ready, bu_full = sem("vb_done"), sem("st_zero"), sem("bst_ready"), sem("bu_full")
        madd_done = sem("madd_done")
        m_full, m_max, m_exp, m_ready, om_full, mt_done = (sem(k) for k in ("m_full", "m_max", "m_exp", "m_ready", "om_full", "mt_done"))
        qm_zero, qm_ready, ms_full = sem("qm_zero"), sem("qm_ready"), sem("ms_full")
        km_in, vm_in = [sem("km_in0"), sem("km_in1")], [sem("vm_in0"), sem("vm_in1")]
        mtr_full, mts_copied = [sem("mtr_full0"), sem("mtr_full1")], [sem("mts_copied0"), sem("mts_copied1")]
        xr_in, y_out = [sem("xr_in0"), sem("xr_in1")], [sem("y_out0"), sem("y_out1")]
        lam_exp, lam_ready = sem("lam_exp"), sem("lam_ready")
        o_full, o_free, osq_done, oroot_done, tail_done = (sem(k) for k in ("o_full", "o_free", "osq_done", "oroot_done", "tail_done"))

        def hv_wait_full(eng, n):
            eng.wait_ge(hv_full[n % 2], n // 2 + 1)

        def hv_wait_free(eng, n):
            eng.wait_ge(hv_free[n % 2], n // 2 + 1)

        def bc(ap, k):
            return ap.unsqueeze(2).to_broadcast([ap.shape[0], ap.shape[1], k])

        def norm_wait(eng, n):
            if JOBS[n][1] in ("k", "mk"):
                eng.wait_ge(nrm_done, KJ.index(n) + 1)
            else:
                hv_wait_free(eng, n)

        def nrm_of(n):
            return (nrmM if JOBS[n][1] == "mq" else nrm)[NJ.index(n) % 2]

        def tanh_reader(n):
            return n if JOBS[n][0] == "cols" else n + 1

        def slot_count(i):
            return 16 * sum(2 if LOADS[x][0][0] == "pair" else 1 for x in range(i % 2, i + 1, 2))

        def z_of(kind):
            return {"az": azT, "gz": gzT, "mz": mzT}[kind]

        def norm_dest(n):
            kind, r = JOBS[n][1], JOBS[n][2]
            dst = {"mk": mkT, "q": qT, "k": kT, "mq": mqT}[kind]
            rows = P if kind == "mk" else ROWS_TILE(r)
            return dst[:, :, r * P:r * P + rows], rows

        def rows_of(r, prompt, sample):
            if r < PT:
                return prompt[0, 0, r * P:(r + 1) * P].rearrange("t h d -> t (h d)")
            return sample[0].rearrange("b q h d -> (b q) (h d)")

        def tail_of(k):
            r = k % (PT + 1)
            n = ROWS_TILE(r)
            return n, (azT if k <= PT else gzT)[:, :, r * P:r * P + n]

        def o_view(ap, n):
            return ap[:, 0:H * n].rearrange("p (h t) -> p h t", h=H)

        ROWS_OUT = [16 * sum(1 for n in KJ if NJ.index(n) % 2 == i) for i in range(2)]
        ROWS_OUT_V = 16 * sum(1 for n in STAGE["X"] if JOBS[n][1] in ("v", "mv"))
        NU = H * PT
        block = ctx.enter_context(nc.Block())

        @block.gpsimd
        def _(pool):
            for n in STAGE["X"]:
                _, kind, r = JOBS[n]
                if kind in ("k", "mk"):
                    pool.wait_ge(nrm_done, KJ.index(n) + 1)
                    dst = (rows_of(r, ka_prompt, ka_sample) if kind == "k" else
                           mk_prompt[0, 0, r * P:(r + 1) * P].rearrange("t h d -> t (h d)"))
                    rows = P if kind == "mk" else ROWS_TILE(r)
                    pool.dma_start(dst, nrm_of(n)[0:rows, :]).then_inc(rows_out[NJ.index(n) % 2], 16)
                elif kind in ("v", "mv"):
                    hv_wait_free(pool, n)
                    if kind == "v":
                        dst, src = rows_of(r, va_prompt, va_sample), vA[0:ROWS_TILE(r), r, :]
                    else:
                        dst, src = mv_prompt[0, 0, r * P:(r + 1) * P].rearrange("t h d -> t (h d)"), mv[:, r, :]
                    pool.dma_start(dst, src).then_inc(out_done, 16)

            pool.memset(qpadA, 0.0).then_inc(qpad_zero, 1)
            pool.wait_ge(qpad_zero, 1)
            pool.wait_ge(tr_free, TRN["norm", STAGE["X"][-3]] + 1)
            for c in range(2):
                for h in range(H):
                    x = 16 * h + 8 * c
                    if c or h:
                        pool.wait_ge(qpad_ready, H * c + h)
                    pool.tensor_copy(qpadA[64 * c:64 * c + 64, h, :, x:x + 8],
                                     qT[64 * c:64 * c + 64, h, NP_TOK:T].rearrange("p (b q) -> p b q", b=NB))\
                        .then_inc(qpad_ready, 1)
            pool.wait_ge(sc_read, 2 * NU)
            pool.wait_ge(tr_free, TRN["norm", STAGE["X"][-2]] + 1)
            pool.wait_ge(qpad_ready, 2 * H)
            for x in range(2):
                pool.tensor_copy(kTsA[x][:, :, PAST:NSK], kT[:, :, NP_TOK:T]).then_inc(new_keys, 1)

            pool.wait_ge(st_ready, 2 * PT)
            pool.dma_start(gla_prompt[0, 0].rearrange("(k e) d v -> (e d) k v", e=2), St[(2 * PT) % 3])\
                .then_inc(st_out[(2 * PT) % 3], 16)
            for b in range(NB):
                pool.wait_ge(bst_ready, b + 1)
                pool.dma_start(gla_sample[0, b].rearrange("(k e) d v -> (e d) k v", e=2), St[(2 + b) % 3])\
                    .then_inc(st_out[(2 + b) % 3], 16)
            hv_wait_free(pool, STAGE["Q"][0])
            pool.memset(qpadM, 0.0).then_inc(qm_zero, 1)
            pool.wait_ge(qm_zero, 1)
            pool.wait_ge(tr_free, TRN["norm", STAGE["Q"][-1]] + 1)
            for h in range(H):
                if h:
                    pool.wait_ge(qm_ready, h)
                pool.tensor_copy(qpadM[:, h, :, 8 * h:8 * h + 8],
                                 mqT[:, h, NP_TOK:T].rearrange("p (b q) -> p b q", b=NB)).then_inc(qm_ready, 1)
            pool.wait_ge(qm_ready, H)
            for s in ("PB", "PM"):
                for n in STAGE[s]:
                    kind, br, f, c = JOBS[n]
                    if kind == "up":
                        x = 3 * KD * (br - 1) + 3 * f + c
                        c0, cw = CH[c]
                        hv_wait_free(pool, n)
                        if x:
                            pool.wait_ge(madd_done, x)
                        pool.tensor_tensor(out=merged[:, f, c0:c0 + cw], in0=merged[:, f, c0:c0 + cw],
                                           in1=tmp[x % 2][:, 0:cw], op=ALU.add).then_inc(madd_done, 1)
            for r in range(PT + 1):
                rows = ROWS_TILE(r)
                for j in range(2):
                    hv_wait_free(pool, STAGE["O"][2 * r + j])
                dst = y_prompt[0, r * P:(r + 1) * P, :] if r < PT else y_sample.rearrange("b q d -> (b q) d")
                pool.dma_start(dst, y_row[r % 2][0:rows, :]).then_inc(y_out[r % 2], 16)

        @block.sync
        def _(sp):
            def load_x(t):
                src, n = TILES[t]
                if t >= 2:
                    sp.wait_ge(xn_done, t - 1)
                sp.dma_start(x_in[t % 2][0:n, :], src).then_inc(x_loaded[t % 2], 16)

            def load_slot(i):
                key, _ = LOADS[i]
                if i >= 2:
                    hv_wait_full(sp, LOADS[i - 2][1])
                slot, done = ring[i % 2], ring_in[i % 2]
                if key[0] == "pair":
                    _, br, f = key
                    c0 = C_GL + br * D + f * P
                    sp.dma_start(slot[:, 0:1024].rearrange("p (k n) -> p k n", k=KD),
                                 w_in[0, :, c0:c0 + P].rearrange("(k p) n -> p k n", p=P)).then_inc(done, 16)
                    sp.dma_start(slot[:, 1024:1536].rearrange("p (k n) -> p k n", k=KW),
                                 w_branch[0, br, :, f * P:(f + 1) * P].rearrange("(k p) n -> p k n", p=P))\
                        .then_inc(done, 16)
                else:
                    kind, f2 = key
                    c0 = {"az": C_AZ, "gq": C_GQ, "gk": C_GK, "gz": C_GZ, "gr": C_GR, "mz": C_MZ}[kind] + 256 * f2
                    wd = 16 if kind == "gr" else 256
                    sp.dma_start(slot[:, 0:KD * wd].rearrange("p (k n) -> p k n", k=KD),
                                 w_in[0, :, c0:c0 + wd].rearrange("(k p) n -> p k n", p=P)).then_inc(done, 16)

            load_x(0)
            load_x(1)
            for k in SMALL:
                sp.dma_start(small[k][:, :], tab[k]).then_inc(consts_in, 16)
            with nc.allow_non_contiguous_dma(reason="gains as columns, 4 K elements in all"):
                sp.dma_start(gx[:, :], norm_x[0].rearrange("(k p) -> p k", p=P)).then_inc(consts_in, 16)
                sp.dma_start(gmem[:, :], norm_mem[0].rearrange("(k p) -> p k", p=P)).then_inc(consts_in, 16)
                sp.dma_start(ba_col[:, :], b_a[0].rearrange("(k p) -> p k", p=P)).then_inc(consts_in, 16)
                for hf in range(2):
                    sp.dma_start(gcol[64 * hf:64 * hf + 64, GQA:GQA + 1],
                                 g_qa.rearrange("a d -> d a")).then_inc(consts_in, 16)
                for i, src in ((GQM, g_qm), (GOA, g_oa), (GOB, g_ob)):
                    sp.dma_start(gcol[:, i:i + 1], src.rearrange("a d -> d a")).then_inc(consts_in, 16)
            sp.dma_start(gka_row[:, :], g_ka[0].partition_broadcast(P)).then_inc(consts_in, 16)
            sp.dma_start(gkm_row[:, :], g_km[0].partition_broadcast(P)).then_inc(consts_in, 16)
            sp.dma_start(nrm[0][:, 0:256], lam[0].rearrange("a d -> (a d)").partition_broadcast(P)).then_inc(consts_in, 16)
            sp.dma_start(w_mem, w_mkv[0].rearrange("(k p) n -> p k n", p=P)).then_inc(tm_w[0], 16)
            for i, c in enumerate((C_AQ, C_AK, C_AV)):
                sp.dma_start(wX[i], w_in[0, :, c:c + W].rearrange("(k p) n -> p k n", p=P))\
                    .then_inc(tm_w[1 + i], 16)
            load_slot(0)
            load_slot(1)
            for t in range(2, NT):
                load_x(t)
            hv_wait_free(sp, STAGE["X"][-1])
            sp.wait_ge(tr_free, len(NJ) - (PT + 1))
            sp.dma_start(S[1][:, 0, :], tab["alibi"]).then_inc(alibi_in, 16)

            for i in range(2, 4):
                load_slot(i)
            sp.dma_start(pt_sb[:, :], page_table.rearrange("(a b) g -> a (b g)", a=1)).then_inc(pt_in, 16)
            sp.wait_ge(sc_read, 2 * NU)
            sp.dma_start(past_t, tab["past"]).then_inc(tabs_in, 16)
            sp.dma_start(new_t, tab["new"].rearrange("p (b t) -> p b t", b=NB)).then_inc(tabs_in, 16)
            sp.wait_ge(pt_in, 16)
            for b in range(NB):
                pages = [sp.value_load(pt_sb[0:1, NPG * b + g:NPG * b + g + 1], min_val=0,
                                       max_val=cache_k.shape[1] - 1) for g in range(NPG)]
                if b < 2:
                    sp.wait_ge(pv_done, NU - 1)
                else:
                    sp.wait_ge(ktr_full[1], b - 1)
                for g, pg in enumerate(pages):
                    sp.dma_start(kpage[b % 2][:, g, :],
                                 cache_k[0, bass.ds(pg, 1), :, :, :].rearrange("a t h d -> (a t) (h d)"))\
                        .then_inc(k_in[b % 2], 16)
                sp.wait_ge(pv_done, NU if b < 2 else NU + b - 1)
                for g, pg in enumerate(pages):
                    sp.dma_start(vpage[b % 2][:, g, :],
                                 cache_v[0, bass.ds(pg, 1), :, :, :].rearrange("a t h d -> (a t) (h d)"))\
                        .then_inc(v_in[b % 2], 16)

            load_slot(4)
            load_slot(5)
            sp.wait_ge(pv_done, NU + NB)
            sp.dma_start(w_gv, w_in[0, :, C_GV:C_GV + W].rearrange("(k p) n -> p k n", p=P)).then_inc(tm_w[4], 16)
            sp.dma_start(wa2[0:16, :], w_a2[0]).then_inc(gw_in, 16)
            sp.dma_start(keep, tab["keep"]).then_inc(gw_in, 16)
            PA0 = LOAD_OF[("pair", 0, 0)]
            for i in range(6, PA0 + KD):
                load_slot(i)
            for b in range(NB):
                x = (2 + b) % 3
                if b < 2:
                    sp.wait_ge(o_full, PT)
                else:
                    sp.wait_ge(st_out[x], 16 * (b // 3 + (x == 1)))
                sp.dma_start(St[x], state_gla[0, b].rearrange("(k e) d v -> (e d) k v", e=2))\
                    .then_inc(st_in[x], 16)
            MZ0 = LOAD_OF[("mz", 0)]
            load_slot(MZ0)
            load_slot(MZ0 + 1)
            for x in range(3):
                sp.wait_ge(st_out[x], 48)
            sp.dma_start(w_mq, w_in[0, :, C_MQ:C_MQ + W].rearrange("(k p) n -> p k n", p=P)).then_inc(tm_w[5], 16)
            load_slot(MZ0 + 2)
            load_slot(MZ0 + 3)
            for b in range(NB):
                if b < 2:
                    hv_wait_full(sp, STAGE["Q"][-1])
                else:
                    sp.wait_ge(mtr_full[1], b - 1)
                sp.dma_start(kpageM[b % 2], mem_k[0, b].rearrange("(g t) h d -> t g (h d)", g=2)).then_inc(km_in[b % 2], 16)
                if b >= 2:
                    sp.wait_ge(om_full, PT + b - 1)
                sp.dma_start(vpageM[b % 2], mem_v[0, b].rearrange("(g t) h d -> t g (h d)", g=2)).then_inc(vm_in[b % 2], 16)
                if b == 1:
                    for i in range(MZ0 + 4, MZ0 + 4 + 4):
                        load_slot(i)
                if b in (2, 3):
                    load_slot(MZ0 + 6 + b)
            load_slot(MZ0 + 10)
            load_slot(MZ0 + 11)
            sp.wait_ge(om_full, PT + NB)
            sp.dma_start(w_out, w_o[0].rearrange("(k p) n -> p k n", p=P)).then_inc(wo_in, 16)
            for i in range(MZ0 + 12, len(LOADS)):
                load_slot(i)
            for r in range(PT + 1):
                if r >= 2:
                    hv_wait_free(sp, STAGE["O"][2 * (r - 2) + 1])
                src = x_prompt[0, r * P:(r + 1) * P, :] if r < PT else xs
                sp.dma_start(x_res[r % 2][0:ROWS_TILE(r), :], src).then_inc(xr_in[r % 2], 16)
            sp.wait_ge(y_out[0], 16 * ((PT + 2) // 2))
            sp.wait_ge(y_out[1], 16 * ((PT + 1) // 2))
            for x in range(3):
                sp.wait_ge(st_out[x], 48)
            sp.wait_ge(out_done, ROWS_OUT_V)
            for i in range(2):
                sp.wait_ge(rows_out[i], ROWS_OUT[i])

        @block.tensor
        def _(pe):
            def tr_begin(*use):
                if TRN[use]:
                    pe.wait_ge(tr_free, TRN[use])

            def hv_begin(n):
                if n >= 2:
                    hv_wait_free(pe, n - 2)

            def heavy(n):
                job = JOBS[n]
                bank = HV[n % 2]
                hv_begin(n)
                if job[0] == "rows":
                    _, kind, r = job
                    i = {"mk": 0, "mv": 0, "q": 1, "k": 2, "v": 3, "gv": 4, "mq": 5}[kind]
                    pe.wait_ge(tm_w[i], 16)
                    rows = P if kind in ("mk", "mv") else ROWS_TILE(r)
                    if kind in ("mk", "mv"):
                        src, w = hT_mem, w_mem[:, :, W * (kind == "mv"):W * (kind == "mv") + W]
                    else:
                        src, w = hT, [None, wX[0], wX[1], wX[2], w_gv, w_mq][i]
                    if n in STAGE["X"]:
                        t = r + (0 if kind in ("mk", "mv") else NMT)
                        pe.wait_ge(xt_done, 2 * (t + 1))
                    for k in range(KD):
                        last = nc.tensor.matmul(bank[0:rows, :], src[:, k, r * P:r * P + rows],
                                                w[:, k, :], start=(k == 0), stop=(k == KD - 1))
                elif job[0] == "out":
                    _, r, j = job
                    rows = ROWS_TILE(r)
                    pe.wait_ge(wo_in, 16)
                    pe.wait_ge(madd_done, 2 * 3 * KD)
                    for k in range(KD):
                        last = nc.tensor.matmul(bank[0:rows, :], merged[:, k, r * P:r * P + rows],
                                                w_out[:, k, j * W:(j + 1) * W], start=(k == 0), stop=(k == KD - 1))
                else:
                    _, kind, f, c = job
                    c0, cw = CH[c]
                    if job[0] == "cols":
                        i = LOAD_OF[(kind, f // 2)]
                        m = 16 if kind == "gr" else P
                        w = ring[i % 2][:, 0:KD * (16 if kind == "gr" else 256)].rearrange("p (k n) -> p k n", k=KD)
                        w = w[:, :, (f % 2) * P:(f % 2) * P + m]
                        src, kb, loads = hT, KD, 1 + i // 2
                    else:
                        i = LOAD_OF[("pair", kind, f)]
                        m = P
                        if job[0] == "gate":
                            w, src, kb = ring[i % 2][:, 0:1024].rearrange("p (k n) -> p k n", k=KD), hT, KD
                        else:
                            w = ring[i % 2][:, 1024:1536].rearrange("p (k n) -> p k n", k=KW)
                            src, kb = (azT, gzT, mzT)[kind], KW
                    pe.wait_ge(ring_in[i % 2], slot_count(i))
                    if job[0] == "up" and f == 0 and c == 0:
                        pe.wait_ge(*((tail_done, PT + 1), (tail_done, 2 * (PT + 1)), (mt_done, PT + 1))[kind])
                    for k in range(kb):
                        last = nc.tensor.matmul(bank[0:m, 0:cw], w[:, k, :], src[:, k, c0:c0 + cw],
                                                start=(k == 0), stop=(k == kb - 1))
                last.then_inc(hv_full[n % 2], 1)

            def x_transposes(t):
                rows = TILES[t][1]
                pe.wait_ge(xn_done, t + 1)
                for j in range(2):
                    if t >= 1:
                        pe.wait_ge(xt_done, 2 * (t - 1) + j + 1)
                    for k in range(4):
                        last = nc.tensor.transpose(sc_all[:, j, k * P:k * P + rows],
                                                   xn[0:rows, (4 * j + k) * P:(4 * j + k + 1) * P],
                                                   ident[0:rows, 0:rows])
                    last.then_inc(xt_full, 1)

            def norm_transposes(n):
                _, rows = norm_dest(n)
                norm_wait(pe, n)
                tr_begin("norm", n)
                for h in range(H):
                    last = nc.tensor.transpose(TR[:, h * P:h * P + rows], nrm_of(n)[0:rows, h * P:(h + 1) * P],
                                               ident[0:rows, 0:rows])
                last.then_inc(tr_full, 1)

            x_transposes(0)
            for n in STAGE["X"]:
                kind, r = JOBS[n][1], JOBS[n][2]
                heavy(n)
                if kind in ("mk", "q") and (t := r + (0 if kind == "mk" else NMT)) + 1 < NT:
                    x_transposes(t + 1)
                if n - 1 in NJ:
                    norm_transposes(n - 1)

            def scores(u):
                i, h = u // H, u % H
                nk = (i + 1) * P
                for c in range(2):
                    if u:
                        pe.wait_ge(sc_read, 2 * (u - 1) + c + 1)
                    for j in range(0, nk, W):
                        w = min(W, nk - j)
                        last = nc.tensor.matmul(sc_all[:, 2 * c + j // W, 0:w],
                                                qT[64 * c:64 * c + 64, h, i * P:(i + 1) * P],
                                                kT[64 * c:64 * c + 64, h, j:j + w], start=True, stop=True)
                    last.then_inc(sc_full, 1)

            def weights_transposed(u, g):
                b0, b1 = groups_A(u)[g]
                tr_begin("a", u, b0)
                for b in range(b0, b1):
                    last = nc.tensor.transpose(TR[:, (b - b0) * P:(b - b0 + 1) * P],
                                               S[u % 2][:, 0, b * P:(b + 1) * P], ident[:, :])
                last.then_inc(tr_full, 1)

            def values(u):
                i, h = u // H, u % H
                if h == 0 and i:
                    pe.wait_ge(o_free, i)
                for b in range(i + 1):
                    if b % 4 == 0:
                        pe.wait_ge(tr_free, TRN["a", u, b] + 1)
                    last = nc.tensor.matmul(OB[:, h * P:(h + 1) * P], vA[:, b, h * P:(h + 1) * P],
                                            aT[u % 2][:, b * P:(b + 1) * P], start=(b == 0), stop=(b == i))
                last.then_inc(pv_done, 1)

            def page_transposes(b, kp, kin, n_in):
                pe.wait_ge(kin[b % 2], n_in * (b // 2 + 1))
                for g in range(2):
                    if b:
                        pe.wait_ge(kts_copied[g], b)
                    for h in range(H):
                        last = nc.tensor.transpose(sc_all[:, g, h * P:(h + 1) * P],
                                                   kp[b % 2][:, g, h * P:(h + 1) * P], ident[:, :])
                    last.then_inc(ktr_full[g], 1)

            def sample_scores(b):
                if b == 0:
                    pe.wait_ge(qpad_ready, 2 * H)
                    pe.wait_ge(new_keys, 2)
                else:
                    pe.wait_ge(ss_read, b)
                for g in range(2):
                    pe.wait_ge(kts_copied[g], b + 1)
                for h in range(H):
                    last = nc.tensor.matmul(sc_all[0:64, 2, 0:NSK], qpadA[:, h, b, :], kTsA[b % 2][:, h, :],
                                            start=(h == 0), stop=(h == H - 1))
                last.then_inc(ss_full, 1)

            def sample_weights(b):
                pe.wait_ge(a_ready, NU + b + 1)
                tr_begin("s", b)
                for j in range(3):
                    m = min(P, NSK - j * P)
                    last = nc.tensor.matmul(TR[0:m, 32 * j:32 * j + 32], Ps[b % 2][0:64, j * P:j * P + m],
                                            comb_t[0:64, :], start=True, stop=True)
                last.then_inc(tr_full, 1)

            def sample_values(b):
                if b == 0:
                    pe.wait_ge(o_free, PT)
                pe.wait_ge(tr_free, TRN["s", b] + 1)
                pe.wait_ge(v_in[b % 2], 32 * (b // 2 + 1))
                for h in range(H):
                    for j in range(3):
                        m = min(P, NSK - j * P)
                        v = vpage[b % 2][:, j, h * P:(h + 1) * P] if j < 2 else vA[0:m, PT, h * P:(h + 1) * P]
                        last = nc.tensor.matmul(OB[:, h * NS_TOK + QB * b:h * NS_TOK + QB * (b + 1)], v,
                                                aTs[b % 2][0:m, j, QB * h:QB * (h + 1)],
                                                start=(j == 0), stop=(j == 2))
                last.then_inc(pv_done, 1)

            def tail_mean(k):
                n, _ = tail_of(k)
                pe.wait_ge(osq_done, k + 1)
                tr_begin("mean", k)
                nc.tensor.matmul(TR[:, 0:H * n], meanm[:, :], sq[:, 0:H * n], start=True, stop=True)\
                    .then_inc(tr_full, 1)

            pe.wait_ge(tr_free, TRN["norm", STAGE["X"][-2]] + 1)
            hv_wait_free(pe, STAGE["X"][-1])
            for u in range(STEPS_A + 1):
                jobs = heavy_A(u) if u < STEPS_A else []
                if u < NU:
                    scores(u)
                elif u == NU:
                    pe.wait_ge(sc_read, 2 * NU)
                    page_transposes(0, kpage, k_in, 32)
                elif u < STEPS_A:
                    sample_scores(u - NU)
                    if u - NU + 1 < NB:
                        page_transposes(u - NU + 1, kpage, k_in, 32)
                if 1 <= u <= NU:
                    pe.wait_ge(a_ready, u)
                    weights_transposed(u - 1, 0)
                for n in jobs:
                    heavy(n)
                if 1 <= u <= NU:
                    if len(groups_A(u - 1)) > 1:
                        weights_transposed(u - 1, 1)
                    values(u - 1)
                elif u > NU:
                    sample_weights(u - 1 - NU)
                    sample_values(u - 1 - NU)
                if u == NU:
                    sample_scores(0)
                    page_transposes(1, kpage, k_in, 32)
                if u % 4 == 1 and 5 <= u <= 33:
                    tail_mean((u - 5) // 4)

            heavy(STAGE["R"][0])
            tail_mean(PT)
            heavy(STAGE["R"][1])
            heavy(STAGE["R"][2])
            heavy(STAGE["V"][0])
            pe.wait_ge(gw_in, 32)
            for c, (c0, cw) in enumerate(CH):
                hv_wait_free(pe, STAGE["R"][c])
                for k in range(2):
                    x = 2 * c + k
                    if x >= 4:
                        pe.wait_ge(lg_read, x - 3)
                    nc.tensor.matmul(sc_all[:, x % 4, 0:cw], wa2[0:16, k * P:(k + 1) * P], gr[0:16, c0:c0 + cw],
                                     start=True, stop=True).then_inc(lg_full, 1)
            for n in list(STAGE["V"])[1:] + list(STAGE["Z"]):
                heavy(n)

            def decayed_transposed(r):
                n = ROWS_TILE(r)
                pe.wait_ge(kd_ready, r + 1)
                tr_begin("kd", r)
                for k in range(2):
                    last = nc.tensor.transpose(TR[0:n, k * P:(k + 1) * P], kd[:, k, 0:n], ident[:, :])
                last.then_inc(tr_full, 1)

            def level(r, lc):
                n, x = ROWS_TILE(r), lc % 2
                pe.wait_ge(lv_ready, lc + 1)
                if lc >= 2:
                    pe.wait_ge(masked, lc - 1)
                for k in range(2):
                    last = nc.tensor.matmul(sc_all[0:n, x, 2 * n * k:2 * n * (k + 1)], kz[x][:, k, 0:n],
                                            qz[x][:, :, k, 0:n], start=True, stop=True)
                last.then_inc(at_full, 1)

            def updates(r, j, count, done, full):
                n = ROWS_TILE(r)
                pe.wait_ge(kdz_ready, count + 1)
                for k in range(2):
                    last = nc.tensor.matmul(sc_all[:, 2 + j, 256 * k:256 * (k + 1)], kdz[j][0:n, k, :],
                                            gv[0:n, r, 256 * k:256 * (k + 1)], start=True, stop=True)
                last.then_inc(full, 1)

            hv_wait_free(pe, STAGE["V"][-1])
            for r in range(PT):
                jobs = STAGE["PA"][5 * r:5 * r + 5]
                heavy(jobs[0])
                if r:
                    tail_mean(PT + r)
                decayed_transposed(r)
                heavy(jobs[1])
                level(r, 3 * r)
                heavy(jobs[2])
                level(r, 3 * r + 1)
                if r:
                    pe.wait_ge(st_ready, 2 * r)
                for j in range(2):
                    updates(r, j, 2 * r + j, None, u_full)
                heavy(jobs[3])
                level(r, 3 * r + 2)
                heavy(jobs[4])
                pe.wait_ge(att_ready, r + 1)
                pe.wait_ge(o_free, PT + 1 + r)
                pe.wait_ge(st_ready, 2 * r + 1)
                pe.wait_ge(st_zero, 1)
                for h in range(H):
                    nc.tensor.matmul(OB[:, h * P:(h + 1) * P], gv[:, r, h * P:(h + 1) * P], att[:, h, :],
                                     start=True, stop=False)
                    for j in range(2):
                        last = nc.tensor.matmul(OB[:, h * P + GC * j:h * P + GC * (j + 1)],
                                                St[(2 * r + j) % 3][:, h // 2, :],
                                                qe[:, h % 2, h // 2, GC * j:GC * (j + 1)], start=False, stop=(j == 1))
                last.then_inc(o_full, 1)
            r = PT
            jobs = STAGE["PA"][5 * PT:]
            heavy(jobs[0])
            tail_mean(2 * PT)
            decayed_transposed(r)
            level(r, 3 * PT)
            pe.wait_ge(st_ready, 2 * PT)
            pe.wait_ge(masked, 3 * PT + 1)
            pe.wait_ge(o_free, PT + 1 + r)
            for b in range(NB):
                if b:
                    heavy(jobs[b])
                pe.wait_ge(st_in[(2 + b) % 3], 16 * (b // 3 + 1))
                for h in range(H):
                    o = OB[:, h * NS_TOK + QB * b:h * NS_TOK + QB * (b + 1)]
                    nc.tensor.matmul(o, gv[0:NS_TOK, r, h * P:(h + 1) * P], att[0:NS_TOK, h, QB * b:QB * (b + 1)],
                                     start=True, stop=False)
                    last = nc.tensor.matmul(o, St[(2 + b) % 3][:, h // 2, :],
                                            qe[:, h % 2, h // 2, QB * b:QB * (b + 1)], start=False, stop=True)
                last.then_inc(vb_done, 1)
                if b >= 2:
                    pe.wait_ge(bst_ready, b - 1)
                updates(r, b % 2, 2 * PT + b, None, bu_full)

            def norm_jobs_Q():
                for n in STAGE["Q"]:
                    heavy(n)
                    if n - 1 in NJ:
                        norm_transposes(n - 1)

            heavy(STAGE["MZ"][0])
            tail_mean(2 * PT + 1)
            for n in list(STAGE["MZ"])[1:]:
                heavy(n)
            norm_jobs_Q()

            def m_scores(i):
                b0 = 2 * (i % 2)
                if i >= 2:
                    pe.wait_ge(m_exp, i - 1)
                for h in range(H):
                    last = nc.tensor.matmul(sc_all[:, b0 + h // 2, NMEM * (h % 2):NMEM * (h % 2 + 1)],
                                            mqT[:, h, i * P:(i + 1) * P], mkT[:, h, :], start=True, stop=True)
                last.then_inc(m_full, 1)

            def m_transposed(i, g):
                tr_begin("m", i, g)
                for x in range(4):
                    h, kb = 2 * g + x // 2, x % 2
                    last = nc.tensor.transpose(TR[:, x * P:(x + 1) * P], Pm[:, h, kb * P:(kb + 1) * P], ident[:, :])
                last.then_inc(tr_full, 1)

            def m_values(i):
                if i:
                    pe.wait_ge(mt_done, i)
                else:
                    pe.wait_ge(o_free, 2 * PT + 2)
                for h in range(H):
                    pe.wait_ge(tr_free, TRN["m", i, h // 2] + 1)
                    for kb in range(2):
                        last = nc.tensor.matmul(OB[:, h * P:(h + 1) * P], mv[:, kb, h * P:(h + 1) * P],
                                                PmT[:, 2 * h + kb, :], start=(kb == 0), stop=(kb == 1))
                last.then_inc(om_full, 1)

            def m_pages(b):
                pe.wait_ge(km_in[b % 2], 16 * (b // 2 + 1))
                for g in range(2):
                    if b:
                        pe.wait_ge(mts_copied[g], b)
                    for h in range(H):
                        last = nc.tensor.transpose(sc_all[:, g, h * P:(h + 1) * P],
                                                   kpageM[b % 2][:, g, h * P:(h + 1) * P], ident[:, :])
                    last.then_inc(mtr_full[g], 1)

            def m_sample_scores(b):
                if b == 0:
                    pe.wait_ge(qm_ready, H)
                else:
                    pe.wait_ge(m_exp, PT + b)
                for g in range(2):
                    pe.wait_ge(mts_copied[g], b + 1)
                for h in range(H):
                    last = nc.tensor.matmul(sc_all[0:32, 2, 0:NMEM], qpadM[:, h, b, :], kTsM[:, h, :],
                                            start=(h == 0), stop=(h == H - 1))
                last.then_inc(ms_full, 1)

            def m_sample_values(b):
                if b == 0:
                    pe.wait_ge(mt_done, PT)
                pe.wait_ge(tr_free, TRN["ms", b] + 1)
                pe.wait_ge(vm_in[b % 2], 16 * (b // 2 + 1))
                for h in range(H):
                    for kb in range(2):
                        last = nc.tensor.matmul(OB[:, h * NS_TOK + QB * b:h * NS_TOK + QB * (b + 1)],
                                                vpageM[b % 2][:, kb, h * P:(h + 1) * P],
                                                aTsM[:, kb, QB * h:QB * (h + 1)], start=(kb == 0), stop=(kb == 1))
                last.then_inc(om_full, 1)

            norm_transposes(STAGE["Q"][-1])
            pe.wait_ge(tr_free, TRN["norm", STAGE["Q"][-1]] + 1)
            m_scores(0)
            for i in range(PT):
                jobs = STAGE["PB"][3 * i:3 * i + 3]
                heavy(jobs[0])
                if i + 1 < PT:
                    m_scores(i + 1)
                pe.wait_ge(m_ready, i + 1)
                m_transposed(i, 0)
                heavy(jobs[1])
                m_transposed(i, 1)
                heavy(jobs[2])
                m_values(i)
            pe.wait_ge(m_exp, PT)
            for b in range(NB):
                jobs = STAGE["PB"][3 * (PT + b):3 * (PT + b) + 3]
                m_pages(b)
                heavy(jobs[0])
                m_sample_scores(b)
                heavy(jobs[1])
                pe.wait_ge(m_ready, PT + b + 1)
                tr_begin("ms", b)
                for kb in range(2):
                    last = nc.tensor.transpose(TR[:, 32 * kb:32 * kb + 32], PsM[0:32, kb * P:(kb + 1) * P],
                                               ident[0:32, 0:32])
                last.then_inc(tr_full, 1)
                heavy(jobs[2])
                m_sample_values(b)
            for s in ("PM", "O"):
                for n in STAGE[s]:
                    heavy(n)

        @block.scalar
        def _(act):
            steps = [0]

            def settle(ins):
                steps[0] += 1
                ins.then_inc(act_step, 1)
                act.wait_ge(act_step, steps[0])

            def tr_wait(*use):
                act.wait_ge(tr_full, TRN[use] + 1)

            def heavy(n):
                job = JOBS[n]
                bank = HV[n % 2]
                if job[0] == "rows":
                    _, kind, r = job
                    rows = P if kind in ("mk", "mv") else ROWS_TILE(r)
                    hv_wait_full(act, n)
                    if kind in NORMED:
                        m, g = NJ.index(n), W // NORMED[kind]
                        if m:
                            act.wait_ge(gsum_done, m)
                        nc.scalar.activation(sq[0:rows, :], bank[0:rows, :], ACT.Square).then_inc(sq_done, 1)
                        act.wait_ge(gsum_done, m + 1)
                        nc.scalar.activation(gstat[0:rows, 1, 0:g], gstat[0:rows, 0, 0:g], ACT.Sqrt,
                                             bias=eps[0:rows, :], scale=float(g) / W).then_inc(groot_done, 1)
                    else:
                        dst = {"v": vA, "mv": mv, "gv": gv}[kind][0:rows, r, :]
                        nc.scalar.copy(dst, bank[0:rows, :]).then_inc(hv_free[n % 2], 1)
                elif job[0] == "out":
                    return
                else:
                    _, kind, f, c = job
                    c0, cw = CH[c]
                    if job[0] == "up":
                        return
                    hv_wait_full(act, n)
                    if n in ZJ:
                        m = ZJ.index(n)
                        if m >= 2:
                            hv_wait_free(act, tanh_reader(ZJ[m - 2]))
                        out = nc.scalar.activation(tanh[m % 2][:, 0:cw], bank[:, 0:cw], ACT.Tanh, scale=0.5)
                        out.then_inc(hv_free[n % 2] if job[0] == "gate" else tanh_done, 1)
                    elif kind == "gr":
                        nc.scalar.copy(gr[0:16, c0:c0 + cw], bank[0:16, 0:cw]).then_inc(hv_free[n % 2], 1)
                    else:
                        dst, s = (gqT, 0.125) if kind == "gq" else (gkT, 1.0)
                        nc.scalar.mul(dst[:, f, c0:c0 + cw], bank[:, 0:cw], s).then_inc(hv_free[n % 2], 1)

            def row_stat(t):
                n = TILES[t][1]
                act.wait_ge(x_loaded[t % 2], 16 * (t // 2 + 1))
                if t >= 1:
                    act.wait_ge(xn_done, t)
                settle(nc.scalar.activation(junk[0:n, :], x_in[t % 2][0:n, :], ACT.Square,
                                            accum_out=rstat[0:n, 0:1]))
                nc.scalar.activation(rstat[0:n, 1:2], rstat[0:n, 0:1], ACT.Sqrt, bias=eps[0:n, :],
                                     scale=1.0 / D).then_inc(root_done, 1)

            def norm_evict(n):
                dst, rows = norm_dest(n)
                tr_wait("norm", n)
                src = TR[:, :].rearrange("p (h t) -> p h t", h=H)[:, :, 0:rows]
                g = {"q": GQA, "mq": GQM}.get(JOBS[n][1])
                if g is None:
                    nc.scalar.copy(dst, src).then_inc(tr_free, 1)
                else:
                    nc.scalar.activation(dst, src, ACT.Copy, scale=gcol[:, g:g + 1]).then_inc(tr_free, 1)

            act.wait_ge(consts_ready, 1)
            row_stat(0)
            for n in STAGE["X"]:
                kind, r = JOBS[n][1], JOBS[n][2]
                if kind in ("mk", "q") and (t := r + (0 if kind == "mk" else NMT)) + 1 < NT:
                    row_stat(t + 1)
                heavy(n)
                if n - 1 in NJ:
                    norm_evict(n - 1)

            def tail_square(k):
                n, _ = tail_of(k)
                act.wait_ge(o_free, k + 1)
                if k:
                    act.wait_ge(tr_full, TRN["mean", k - 1] + 1)
                nc.scalar.activation(sq[:, 0:H * n], og[:, 0:H * n], ACT.Square).then_inc(osq_done, 1)

            def tail_root(k):
                n, _ = tail_of(k)
                tr_wait("mean", k)
                if k:
                    act.wait_ge(tail_done, k)
                nc.scalar.activation(rs_t[:, 0:H * n], TR[:, 0:H * n], ACT.Sqrt, bias=eps[:, :]).then_inc(tr_free, 1)

            def exps(u):
                nk = (u // H + 1) * P
                act.wait_ge(nmx_ready, u + 1)
                for c in range(2):
                    last = nc.scalar.activation(S[u % 2][:, c, 0:nk], S[u % 2][:, c, 0:nk], ACT.Exp,
                                                bias=nmx[:, c:c + 1], accum_out=psum_r[:, c:c + 1])
                last.then_inc(p_ready, 1)

            def weights_evict(u, g):
                b0, b1 = groups_A(u)[g]
                tr_wait("a", u, b0)
                if u >= 2:
                    act.wait_ge(pv_done, u - 1)
                nc.scalar.copy(aT[u % 2][:, b0 * P:b1 * P], TR[:, 0:(b1 - b0) * P]).then_inc(tr_free, 1)

            def page_evict(b, dst, g):
                act.wait_ge(ktr_full[g], b + 1)
                nc.scalar.copy(dst[:, :, g * P:(g + 1) * P], sc_all[:, g, :].rearrange("p (h t) -> p h t", h=H))\
                    .then_inc(kts_copied[g], 1)

            def sample_exp(b):
                act.wait_ge(nmx_ready, NU + b + 1)
                nc.scalar.activation(Ps[b % 2][0:64, :], Ps[b % 2][0:64, :], ACT.Exp, bias=nmx[0:64, 0:1],
                                     accum_out=psum_r[0:64, 0:1]).then_inc(p_ready, 1)

            def sample_evict(b):
                tr_wait("s", b)
                if b >= 2:
                    act.wait_ge(pv_done, NU + b - 1)
                nc.scalar.copy(aTs[b % 2][:, 0:2, :], TR[:, 0:64].rearrange("p (j n) -> p j n", j=2))
                nc.scalar.copy(aTs[b % 2][0:64, 2, :], TR[0:64, 64:96]).then_inc(tr_free, 1)

            nc.scalar.activation(lam_sum[:, 2:4], lam_sum[:, 0:2], ACT.Exp).then_inc(lam_exp, 1)
            for i in range(2):
                act.wait_ge(rows_out[i], ROWS_OUT[i])
            for u in range(STEPS_A + 1):
                jobs = heavy_A(u) if u < STEPS_A else []
                if 1 <= u <= NU:
                    if u == NU:
                        act.wait_ge(sc_read, 2 * NU)
                        page_evict(0, kTsA[0], 1)
                    weights_evict(u - 1, 0)
                if u < NU:
                    exps(u)
                elif NU < u < STEPS_A:
                    if u - NU + 1 < NB:
                        if u - NU + 1 >= 2:
                            act.wait_ge(ss_full, u - NU)
                        page_evict(u - NU + 1, kTsA[(u - NU + 1) % 2], 1)
                    sample_exp(u - NU)
                for n in jobs:
                    heavy(n)
                if 1 <= u <= NU:
                    if len(groups_A(u - 1)) > 1:
                        weights_evict(u - 1, 1)
                elif u > NU:
                    sample_evict(u - 1 - NU)
                if u == NU:
                    page_evict(1, kTsA[1], 1)
                    sample_exp(0)
                if u % 4 == 0 and 4 <= u <= 32:
                    tail_square(u // 4 - 1)
                if u % 4 == 1 and 5 <= u <= 33:
                    tail_root((u - 5) // 4)
            tail_square(PT)

            act.wait_ge(out_done, ROWS_OUT_V)
            act.wait_ge(pv_done, NU + NB)
            heavy(STAGE["R"][0])
            tail_root(PT)
            for n in [*list(STAGE["R"])[1:], *list(STAGE["V"])[:2]]:
                heavy(n)
            act.wait_ge(lg_read, 6)
            settle(nc.scalar.activation(lsig, lsig, ACT.Abs))
            settle(nc.scalar.activation(lsig, lsig, ACT.Exp, scale=-1.0))
            nc.scalar.activation(lsig, lsig, ACT.Ln, bias=1.0).then_inc(lsig_done, 1)
            for n in [*list(STAGE["V"])[2:], *STAGE["Z"]]:
                heavy(n)

            def decays(r):
                n, L = ROWS_TILE(r), (GC if r < PT else QB)
                b = bb[:, :, r * P:r * P + n]
                act.wait_ge(gd_in, r + 1)
                if r:
                    act.wait_ge(st_ready, 2 * r)
                nc.scalar.activation(edel[:, :, 0:n], edel[:, :, 0:n], ACT.Exp, scale=1.0 / 16)
                nc.scalar.activation(dlt[:, :, 0:n], b, ACT.Exp, scale=1.0 / 16)
                nc.scalar.activation(dec[:, :, 0:n // L], b.rearrange("p k (c l) -> p k c l", l=L)[:, :, :, L - 1],
                                     ACT.Exp, scale=1.0 / 16).then_inc(gd_exp, 1)

            def decayed_evict(r):
                n = ROWS_TILE(r)
                tr_wait("kd", r)
                if r:
                    act.wait_ge(kdz_ready, 2 * r)
                nc.scalar.copy(kdt[0:n, :], TR[0:n, 0:256]).then_inc(tr_free, 1)

            def level_exps(r, lc):
                n = ROWS_TILE(r)
                act.wait_ge(lv_in, lc + 1)
                nc.scalar.activation(dk[:, :, 0:n], dk[:, :, 0:n], ACT.Exp, scale=-1.0 / 16)
                nc.scalar.activation(dq[:, :, 0:n], dq[:, :, 0:n], ACT.Exp, scale=1.0 / 16).then_inc(lv_exp, 1)

            for r in range(PT):
                jobs = STAGE["PA"][5 * r:5 * r + 5]
                decays(r)
                heavy(jobs[0])
                if r:
                    tail_root(PT + r)
                level_exps(r, 3 * r)
                decayed_evict(r)
                heavy(jobs[1])
                level_exps(r, 3 * r + 1)
                heavy(jobs[2])
                level_exps(r, 3 * r + 2)
                heavy(jobs[3])
                heavy(jobs[4])
                tail_square(PT + 1 + r)
            jobs = STAGE["PA"][5 * PT:]
            decays(PT)
            heavy(jobs[0])
            tail_root(2 * PT)
            level_exps(PT, 3 * PT)
            decayed_evict(PT)
            for n in jobs[1:]:
                heavy(n)
            tail_square(2 * PT + 1)

            heavy(STAGE["MZ"][0])
            tail_root(2 * PT + 1)
            for n in list(STAGE["MZ"])[1:]:
                heavy(n)
            for n in STAGE["Q"]:
                heavy(n)
                if n - 1 in NJ:
                    norm_evict(n - 1)
            norm_evict(STAGE["Q"][-1])

            def m_exps(i):
                act.wait_ge(m_max, i + 1)
                if i:
                    act.wait_ge(tr_full, TRN["m", i - 1, 1] + 1)
                b0 = 2 * (i % 2)
                for h in range(H):
                    last = nc.scalar.activation(Pm[:, h, :], sc_all[:, b0 + h // 2, NMEM * (h % 2):NMEM * (h % 2 + 1)],
                                                ACT.Exp, bias=nmx[:, h:h + 1], accum_out=psum_r[:, h:h + 1])
                last.then_inc(m_exp, 1)

            def m_evict(i, g):
                tr_wait("m", i, g)
                if i:
                    act.wait_ge(om_full, i)
                nc.scalar.copy(PmT[:, 4 * g:4 * g + 4, :], TR[:, :].rearrange("p (x t) -> p x t", x=4)).then_inc(tr_free, 1)

            m_exps(0)
            for i in range(PT):
                jobs = STAGE["PB"][3 * i:3 * i + 3]
                heavy(jobs[0])
                m_evict(i, 0)
                heavy(jobs[1])
                m_evict(i, 1)
                if i + 1 < PT:
                    m_exps(i + 1)
                heavy(jobs[2])
            for b in range(NB):
                jobs = STAGE["PB"][3 * (PT + b):3 * (PT + b) + 3]
                act.wait_ge(mtr_full[1], b + 1)
                if b:
                    act.wait_ge(ms_full, b)
                nc.scalar.copy(kTsM[:, :, P:2 * P], sc_all[:, 1, :].rearrange("p (h t) -> p h t", h=H))\
                    .then_inc(mts_copied[1], 1)
                heavy(jobs[0])
                act.wait_ge(m_max, PT + b + 1)
                if b:
                    act.wait_ge(tr_full, TRN["ms", b - 1] + 1)
                nc.scalar.activation(PsM[0:32, :], sc_all[0:32, 2, 0:NMEM], ACT.Exp, bias=nmx[0:32, 0:1],
                                     accum_out=psum_r[0:32, 0:1]).then_inc(m_exp, 1)
                heavy(jobs[1])
                tr_wait("ms", b)
                if b:
                    act.wait_ge(om_full, PT + b)
                nc.scalar.copy(aTsM, TR[:, 0:64].rearrange("p (k n) -> p k n", k=2)).then_inc(tr_free, 1)
                heavy(jobs[2])
            for n in STAGE["PM"]:
                heavy(n)

        @block.vector
        def _(dve):
            steps = [0]

            def settle(ins):
                steps[0] += 1
                ins.then_inc(dve_step, 1)
                dve.wait_ge(dve_step, steps[0])

            def heavy(n):
                job = JOBS[n]
                bank = HV[n % 2]
                if job[0] == "rows":
                    _, kind, r = job
                    if kind not in NORMED:
                        return
                    rows = P if kind == "mk" else ROWS_TILE(r)
                    m, wd = NJ.index(n), NORMED[kind]
                    g = W // wd
                    dst = nrm_of(n)[0:rows, :].rearrange("p (g d) -> p g d", g=g)
                    dve.wait_ge(sq_done, m + 1)
                    nc.vector.reduce_sum(gstat[0:rows, 0, 0:g], sq[0:rows, :].rearrange("p (g d) -> p g d", g=g),
                                         axis=AX.X).then_inc(gsum_done, 1)
                    dve.wait_ge(groot_done, m + 1)
                    settle(nc.vector.reciprocal(gstat[0:rows, 2, 0:g], gstat[0:rows, 1, 0:g]))
                    if m >= 2:
                        dve.wait_ge(tr_full, TRN["norm", NJ[m - 2]] + 1)
                        if NJ[m - 2] in KJ:
                            dve.wait_ge(rows_out[m % 2], 16 * sum(1 for x in KJ if x < n and NJ.index(x) % 2 == m % 2))
                    nc.vector.tensor_tensor(out=dst, in0=bank[0:rows, :].rearrange("p (g d) -> p g d", g=g),
                                            in1=bc(gstat[0:rows, 2, 0:g], wd), op=ALU.mult).then_inc(hv_free[n % 2], 1)
                    if n in KJ:
                        hv_wait_free(dve, n)
                        row = (gka_row if kind == "k" else gkm_row)[0:rows, :]
                        nc.vector.tensor_tensor(out=dst, in0=dst,
                                                in1=row.unsqueeze(1).to_broadcast([rows, g, wd]),
                                                op=ALU.mult).then_inc(nrm_done, 1)
                elif job[0] == "cols":
                    _, kind, f, c = job
                    if n not in ZJ:
                        return
                    c0, cw = CH[c]
                    m = ZJ.index(n)
                    dve.wait_ge(tanh_done, sum(1 for x in ZJ[:m + 1] if JOBS[x][0] == "cols"))
                    nc.vector.scalar_tensor_tensor(out=z_of(kind)[:, f, c0:c0 + cw], in0=tanh[m % 2][:, 0:cw],
                                                   scalar=1.0, in1=bank[:, 0:cw], op0=ALU.add, op1=ALU.mult)\
                        .then_inc(hv_free[n % 2], 1)

                elif job[0] == "up":
                    _, br, f, c = job
                    c0, cw = CH[c]
                    hv_wait_full(dve, n)
                    hv_wait_free(dve, n - 1)
                    m = ZJ.index(n - 1)
                    if br == 0:
                        out = merged[:, f, c0:c0 + cw]
                    else:
                        x = 3 * KD * (br - 1) + 3 * f + c
                        if x >= 2:
                            dve.wait_ge(madd_done, x - 1)
                        out = tmp[x % 2][:, 0:cw]
                    nc.vector.scalar_tensor_tensor(out=out, in0=tanh[m % 2][:, 0:cw], scalar=1.0,
                                                   in1=bank[:, 0:cw], op0=ALU.add, op1=ALU.mult)                        .then_inc(hv_free[n % 2], 1)
                elif job[0] == "out":
                    _, r, j = job
                    rows = ROWS_TILE(r)
                    hv_wait_full(dve, n)
                    if j == 0:
                        dve.wait_ge(xr_in[r % 2], 16 * (r // 2 + 1))
                        if r >= 2:
                            dve.wait_ge(y_out[r % 2], 16 * (r // 2))
                    nc.vector.tensor_tensor(out=y_row[r % 2][0:rows, j * W:(j + 1) * W], in0=bank[0:rows, :],
                                            in1=x_res[r % 2][0:rows, j * W:(j + 1) * W], op=ALU.add)                        .then_inc(hv_free[n % 2], 1)

            nc.vector.memset(eps[:, :], EPS)
            dve.wait_ge(consts_in, 16 * N_CONSTS)
            settle(nc.vector.tensor_scalar(gcol[:, GQA:GQA + 1], gcol[:, GQA:GQA + 1], 0.125, None, ALU.mult))
            settle(nc.vector.tensor_scalar(gcol[:, GQM:GQM + 1], gcol[:, GQM:GQM + 1], P ** -0.5, None, ALU.mult))
            settle(nc.vector.tensor_scalar(gcol[:, GOA:GOA + 1], gcol[:, GOA:GOA + 1], 0.25 * (1.0 - LAM_INIT), None, ALU.mult))
            settle(nc.vector.tensor_scalar(gcol[:, GOB:GOB + 1], gcol[:, GOB:GOB + 1], 0.25, None, ALU.mult))
            for i in range(2):
                settle(nc.vector.tensor_tensor(out=nrm[1][:, 0:64], in0=nrm[0][:, 128 * i:128 * i + 64],
                                               in1=nrm[0][:, 128 * i + 64:128 * i + 128], op=ALU.mult))
                settle(nc.vector.reduce_sum(lam_sum[:, i:i + 1], nrm[1][:, 0:64], axis=AX.X))
            nc.vector.tensor_copy(lam_sum[:, 2:4], lam_sum[:, 0:2]).then_inc(consts_ready, 1)

            def x_normed(t):
                rows = TILES[t][1]
                dve.wait_ge(root_done, t + 1)
                settle(nc.vector.reciprocal(rstat[0:rows, 2:3], rstat[0:rows, 1:2]))
                if t:
                    dve.wait_ge(xt_full, 2 * t)
                nc.vector.tensor_scalar(xn[0:rows, :], x_in[t % 2][0:rows, :], rstat[0:rows, 2:3], None,
                                        ALU.mult).then_inc(xn_done, 1)

            def x_evict(t):
                rows = TILES[t][1]
                for j in range(2):
                    dve.wait_ge(xt_full, 2 * t + j + 1)
                    src = sc_all[:, j, :].rearrange("p (k t) -> p k t", k=4)[:, :, 0:rows]
                    g = (gmem if t < NMT else gx)[:, 4 * j:4 * j + 4]
                    dst = (hT_mem[:, 4 * j:4 * j + 4, t * P:(t + 1) * P] if t < NMT else
                           hT[:, 4 * j:4 * j + 4, (t - NMT) * P:(t - NMT) * P + rows])
                    nc.vector.tensor_tensor(out=dst, in0=src, in1=bc(g, rows), op=ALU.mult).then_inc(xt_done, 1)

            x_normed(0)
            x_evict(0)
            for n in STAGE["X"]:
                kind, r = JOBS[n][1], JOBS[n][2]
                nxt = kind in ("mk", "q") and (t := r + (0 if kind == "mk" else NMT)) + 1 < NT
                if nxt:
                    x_normed(t + 1)
                heavy(n)
                if nxt:
                    x_evict(t + 1)

            def o_ready(k):
                if k <= PT:
                    dve.wait_ge(pv_done, H * (k + 1) if k < PT else NU + NB)
                elif k <= 2 * PT:
                    dve.wait_ge(o_full, k - PT)
                else:
                    dve.wait_ge(vb_done, NB)

            def tail_copy(k):
                n, _ = tail_of(k)
                o_ready(k)
                if k:
                    dve.wait_ge(tail_done, k)
                nc.vector.tensor_copy(og[:, 0:H * n], OB[:, 0:H * n]).then_inc(o_free, 1)

            def tail_final(k):
                n, z = tail_of(k)
                g = GOA if k <= PT else GOB
                dve.wait_ge(tr_free, TRN["mean", k] + 1)
                settle(nc.vector.reciprocal(rs_t[:, 0:H * n], rs_t[:, 0:H * n]))
                settle(nc.vector.scalar_tensor_tensor(out=og[:, 0:H * n], in0=og[:, 0:H * n],
                                                      scalar=gcol[:, g:g + 1], in1=rs_t[:, 0:H * n],
                                                      op0=ALU.mult, op1=ALU.mult))
                if k <= PT:
                    c = min((k * P + n - 1) // CHW, 2)
                    for x in range(2):
                        hv_wait_free(dve, STAGE["A"][0] + KW * (c + 1) - 1 - x)
                else:
                    hv_wait_free(dve, STAGE["Z"][-1])
                nc.vector.tensor_tensor(out=z, in0=z, in1=o_view(og, n), op=ALU.mult).then_inc(tail_done, 1)

            def softmax_head(u):
                i, h = u // H, u % H
                nk = (i + 1) * P
                if u >= 2:
                    dve.wait_ge(tr_full, TRN["a", u - 2, groups_A(u - 2)[-1][0]] + 1)
                if u:
                    dve.wait_ge(p_ready, u)
                for c in range(2):
                    dve.wait_ge(sc_full, 2 * u + c + 1)
                    nc.vector.tensor_tensor_reduce(
                        out=S[u % 2][:, c, 0:nk], in0=alibi[:, h, NP_TOK - nk:NP_TOK],
                        in1=sc_all[:, 2 * c:2 * c + 2, :].rearrange("p a n -> p (a n)")[:, 0:nk],
                        scale=1.0, scalar=NEG, op0=ALU.add, op1=ALU.max,
                        accum_out=mx[:, c:c + 1]).then_inc(sc_read, 1)
                dve.wait_ge(sc_read, 2 * u + 2)
                nc.vector.tensor_scalar(nmx[:, 0:2], mx[:, 0:2], -1.0, None, ALU.mult).then_inc(nmx_ready, 1)

            def combine(u):
                nk = (u // H + 1) * P
                dve.wait_ge(p_ready, u + 1)
                settle(nc.vector.reciprocal(coef[:, 0:2], psum_r[:, 0:2]))
                settle(nc.vector.tensor_scalar(coef[:, 1:2], coef[:, 1:2], neg_lam[:, :], None, ALU.mult))
                p0, p1 = S[u % 2][:, 0, 0:nk], S[u % 2][:, 1, 0:nk]
                settle(nc.vector.tensor_scalar(p0, p0, coef[:, 0:1], None, ALU.mult))
                nc.vector.scalar_tensor_tensor(out=p0, in0=p1, scalar=coef[:, 1:2], in1=p0, op0=ALU.mult,
                                               op1=ALU.add).then_inc(a_ready, 1)

            def sample_head(b):
                P_ = Ps[b % 2]
                if b >= 2:
                    dve.wait_ge(tr_full, TRN["s", b - 2] + 1)
                else:
                    dve.wait_ge(pv_done, NU - 1)
                dve.wait_ge(p_ready, NU + b)
                dve.wait_ge(ss_full, b + 1)
                settle(nc.vector.tensor_tensor_reduce(
                    out=P_[0:64, 0:PAST], in0=past_t[0:64, :], in1=sc_all[0:64, 2, 0:PAST], scale=1.0, scalar=NEG,
                    op0=ALU.add, op1=ALU.max, accum_out=mx[0:64, 0:1]))
                nc.vector.tensor_tensor_reduce(
                    out=P_[0:64, PAST:NSK], in0=new_t[0:64, b, :], in1=sc_all[0:64, 2, PAST:NSK], scale=1.0,
                    scalar=mx[0:64, 0:1], op0=ALU.add, op1=ALU.max, accum_out=mx[0:64, 1:2]).then_inc(ss_read, 1)
                dve.wait_ge(ss_read, b + 1)
                nc.vector.tensor_scalar(nmx[0:64, 0:1], mx[0:64, 1:2], -1.0, None, ALU.mult).then_inc(nmx_ready, 1)

            def sample_scale(b):
                dve.wait_ge(p_ready, NU + b + 1)
                settle(nc.vector.reciprocal(coef[0:64, 0:1], psum_r[0:64, 0:1]))
                nc.vector.tensor_scalar(Ps[b % 2][0:64, :], Ps[b % 2][0:64, :], coef[0:64, 0:1], wrow[0:64, :],
                                        ALU.mult, ALU.mult).then_inc(a_ready, 1)

            def page_evict(b, dst, g):
                dve.wait_ge(ktr_full[g], b + 1)
                nc.vector.tensor_copy(dst[:, :, g * P:(g + 1) * P], sc_all[:, g, :].rearrange("p (h t) -> p h t", h=H))\
                    .then_inc(kts_copied[g], 1)

            dve.wait_ge(lam_exp, 1)
            settle(nc.vector.tensor_tensor(out=lam_sum[:, 0:1], in0=lam_sum[:, 3:4], in1=lam_sum[:, 2:3], op=ALU.subtract))
            settle(nc.vector.tensor_scalar(neg_lam[:, :], lam_sum[:, 0:1], LAM_INIT, None, ALU.subtract))
            nc.vector.scalar_tensor_tensor(out=wrow[:, :], in0=small["map"][:, 1:2], scalar=neg_lam[:, :],
                                           in1=small["map"][:, 0:1], op0=ALU.mult, op1=ALU.add)
            dve.wait_ge(alibi_in, 16)
            hv_wait_full(dve, STAGE["X"][-1])
            for h in range(H):
                ins = nc.vector.tensor_scalar(alibi[:, h, :], S[1][:, 0, :], 2.0 ** (-8.0 * (h + 1) / H), None, ALU.mult)
                settle(ins)
            for u in range(STEPS_A + 1):
                jobs = heavy_A(u) if u < STEPS_A else []
                if u < NU:
                    softmax_head(u)
                elif u == NU:
                    page_evict(0, kTsA[0], 0)
                elif u < STEPS_A:
                    sample_head(u - NU)
                    if u - NU + 1 < NB:
                        page_evict(u - NU + 1, kTsA[(u - NU + 1) % 2], 0)
                for n in jobs:
                    heavy(n)
                if u < NU:
                    combine(u)
                elif NU < u < STEPS_A:
                    sample_scale(u - NU)
                if u % 4 == 0 and 4 <= u <= 32:
                    tail_copy(u // 4 - 1)
                if u == NU:
                    dve.wait_ge(tabs_in, 32)
                    sample_head(0)
                    page_evict(1, kTsA[1], 0)
                    sample_scale(0)
                if u % 4 == 1 and 5 <= u <= 33:
                    tail_final((u - 5) // 4)
            tail_copy(PT)

            dve.wait_ge(pv_done, NU + NB)
            tail_final(PT)
            for c, (c0, cw) in enumerate(CH):
                for k in range(2):
                    x = 2 * c + k
                    dve.wait_ge(lg_full, x + 1)
                    nc.vector.tensor_scalar(bb[:, k, c0:c0 + cw], sc_all[:, x % 4, 0:cw], ba_col[:, k:k + 1], 0.0,
                                            ALU.add, ALU.min)
                    nc.vector.tensor_scalar(lsig[:, k, c0:c0 + cw], sc_all[:, x % 4, 0:cw], ba_col[:, k:k + 1],
                                            None, ALU.add).then_inc(lg_read, 1)
            dve.wait_ge(lsig_done, 1)
            settle(nc.vector.tensor_tensor(out=bb, in0=bb, in1=lsig, op=ALU.subtract))
            dve.wait_ge(gw_in, 32)
            for k in range(2):
                settle(nc.vector.tensor_tensor_scan(out=bb[:, k, :], data0=keep, data1=bb[:, k, :], initial=0.0,
                                                    op0=ALU.mult, op1=ALU.add))

            def tile_views(r):
                n, L = ROWS_TILE(r), (GC if r < PT else QB)
                t = slice(r * P, r * P + n)
                return n, L, bb[:, :, t], gqT[:, :, t], gkT[:, :, t]

            def decay_start(r):
                n, L, b, _, _ = tile_views(r)
                b4 = b.rearrange("p k (c l) -> p k c l", l=L)
                for k in range(2):
                    last = nc.vector.tensor_tensor(out=edel[:, k, 0:n].rearrange("p (c l) -> p c l", l=L),
                                                   in0=bc(b4[:, k, :, L - 1], L), in1=b4[:, k], op=ALU.subtract)
                last.then_inc(gd_in, 1)

            def decay_apply(r):
                n, L, b, q, kk = tile_views(r)
                dve.wait_ge(gd_exp, r + 1)
                if r:
                    dve.wait_ge(tr_full, TRN["kd", r - 1] + 1)
                nc.vector.tensor_tensor(out=kd[:, :, 0:n], in0=kk, in1=edel[:, :, 0:n], op=ALU.mult).then_inc(kd_ready, 1)
                if r:
                    dve.wait_ge(o_full, r)
                for x in range(2):
                    last = nc.vector.scalar_tensor_tensor(out=qe[:, x, :, 0:n], in0=q, scalar=half_t[:, x:x + 1],
                                                          in1=dlt[:, :, 0:n], op0=ALU.mult, op1=ALU.mult)
                settle(last)

            def level_operands(r, lc, L, ref, diag):
                n, _, b, q, kk = tile_views(r)
                x = lc % 2
                b4 = b.rearrange("p k (c l) -> p k c l", l=L)
                for k in range(2):
                    last = nc.vector.tensor_tensor(out=dlt[:, k, 0:n].rearrange("p (c l) -> p c l", l=L), in0=b4[:, k],
                                                   in1=bc(b4[:, k, :, ref], L), op=ALU.subtract)
                settle(last)
                d = dlt[:, :, 0:n]
                if diag:
                    nc.vector.tensor_scalar(dq[:, :, 0:n], d, CLIP, -CLIP, ALU.min, ALU.max)
                    nc.vector.tensor_scalar(dk[:, :, 0:n], d, CLIP, -CLIP, ALU.min, ALU.max).then_inc(lv_in, 1)
                else:
                    nc.vector.tensor_scalar(dq[:, :, 0:n], d, 0.0, None, ALU.min)
                    nc.vector.tensor_scalar(dk[:, :, 0:n], d, 0.0, None, ALU.max).then_inc(lv_in, 1)
                dve.wait_ge(lv_exp, lc + 1)
                if lc >= 2:
                    dve.wait_ge(at_full, lc - 1)
                nc.vector.tensor_tensor(out=kz[x][:, :, 0:n], in0=kk, in1=dk[:, :, 0:n], op=ALU.mult)
                for y in range(2):
                    last = nc.vector.scalar_tensor_tensor(out=qz[x][:, y, :, 0:n], in0=q, scalar=half_t[:, y:y + 1],
                                                          in1=dq[:, :, 0:n], op0=ALU.mult, op1=ALU.mult)
                last.then_inc(lv_ready, 1)

            def masked_add(r, lc, mask, first, final):
                n = ROWS_TILE(r)
                dve.wait_ge(at_full, lc + 1)
                if first and r:
                    dve.wait_ge(o_full, r)
                src = sc_all[0:n, lc % 2, 0:H * n].rearrange("p (h t) -> p h t", h=H)
                mk_ = gmask[0:n, mask, 0:n].unsqueeze(1).to_broadcast([n, H, n])
                dst = att if first else atm
                nc.vector.tensor_tensor(out=dst[0:n, :, 0:n], in0=src, in1=mk_, op=ALU.mult).then_inc(masked, 1)
                dve.wait_ge(masked, lc + 1)
                if not first:
                    ins = nc.vector.tensor_tensor(out=att[:, :, :], in0=att[:, :, :], in1=atm[:, :, :], op=ALU.add)
                    if final:
                        ins.then_inc(att_ready, 1)
                    else:
                        settle(ins)

            def split_keys(r, j, count, sel):
                n = ROWS_TILE(r)
                if count >= 2 * PT + 2:
                    dve.wait_ge(bu_full, count - 2 * PT - 1)
                nc.vector.tensor_scalar(kdz[j][0:n, :, :].rearrange("p k d -> p (k d)"), kdt[0:n, :], sel, None,
                                        ALU.mult).then_inc(kdz_ready, 1)

            def state_step(new, old, c, bank, done):
                for k in range(2):
                    for x in range(2):
                        p = slice(64 * x, 64 * x + 64)
                        last = nc.vector.scalar_tensor_tensor(
                            out=new[p, k, :], in0=old[p, k, :], scalar=dec[p, k, c:c + 1],
                            in1=sc_all[p, bank, 256 * k + P * x:256 * k + P * (x + 1)], op0=ALU.mult, op1=ALU.add)
                last.then_inc(done, 1)

            nc.vector.memset(St[0], 0.0).then_inc(st_zero, 1)
            for n in STAGE["Z"]:
                heavy(n)
            dve.wait_ge(st_zero, 1)
            for r in range(PT):
                jobs = STAGE["PA"][5 * r:5 * r + 5]
                decay_start(r)
                decay_apply(r)
                heavy(jobs[0])
                if r:
                    tail_final(PT + r)
                level_operands(r, 3 * r, *LEVELS[0][:2], True)
                heavy(jobs[1])
                dve.wait_ge(tr_free, TRN["kd", r] + 1)
                if r:
                    dve.wait_ge(u_full, 2 * r)
                for j in range(2):
                    split_keys(r, j, 2 * r + j, half_t[:, j:j + 1])
                level_operands(r, 3 * r + 1, *LEVELS[1][:2], False)
                heavy(jobs[2])
                masked_add(r, 3 * r, 0, True, False)
                level_operands(r, 3 * r + 2, *LEVELS[2][:2], False)
                heavy(jobs[3])
                for j in range(2):
                    c = 2 * r + j
                    dve.wait_ge(u_full, c + 1)
                    if c:
                        dve.wait_ge(st_ready, c)
                    state_step(St[(c + 1) % 3], St[c % 3], j, 2 + j, st_ready)
                masked_add(r, 3 * r + 1, 1, False, False)
                heavy(jobs[4])
                masked_add(r, 3 * r + 2, 2, False, True)
                tail_copy(PT + 1 + r)
            jobs = STAGE["PA"][5 * PT:]
            r = PT
            decay_start(r)
            decay_apply(r)
            heavy(jobs[0])
            tail_final(2 * PT)
            level_operands(r, 3 * PT, *LEVELS_S[0][:2], True)
            masked_add(r, 3 * PT, 3, True, False)
            dve.wait_ge(tr_free, TRN["kd", r] + 1)
            dve.wait_ge(u_full, 2 * PT)
            for b in range(2):
                split_keys(r, b, 2 * PT + b, batch_t[0:NS_TOK, b:b + 1])
            for b in range(NB):
                if b:
                    heavy(jobs[b])
                dve.wait_ge(bu_full, b + 1)
                dve.wait_ge(st_in[(2 + b) % 3], 16 * (b // 3 + 1))
                state_step(St[(2 + b) % 3], St[(2 + b) % 3], b, 2 + b % 2, bst_ready)
                if b + 2 < NB:
                    split_keys(r, b % 2, 2 * PT + b + 2, batch_t[0:NS_TOK, b + 2:b + 3])
            tail_copy(2 * PT + 1)

            heavy(STAGE["MZ"][0])
            tail_final(2 * PT + 1)
            for n in list(STAGE["MZ"])[1:] + list(STAGE["Q"]):
                heavy(n)

            def m_maxima(i, src, rows, k):
                if i:
                    dve.wait_ge(m_exp, i)
                settle(nc.vector.reduce_max(mx[0:rows, 0:k], src, axis=AX.X))
                nc.vector.tensor_scalar(nmx[0:rows, 0:k], mx[0:rows, 0:k], -1.0, None, ALU.mult).then_inc(m_max, 1)

            def m_max_of(i):
                dve.wait_ge(m_full, i + 1)
                m_maxima(i, sc_all[:, 2 * (i % 2):2 * (i % 2) + 2, :].rearrange("p a n -> p (a n)")
                         .rearrange("p (h m) -> p h m", h=H), P, H)

            def m_weights(i):
                dve.wait_ge(m_exp, i + 1)
                settle(nc.vector.reciprocal(coef[:, :], psum_r[:, :]))
                for h in range(H):
                    last = nc.vector.tensor_scalar(Pm[:, h, :], Pm[:, h, :], coef[:, h:h + 1], None, ALU.mult)
                last.then_inc(m_ready, 1)

            def m_tail(k):
                n = ROWS_TILE(k)
                dve.wait_ge(om_full, k + 1 if k < PT else PT + NB)
                z = mzT[:, :, k * P:k * P + n]
                nc.vector.scalar_tensor_tensor(out=z, in0=o_view(OB, n), scalar=0.25, in1=z, op0=ALU.mult,
                                               op1=ALU.mult).then_inc(mt_done, 1)

            m_max_of(0)
            for i in range(PT):
                jobs = STAGE["PB"][3 * i:3 * i + 3]
                m_weights(i)
                heavy(jobs[0])
                if i + 1 < PT:
                    m_max_of(i + 1)
                heavy(jobs[1])
                heavy(jobs[2])
                m_tail(i)
            for b in range(NB):
                jobs = STAGE["PB"][3 * (PT + b):3 * (PT + b) + 3]
                dve.wait_ge(mtr_full[0], b + 1)
                if b:
                    dve.wait_ge(ms_full, b)
                nc.vector.tensor_copy(kTsM[:, :, 0:P], sc_all[:, 0, :].rearrange("p (h t) -> p h t", h=H))\
                    .then_inc(mts_copied[0], 1)
                heavy(jobs[0])
                dve.wait_ge(ms_full, b + 1)
                m_maxima(PT + b, sc_all[0:32, 2, 0:NMEM], 32, 1)
                dve.wait_ge(m_exp, PT + b + 1)
                settle(nc.vector.reciprocal(coef[0:32, 0:1], psum_r[0:32, 0:1]))
                nc.vector.tensor_scalar(PsM[0:32, :], PsM[0:32, :], coef[0:32, 0:1], None, ALU.mult).then_inc(m_ready, 1)
                heavy(jobs[1])
                heavy(jobs[2])
            m_tail(PT)
            for s in ("PM", "O"):
                for n in STAGE[s]:
                    heavy(n)


_INS = ["x_prompt", "x_sample", "cache_k_a", "cache_v_a", "page_table", "state_gla", "cache_mem_k",
        "cache_mem_v", "mem_prompt", "norm_x", "w_in", "g_qa", "g_ka", "lam", "g_oa", "w_a2", "b_a",
        "g_ob", "g_qm", "g_km", "norm_mem", "w_mkv", "w_branch", "w_o"]
_OUTS = [(1, NP_TOK, D), (NB, QB, D), (1, 1, NP_TOK, H, P), (1, 1, NP_TOK, H, P),
         (1, NB, QB, H, P), (1, NB, QB, H, P), (1, 1, H, 64, P), (1, NB, H, 64, P),
         (1, 1, NMEM, H, P), (1, 1, NMEM, H, P)]


def kernel(**inputs):
    import concourse.bacc as bacc
    from concourse.bass_utils import run_bass_kernel_spmd

    nc = bacc.Bacc("TRN2", target_bir_lowering=False, num_devices=1)
    arrays, args, outs = {}, [], []
    for name in _INS:
        a = np.ascontiguousarray(inputs[name])
        arrays[name] = a
        args.append(nc.dram_tensor(name, a.shape, mybir.dt.from_np(a.dtype), kind="ExternalInput").ap())
    tabs = {}
    for name, a in shape_tables().items():
        arrays["tab_" + name] = a
        tabs[name] = nc.dram_tensor("tab_" + name, a.shape, F32, kind="ExternalInput").ap()
    for i, shape in enumerate(_OUTS):
        outs.append(nc.dram_tensor(f"out_{i}", shape, F32, kind="ExternalOutput").ap())
    hybrid_step(nc, *args, tabs, *outs)
    r = run_bass_kernel_spmd(nc, [arrays], core_ids=[0])
    return tuple(r.results[0][f"out_{i}"] for i in range(len(_OUTS)))
```

```python
import math
from contextlib import ExitStack

import numpy as np
import concourse.bass as bass
from concourse import mybir

F32 = mybir.dt.float32
F32R = mybir.dt.float32r
I32 = mybir.dt.int32
ALU = mybir.AluOpType
ACT = mybir.ActivationFunctionType
AX = mybir.AxisListType

P = 128
D = 1024
KD = D // P
NP_TOK, NS_TOK = 1024, 64
T = NP_TOK + NS_TOK
NMEM = 256
H = 4
W = 512
KW = W // P
NB = 8
QB = 8
PAST, PAGE = 256, 128
NPG = PAST // PAGE
GC = 64
EPS = 1e-6
LAM_INIT = 0.8 - 0.6 * math.exp(-0.3 * 0)
NEG = -1e30
CLIP = 43.0 * 16.0

C_AQ, C_AK, C_AV, C_AZ = 0, 512, 1024, 1536
C_GQ, C_GK, C_GV, C_GZ, C_GR = 2048, 2304, 2560, 3072, 3584
C_MQ, C_MZ, C_GL = 3600, 4112, 4624

PT = NP_TOK // P
CH = [(0, 364), (364, 364), (728, 360)]
CHW = 364

def shape_tables():
    p = np.arange(P)[:, None]
    tabs = {}
    tabs["ident"] = np.eye(P)
    tabs["mean"] = np.full((P, P), 1.0 / P)
    j = np.arange(NP_TOK)[None, :] - (NP_TOK - P) - p
    tabs["alibi"] = np.where(j <= 0, j, NEG)
    r = np.arange(P)
    half = np.stack([(r < 64), (r >= 64)], 1)
    tabs["half"] = half
    tabs["batch"] = (np.minimum(r, 63)[:, None] // QB == np.arange(NB)[None, :]) & (r < 64)[:, None]
    row = np.arange(P)
    hh, cc, qq = (row // 16) % 4, (row // 8) % 2, row % 8
    slope = 2.0 ** (-8.0 * (hh + 1) / H)
    tabs["past"] = -slope[:, None] * (PAST + qq[:, None] - np.arange(PAST)[None, :])
    new = np.zeros((P, NB, NS_TOK))
    for b in range(NB):
        u = np.arange(NS_TOK)[None, :] - QB * b
        new[:, b] = np.where((u >= 0) & (u <= qq[:, None]), -slope[:, None] * (qq[:, None] - u), NEG)
    tabs["new"] = new.reshape(P, -1)
    tabs["map"] = np.stack([cc == 0, cc == 1], 1)
    comb = np.zeros((P, 32))
    for x in range(64):
        comb[x, hh[x] * 8 + qq[x]] = 1.0
    tabs["comb"] = comb
    s, t = np.arange(P)[:, None], np.arange(P)[None, :]
    tabs["gmask"] = np.concatenate([
        (s // 16 == t // 16) & (s <= t),
        (s // 32 == t // 32) & (s % 32 < 16) & (t % 32 >= 16),
        (s // 64 == t // 64) & (s % 64 < 32) & (t % 64 >= 32),
        (s // 8 == t // 8) & (s <= t)], 1)
    keep = np.ones((P, T))
    keep[:, 0:NP_TOK:GC] = 0
    keep[:, NP_TOK::QB] = 0
    tabs["keep"] = keep
    return {k: np.ascontiguousarray(v, dtype=np.float32) for k, v in tabs.items()}


SMALL = ["ident", "mean", "half", "batch", "map", "comb", "gmask"]


def heavy_jobs():
    jobs, stage = [], {}

    def add(name, some):
        stage[name] = range(len(jobs), len(jobs) + len(some))
        jobs.extend(some)

    add("X", [("rows", k, t) for t in range(NMEM // P) for k in ("mk", "mv")]
        + [("rows", "v", 0)]
        + [("rows", k, x) for r in range(PT + 1) for k, x in (("v", r + 1), ("q", r), ("k", r)) if x <= PT])
    add("A", [("cols", "az", f, c) for c in range(3) for f in range(KW)]
        + [("cols", k, f, c) for k in ("gq", "gk") for f in range(2) for c in range(3)])
    add("R", [("cols", "gr", 0, c) for c in range(3)])
    add("V", [("rows", "gv", r) for r in range(PT + 1)])
    add("Z", [("cols", "gz", f, c) for f in range(KW) for c in range(3)])
    pairs = lambda br: [(k, br, f, c) for f in range(KD) for c in range(3) for k in ("gate", "up")]
    add("PA", pairs(0))
    add("MZ", [("cols", "mz", f, c) for f in range(KW) for c in range(3)])
    add("Q", [("rows", "mq", r) for r in range(PT + 1)])
    add("PB", pairs(1))
    add("PM", pairs(2))
    add("O", [("out", r, j) for r in range(PT + 1) for j in range(2)])
    return jobs, stage


JOBS, STAGE = heavy_jobs()
NORMED = {"mk": 128, "q": 64, "k": 64, "mq": 128}
NJ = [n for n, j in enumerate(JOBS) if j[0] == "rows" and j[1] in NORMED]
KJ = [n for n in NJ if JOBS[n][1] in ("k", "mk")]
ZJ = [n for n, j in enumerate(JOBS) if j[0] == "gate" or (j[0] == "cols" and j[1] in ("az", "gz", "mz"))]


def ring_loads():
    first, last = {}, {}
    for n, j in enumerate(JOBS):
        if j[0] == "cols":
            key = (j[1], j[2] // 2)
        elif j[0] in ("gate", "up"):
            key = ("pair", j[1], j[2])
        else:
            continue
        first.setdefault(key, n)
        last[key] = n
    return [(key, last[key]) for key in first]


LOADS = ring_loads()
LOAD_OF = {key: i for i, (key, _) in enumerate(LOADS)}
STEPS_A = H * PT + NB
COPY_AT = {min(H * (k + 1) + 1, H * PT): k for k in range(PT)}
MEAN_AT = {u + 1: k for u, k in COPY_AT.items()}


def heavy_A(u):
    js, n = STAGE["A"], 27
    return [js[x] for x in range(len(js) * min(u, n) // n, len(js) * min(u + 1, n) // n)]


def groups_A(u):
    nb = u // H + 1
    return [(g, min(g + 4, nb)) for g in range(0, nb, 4)]


def transposed_uses():
    uses = [("norm", n) for n in NJ if n in STAGE["X"]]
    for u in range(1, STEPS_A + 1):
        if u <= H * PT:
            uses += [("a", u - 1, g) for g, _ in groups_A(u - 1)]
        else:
            uses.append(("s", u - 1 - H * PT))
        if u in MEAN_AT:
            uses.append(("mean", MEAN_AT[u]))
    uses.append(("mean", PT))
    for r in range(PT + 1):
        uses += [("kd", r)] + ([("mean", PT + r)] if r else [])
    uses.append(("mean", 2 * PT + 1))
    uses += [("norm", n) for n in NJ if n not in STAGE["X"]]
    for i in range(PT):
        uses += [("m", i, 0), ("m", i, 1)]
    uses += [("ms", b) for b in range(NB)]
    return {key: i for i, key in enumerate(uses)}


TRN = transposed_uses()
LEVELS = [(16, 7, 0), (32, 15, 1), (64, 31, 2)]
LEVELS_S = [(QB, 3, 3)]
N_CONSTS = len(SMALL) - 1 + 9
ROWS_TILE = lambda r: P if r < PT else NS_TOK


def hybrid_step(nc, x_prompt, x_sample, cache_k, cache_v, page_table, state_gla, mem_k, mem_v,
                mem_prompt, norm_x, w_in, g_qa, g_ka, lam, g_oa, w_a2, b_a, g_ob, g_qm, g_km,
                norm_mem, w_mkv, w_branch, w_o, tab,
                y_prompt, y_sample, ka_prompt, va_prompt, ka_sample, va_sample,
                gla_prompt, gla_sample, mk_prompt, mv_prompt):
    ctx = ExitStack()

    def sb(name, shape, dt=F32):
        return ctx.enter_context(nc.sbuf_tensor(name, shape, dt))

    def sem(name):
        return ctx.enter_context(nc.semaphore(name))

    xs = x_sample.rearrange("b q d -> (b q) d")
    NMT = NMEM // P
    TILES = [(mem_prompt[0, t * P:(t + 1) * P, :], P) for t in range(NMT)] + \
            [(x_prompt[0, t * P:(t + 1) * P, :], P) for t in range(PT)] + [(xs, NS_TOK)]
    NT = len(TILES)

    with ctx:
        arena_base = -(-nc.sbuf_base // 32) * 32
        arena = sb("arena", [P, 51928])

        def shaped(v, shape):
            if len(shape) == 1:
                return v
            names = "abcd"[:len(shape)]
            return v.rearrange(f"p ({' '.join(names)}) -> p {' '.join(names)}",
                               **{c: s for c, s in zip(names, shape)})

        def at(off, shape):
            return shaped(arena[:, off:off + int(np.prod(shape))], shape)

        def part(name, off, shape):
            n = int(np.prod(shape))
            t = nc.alloc_sbuf_tensor_at(name, [P, n], F32R, offset=arena_base + 4 * off)
            return shaped(t[:, 0:n], shape)

        def pairs_of(name, places, width):
            return [part(f"{name}{i}_{x}", o + 2 * width * x, [2, width])
                    for i, (o, n) in enumerate(places) for x in range(n)]

        hT = at(0, [KD, T])
        qT, kT, vA = at(8704, [H, T]), at(13056, [H, T]), at(17408, [9, W])
        w_mem, hT_mem = at(8704, [KD, 2 * W]), at(17408, [KD, NMEM])
        wX = [at(22272 + 8192 * i + 4096, [KD, W]) for i in range(2)]
        merged = at(8704, [KD, T])
        w_gv = at(8704, [KD, W])
        azT, gzT = at(22016, [KW, T]), at(26368, [KW, T])
        alibi = at(26368, [H, NP_TOK])
        gqT, gkT = at(30720, [2, T]), at(30720 + 2176, [2, T])
        mqT, mzT = at(30720, [H, T]), at(17408, [KW, T])
        gv = at(17408, [9, W])
        ring = [at(35072 + 2048 * i, [2048]) for i in range(2)]
        mkT, mv = at(39168, [H, NMEM]), at(39168 + 1024, [2, W])
        SCR = 41216
        w_av = at(SCR, [KD, W])
        x_in = [at(SCR + 4096 + 1024 * i, [D]) for i in range(2)]
        xn = at(SCR + 6144, [D])
        junk = at(SCR + 8448 + 1240, [D])
        nrm = [at(SCR + 7168 + 512 * i, [W]) for i in range(2)]
        S = [at(SCR + 2048 * i, [2, NP_TOK]) for i in range(2)]
        aT = [at(SCR + 4096 + 1024 * i, [NP_TOK]) for i in range(2)]
        qpadA = at(SCR + 6144, [H, NB, NS_TOK])
        NSK = PAST + NS_TOK
        kpage = [at(SCR + 1024 * i, [NPG, W]) for i in range(2)]
        vpage = [at(SCR + 2048 + 1024 * i, [NPG, W]) for i in range(2)]
        Ps = [at(SCR + 4096 + 320 * i, [NSK]) for i in range(2)]
        WIN = NS_TOK - QB + NS_TOK * H
        aTs = at(SCR + 4736, [3, WIN])
        otok = at(SCR, [W])
        kTsA = [at(26368 + 1280 * i, [H, NSK]) for i in range(2)]
        past_t, new_t = at(26368 + 2560, [PAST]), at(26368 + 2816, [NB, NS_TOK])
        bb = at(SCR, [2, T])
        GT = SCR + 2176
        lsig = at(GT, [2, T])
        gr = at(GT + 2176, [T])
        keep = at(GT + 3264, [T])
        wa2 = at(GT + 4352, [256])
        edel, dlt, dq, dk = (at(GT + 256 * i, [2, P]) for i in range(4))
        qz = [at(GT + 1024 + 512 * i, [2, 2, P]) for i in range(2)]
        kz = [at(GT + 2048 + 256 * i, [2, P]) for i in range(2)]
        kd = at(GT + 2560, [2, P])
        kdt = at(GT + 2816, [256])
        kdz = [at(GT + 3072 + 256 * i, [2, P]) for i in range(2)]
        att = at(GT + 3584, [H, P])
        atm = at(8704 + 7 * T, [H, P])
        qe = at(GT + 4096, [2, 2, 2, P])
        St = [at(GT + 5120 + 256 * i, [2, P]) for i in range(3)]
        w_mq = at(SCR + 4352, [KD, W])
        Pm = at(SCR + 4352, [H, NMEM])
        PmT = at(SCR + 5376, [8, P])
        qpadM = at(SCR + 6400, [H, NB, 32])
        kpageM = [at(30720 + 1024 * i, [2, W]) for i in range(2)]
        vpageM = [at(30720 + 2048 + 1024 * i, [2, W]) for i in range(2)]
        PsM = at(30720 + 4096, [NMEM])
        kTsM = at(SCR + 4352, [H, NMEM])
        aTsM = at(SCR + 5376, [2, WIN])
        TAIL = SCR + 8448
        distance = at(SCR + 2048, [NP_TOK])
        otokM = at(TAIL + 728, [W])
        nrmM = [at(TAIL + 1240 + 512 * i, [W]) for i in range(2)]
        x_hi = [part(f"x_hi{i}", o, [KD // 2, P]) for i, o in enumerate((38656, SCR + 8192))]
        xs_hi = part("xs_hi", SCR, [KD, NS_TOK])
        wx_hi, wx_lo = ([[part(f"w{k}_{name}{x}", 22272 + 8192 * i + o + 2048 * x, [KD // 2, W]) for x in range(2)]
                         for i, k in enumerate("qk")] for name, o in (("hi", 0), ("lo", 4096)))
        h_hi = pairs_of("h_hi", [(22016, 2), (SCR, 2)], T)
        h_lo = pairs_of("h_lo", [(0, 4)], T)
        mz_hi, mz_lo = pairs_of("mz_hi", [(26368, 2)], T), pairs_of("mz_lo", [(17408, 2)], T)
        wg_hi = [[part(f"wg_hi{i}_{x}", o + step * x, [KD // 2, P]) for x in range(2)]
                 for i, (o, step) in enumerate(((35072 + 1536, 2048), (SCR + 7424, 512)))]
        wg_lo = [part(f"wg_lo{i}", 35072 + 2048 * i, [KD, P]) for i in range(2)]
        wu_lo = [part(f"wu_lo{i}", 35072 + 2048 * i + 1024, [KW, P]) for i in range(2)]
        wu_hi = [part(f"wu_hi{i}", 39168 + 512 * i, [KW, P]) for i in range(2)]
        wo_hi, wo_lo = pairs_of("wo_hi", [(0, 4)], D), pairs_of("wo_lo", [(22016, 4)], D)
        m_hi = [part(f"m_hi{i}", 17408 + 1024 * i, [KD, P]) for i in range(2)]
        m_lo = [part(f"m_lo{i}", 17408 + 2048 + 1024 * i, [KD, P]) for i in range(2)]
        OUT_W = ((0, 4, 30720), (4, 3, SCR + 4352), (7, 1, 39168 + 1024))
        w_out = [at(o + D * k, [D]) for _, n, o in OUT_W for k in range(n)]
        x_res = [at(SCR + 1024 * i, [D]) for i in range(2)]
        y_row = [at(SCR + 2048 + 1024 * i, [D]) for i in range(2)]
        tanh = [at(TAIL + CHW * i, [CHW]) for i in range(2)]
        sq = at(TAIL + 728, [W])
        rs_t = at(TAIL + 728 + 512, [W])
        og = at(TAIL + 728 + 1024, [W])

        small = {k: sb("t_" + k, [P, tab[k].shape[1]]) for k in SMALL}
        ident, meanm = small["ident"], small["mean"]
        half_t, batch_t, comb_t = small["half"], small["batch"], small["comb"]
        gmask = small["gmask"][:, :].rearrange("p (l t) -> p l t", l=4)
        gx, gmem = sb("gx", [P, KD]), sb("gmem", [P, KD])
        gka_row, gkm_row = sb("gka_row", [P, 64]), sb("gkm_row", [P, P])
        ba_col = sb("ba_col", [P, 2])
        gcol = sb("gcol", [P, 4])
        GQA, GQM, GOA, GOB = range(4)
        eps = sb("eps", [P, 1])
        rstat = sb("rstat", [P, 3])
        gstat = sb("gstat", [P, 3, 8])
        lam_sum = sb("lam_sum", [P, 4])
        neg_lam, wrow = sb("neg_lam", [P, 1]), sb("wrow", [P, 1])
        mx, nmx, psum_r, coef = (sb(k, [P, 4]) for k in ("mx", "nmx", "psum_r", "coef"))
        dec = sb("dec", [P, 2, NB])
        pt_sb = sb("pt_sb", [1, NB * NPG], I32)

        sc_all = ctx.enter_context(nc.psum_tensor("scores", [P, 4, W], F32))
        HV = [ctx.enter_context(nc.psum_tensor(f"heavy{i}", [P, W], F32)) for i in range(2)]
        TR = ctx.enter_context(nc.psum_tensor("transposed", [P, W], F32))
        OB = ctx.enter_context(nc.psum_tensor("attended", [P, W], F32))

        tmp = [at(TAIL + 728 + 512 + CHW * i, [CHW]) for i in range(2)]

        hv_full = [sem("hv_full0"), sem("hv_full1")]
        hv_free = [sem("hv_free0"), sem("hv_free1")]
        ring_in = [sem("ring_in0"), sem("ring_in1")]
        tm_w = [sem(f"tm_w{i}") for i in range(7)]
        wo_in = sem("wo_in")
        first_in, consts_in = sem("first_in"), sem("consts_in")
        eps_ready, consts_ready = sem("eps_ready"), sem("consts_ready")
        x_loaded = [sem("x_loaded0"), sem("x_loaded1")]
        root_done, xn_done, xt_full, xt_done = (sem(k) for k in ("root_done", "xn_done", "xt_full", "xt_done"))
        sq_done, gsum_done, groot_done, nrm_done = (sem(k) for k in ("sq_done", "gsum_done", "groot_done", "nrm_done"))
        tr_full, tr_free = sem("tr_full"), sem("tr_free")
        rows_out = [sem("rows_out0"), sem("rows_out1")]
        out_done = sem("out_done")
        tanh_done = sem("tanh_done")
        dve_step, act_step = sem("dve_step"), sem("act_step")
        alibi_in, alibi_ready = sem("alibi_in"), sem("alibi_ready")
        sc_full, sc_read, nmx_ready, p_ready, a_ready = (sem(k) for k in ("sc_full", "sc_read", "nmx_ready", "p_ready", "a_ready"))
        pv_done = sem("pv_done")
        qpad_zero, qpad_ready, new_keys = sem("qpad_zero"), sem("qpad_ready"), sem("new_keys")
        tabs_in, pt_in = sem("tabs_in"), sem("pt_in")
        k_in, v_in = [sem("k_in0"), sem("k_in1")], [sem("v_in0"), sem("v_in1")]
        ktr_full, kts_copied = [sem("ktr_full0"), sem("ktr_full1")], [sem("kts_copied0"), sem("kts_copied1")]
        ss_full, ss_read = sem("ss_full"), sem("ss_read")
        gw_in, lg_full, lg_read, lsig_done = (sem(k) for k in ("gw_in", "lg_full", "lg_read", "lsig_done"))
        gd_in, gd_exp, kd_ready, kdz_ready, u_full, st_ready = (sem(k) for k in ("gd_in", "gd_exp", "kd_ready", "kdz_ready", "u_full", "st_ready"))
        lv_in, lv_exp, lv_ready, at_full, masked, att_ready = (sem(k) for k in ("lv_in", "lv_exp", "lv_ready", "at_full", "masked", "att_ready"))
        st_in, st_out = [sem(f"st_in{i}") for i in range(3)], [sem(f"st_out{i}") for i in range(3)]
        vb_done, st_zero, bst_ready, bu_full = sem("vb_done"), sem("st_zero"), sem("bst_ready"), sem("bu_full")
        madd_done = sem("madd_done")
        m_full, m_max, m_exp, m_ready, om_full, mt_done = (sem(k) for k in ("m_full", "m_max", "m_exp", "m_ready", "om_full", "mt_done"))
        ats_zero, atsm_zero, otok_ready, os_full = sem("ats_zero"), sem("atsm_zero"), sem("otok_ready"), sem("os_full")
        qm_zero, qm_ready, ms_full = sem("qm_zero"), sem("qm_ready"), sem("ms_full")
        km_in, vm_in = [sem("km_in0"), sem("km_in1")], [sem("vm_in0"), sem("vm_in1")]
        mtr_full, mts_copied = [sem("mtr_full0"), sem("mtr_full1")], [sem("mts_copied0"), sem("mts_copied1")]
        xr_in, y_out = [sem("xr_in0"), sem("xr_in1")], [sem("y_out0"), sem("y_out1")]
        x_high, x_split, x_whole, wx_high, wx_split = (sem(k) for k in ("x_high", "x_split", "x_whole", "wx_high", "wx_split"))
        mz_split, h_high = sem("mz_split"), sem("h_high")
        mz_high, h_split, wh_high, w_split = (sem(k) for k in ("mz_high", "h_split", "wh_high", "w_split"))
        wo_high, wo_split, mt_high, mt_split = (sem(k) for k in ("wo_high", "wo_split", "mt_high", "mt_split"))
        lam_exp = sem("lam_exp")
        o_full, o_free, osq_done, oroot_done, tail_done = (sem(k) for k in ("o_full", "o_free", "osq_done", "oroot_done", "tail_done"))

        def hv_wait_full(eng, n):
            eng.wait_ge(hv_full[n % 2], n // 2 + 1)

        def hv_wait_free(eng, n):
            eng.wait_ge(hv_free[n % 2], n // 2 + 1)

        def bc(ap, k):
            return ap.unsqueeze(2).to_broadcast([ap.shape[0], ap.shape[1], k])

        def norm_wait(eng, n):
            if JOBS[n][1] in ("k", "mk"):
                eng.wait_ge(nrm_done, KJ.index(n) + 1)
            else:
                hv_wait_free(eng, n)

        def nrm_of(n):
            return (nrmM if JOBS[n][1] == "mq" else nrm)[NJ.index(n) % 2]

        def tanh_reader(n):
            return n if JOBS[n][0] == "cols" else n + 1

        def slot_count(i):
            return 16 * sum(2 if LOADS[x][0][0] == "pair" else 1 for x in range(i % 2, i + 1, 2))

        V_JOBS = [n for n in STAGE["X"] if JOBS[n][1] == "v"]
        K_JOBS = [n for n in STAGE["X"] if JOBS[n][1] == "k"]

        def is_split(n):
            j = JOBS[n]
            return (j[0] == "rows" and j[1] in ("q", "k") or (j[0] == "gate" and j[1] >= 1) or (j[0] == "up" and j[1] == 2 and j[2] >= 1)
                    or (j[0] == "out" and j[1] >= 2))

        def weights_number(br, f):
            return KD * (br - 1) + f

        def tile_pairs(r):
            t = slice(r * P, r * P + ROWS_TILE(r))
            return [(xs_hi[:, 2 * x:2 * x + 2, :] if r == PT else x_hi[x // 2][:, 2 * (x % 2):2 * (x % 2) + 2, :], h_lo[x][:, :, t],
                     hT[:, 2 * x:2 * x + 2, t]) for x in range(KD // 2)]

        def batch_columns(buf, j):
            return buf[:, j, NS_TOK - QB:WIN].rearrange("p (h t) -> p h t", h=H)[:, :, 0:QB]

        def batch_window(buf, j, h, b):
            x = NS_TOK - QB + NS_TOK * h - QB * b
            return buf[:, j, x:x + NS_TOK]

        def z_of(kind):
            return {"az": azT, "gz": gzT, "mz": mzT}[kind]

        def norm_dest(n):
            kind, r = JOBS[n][1], JOBS[n][2]
            dst = {"mk": mkT, "q": qT, "k": kT, "mq": mqT}[kind]
            rows = P if kind == "mk" else ROWS_TILE(r)
            return dst[:, :, r * P:r * P + rows], rows

        def rows_of(r, prompt, sample):
            if r < PT:
                return prompt[0, 0, r * P:(r + 1) * P].rearrange("t h d -> t (h d)")
            return sample[0].rearrange("b q h d -> (b q) (h d)")

        def tail_of(k):
            r = k % (PT + 1)
            n = ROWS_TILE(r)
            return n, (azT if k <= PT else gzT)[:, :, r * P:r * P + n]

        def o_view(ap, n):
            return ap[:, 0:H * n].rearrange("p (h t) -> p h t", h=H)

        ROWS_OUT = [16 * sum(1 for n in KJ if NJ.index(n) % 2 == i) for i in range(2)]
        ROWS_OUT_V = 16 * sum(1 for n in STAGE["X"] if JOBS[n][1] in ("v", "mv"))
        NU = H * PT
        block = ctx.enter_context(nc.Block())

        @block.gpsimd
        def _(pool):
            for n in STAGE["X"]:
                _, kind, r = JOBS[n]
                if kind in ("k", "mk"):
                    pool.wait_ge(nrm_done, KJ.index(n) + 1)
                    dst = (rows_of(r, ka_prompt, ka_sample) if kind == "k" else
                           mk_prompt[0, 0, r * P:(r + 1) * P].rearrange("t h d -> t (h d)"))
                    rows = P if kind == "mk" else ROWS_TILE(r)
                    pool.dma_start(dst, nrm_of(n)[0:rows, :]).then_inc(rows_out[NJ.index(n) % 2], 16)
                elif kind in ("v", "mv"):
                    hv_wait_free(pool, n)
                    if kind == "v":
                        dst, src = rows_of(r, va_prompt, va_sample), vA[0:ROWS_TILE(r), r, :]
                    else:
                        dst, src = mv_prompt[0, 0, r * P:(r + 1) * P].rearrange("t h d -> t (h d)"), mv[:, r, :]
                    pool.dma_start(dst, src).then_inc(out_done, 16)

            pool.wait_ge(tr_full, TRN["norm", STAGE["X"][-1]] + 1)
            for i in range(2):
                pool.wait_ge(rows_out[i], ROWS_OUT[i])
            pool.memset(qpadA, 0.0).then_inc(qpad_zero, 1)
            pool.wait_ge(qpad_zero, 1)
            pool.wait_ge(tr_free, TRN["norm", STAGE["X"][-2]] + 1)
            for c in range(2):
                for h in range(H):
                    x = 16 * h + 8 * c
                    if c or h:
                        pool.wait_ge(qpad_ready, H * c + h)
                    pool.tensor_copy(qpadA[64 * c:64 * c + 64, h, :, x:x + 8],
                                     qT[64 * c:64 * c + 64, h, NP_TOK:T].rearrange("p (b q) -> p b q", b=NB))\
                        .then_inc(qpad_ready, 1)
            pool.wait_ge(sc_read, 2 * NU)
            pool.wait_ge(tr_free, TRN["norm", STAGE["X"][-1]] + 1)
            pool.wait_ge(qpad_ready, 2 * H)
            for x in range(2):
                pool.tensor_copy(kTsA[x][:, :, PAST:NSK], kT[:, :, NP_TOK:T]).then_inc(new_keys, 1)
                pool.wait_ge(new_keys, x + 1)
            pool.wait_ge(pv_done, NU)
            pool.memset(aTs, 0.0).then_inc(ats_zero, 1)

            pool.wait_ge(st_ready, 2 * PT)
            pool.dma_start(gla_prompt[0, 0].rearrange("(k e) d v -> (e d) k v", e=2), St[(2 * PT) % 3])\
                .then_inc(st_out[(2 * PT) % 3], 16)
            for b in range(NB):
                pool.wait_ge(bst_ready, b + 1)
                pool.dma_start(gla_sample[0, b].rearrange("(k e) d v -> (e d) k v", e=2), St[(2 + b) % 3])\
                    .then_inc(st_out[(2 + b) % 3], 16)
            hv_wait_full(pool, STAGE["Q"][-1])
            pool.memset(qpadM, 0.0).then_inc(qm_zero, 1)
            pool.wait_ge(qm_zero, 1)
            pool.wait_ge(tr_free, TRN["norm", STAGE["Q"][-1]] + 1)
            for h in range(H):
                if h:
                    pool.wait_ge(qm_ready, h)
                pool.tensor_copy(qpadM[:, h, :, 8 * h:8 * h + 8],
                                 mqT[:, h, NP_TOK:T].rearrange("p (b q) -> p b q", b=NB)).then_inc(qm_ready, 1)
            pool.wait_ge(qm_ready, H)
            for s in ("PB", "PM"):
                for n in STAGE[s]:
                    kind, br, f, c = JOBS[n]
                    if kind == "up":
                        x = 3 * KD * (br - 1) + 3 * f + c
                        c0, cw = CH[c]
                        hv_wait_free(pool, n)
                        if x:
                            pool.wait_ge(madd_done, x)
                        pool.tensor_tensor(out=merged[:, f, c0:c0 + cw], in0=merged[:, f, c0:c0 + cw],
                                           in1=tmp[x % 2][:, 0:cw], op=ALU.add).then_inc(madd_done, 1)
            for r in range(PT + 1):
                rows = ROWS_TILE(r)
                for j in range(2):
                    hv_wait_free(pool, STAGE["O"][2 * r + j])
                dst = y_prompt[0, r * P:(r + 1) * P, :] if r < PT else y_sample.rearrange("b q d -> (b q) d")
                pool.dma_start(dst, y_row[r % 2][0:rows, :]).then_inc(y_out[r % 2], 16)

        @block.sync
        def _(sp):
            def load_x(t):
                src, n = TILES[t]
                if t >= 2:
                    sp.wait_ge(xn_done, t - 1)
                sp.dma_start(x_in[t % 2][0:n, :], src).then_inc(x_loaded[t % 2], 16)

            def load_slot(i):
                key, _ = LOADS[i]
                if i >= 2:
                    hv_wait_full(sp, LOADS[i - 2][1])
                slot, done = ring[i % 2], ring_in[i % 2]
                if key[0] == "pair":
                    _, br, f = key
                    c0 = C_GL + br * D + f * P
                    sp.dma_start(slot[:, 0:1024].rearrange("p (k n) -> p k n", k=KD),
                                 w_in[0, :, c0:c0 + P].rearrange("(k p) n -> p k n", p=P)).then_inc(done, 16)
                    sp.dma_start(slot[:, 1024:1536].rearrange("p (k n) -> p k n", k=KW),
                                 w_branch[0, br, :, f * P:(f + 1) * P].rearrange("(k p) n -> p k n", p=P))\
                        .then_inc(done, 16)
                else:
                    kind, f2 = key
                    c0 = {"az": C_AZ, "gq": C_GQ, "gk": C_GK, "gz": C_GZ, "gr": C_GR, "mz": C_MZ}[kind] + 256 * f2
                    wd = 16 if kind == "gr" else 256
                    sp.dma_start(slot[:, 0:KD * wd].rearrange("p (k n) -> p k n", k=KD),
                                 w_in[0, :, c0:c0 + wd].rearrange("(k p) n -> p k n", p=P)).then_inc(done, 16)

            def load_mem_w(x):
                sp.dma_start(w_mem[:, :, x * W:(x + 1) * W], w_mkv[0, :, x * W:(x + 1) * W]
                             .rearrange("(k p) n -> p k n", p=P)).then_inc(tm_w[6 * x], 16)

            load_x(0)
            sp.dma_start(ident[:, :], tab["ident"]).then_inc(first_in, 16)
            with nc.allow_non_contiguous_dma(reason="gains as columns, 4 K elements in all"):
                sp.dma_start(gmem[:, :], norm_mem[0].rearrange("(k p) -> p k", p=P)).then_inc(first_in, 16)
                sp.dma_start(gx[:, :], norm_x[0].rearrange("(k p) -> p k", p=P)).then_inc(first_in, 16)
            load_mem_w(0)
            load_x(1)
            load_mem_w(1)
            for k in SMALL[1:]:
                sp.dma_start(small[k][:, :], tab[k]).then_inc(consts_in, 16)
            with nc.allow_non_contiguous_dma(reason="gains as columns, 1 K elements in all"):
                sp.dma_start(ba_col[:, :], b_a[0].rearrange("(k p) -> p k", p=P)).then_inc(consts_in, 16)
                for hf in range(2):
                    sp.dma_start(gcol[64 * hf:64 * hf + 64, GQA:GQA + 1],
                                 g_qa.rearrange("a d -> d a")).then_inc(consts_in, 16)
                for i, src in ((GQM, g_qm), (GOA, g_oa), (GOB, g_ob)):
                    sp.dma_start(gcol[:, i:i + 1], src.rearrange("a d -> d a")).then_inc(consts_in, 16)
            sp.dma_start(gka_row[:, :], g_ka[0].partition_broadcast(P)).then_inc(consts_in, 16)
            sp.dma_start(gkm_row[:, :], g_km[0].partition_broadcast(P)).then_inc(consts_in, 16)
            sp.dma_start(nrm[0][:, 0:256], lam[0].rearrange("a d -> (a d)").partition_broadcast(P)).then_inc(consts_in, 16)
            for i, c in ((0, C_AQ), (2, C_AV), (1, C_AK)):
                sp.dma_start(w_av if i == 2 else wX[i], w_in[0, :, c:c + W].rearrange("(k p) n -> p k n", p=P))\
                    .then_inc(tm_w[1 + i], 16)
            for t in range(2, NT):
                load_x(t)
            hv_wait_full(sp, V_JOBS[-1])
            sp.dma_start(distance, tab["alibi"]).then_inc(alibi_in, 16)
            hv_wait_full(sp, STAGE["X"][-1])
            sp.wait_ge(x_whole, PT + 1)
            load_slot(0)
            load_slot(1)

            for i in range(2, 4):
                load_slot(i)
            sp.dma_start(pt_sb[:, :], page_table.rearrange("(a b) g -> a (b g)", a=1)).then_inc(pt_in, 16)
            sp.wait_ge(sc_read, 2 * NU)
            sp.dma_start(past_t, tab["past"]).then_inc(tabs_in, 16)
            sp.dma_start(new_t, tab["new"].rearrange("p (b t) -> p b t", b=NB)).then_inc(tabs_in, 16)
            sp.wait_ge(pt_in, 16)
            pages = {}

            def page_keys(b):
                pages[b] = [sp.value_load(pt_sb[0:1, NPG * b + g:NPG * b + g + 1], min_val=0,
                                          max_val=cache_k.shape[1] - 1) for g in range(NPG)]
                if b < 2:
                    sp.wait_ge(pv_done, NU - 1)
                else:
                    sp.wait_ge(ktr_full[1], b - 1)
                for g, pg in enumerate(pages[b]):
                    sp.dma_start(kpage[b % 2][:, g, :],
                                 cache_k[0, bass.ds(pg, 1), :, :, :].rearrange("a t h d -> (a t) (h d)"))\
                        .then_inc(k_in[b % 2], 16)

            def page_values(b):
                sp.wait_ge(pv_done, NU if b < 2 else NU + b - 1)
                for g, pg in enumerate(pages[b]):
                    sp.dma_start(vpage[b % 2][:, g, :],
                                 cache_v[0, bass.ds(pg, 1), :, :, :].rearrange("a t h d -> (a t) (h d)"))\
                        .then_inc(v_in[b % 2], 16)

            page_keys(0)
            page_keys(1)
            page_values(0)
            page_keys(2)
            for b in range(1, NB):
                page_values(b)
                if b + 2 < NB:
                    page_keys(b + 2)

            load_slot(4)
            load_slot(5)
            sp.wait_ge(pv_done, NU + NB)
            sp.dma_start(w_gv, w_in[0, :, C_GV:C_GV + W].rearrange("(k p) n -> p k n", p=P)).then_inc(tm_w[4], 16)
            sp.dma_start(wa2[0:16, :], w_a2[0]).then_inc(gw_in, 16)
            sp.dma_start(keep, tab["keep"]).then_inc(gw_in, 16)
            PA0 = LOAD_OF[("pair", 0, 0)]
            for i in range(6, PA0 + KD):
                load_slot(i)
            MZ0 = LOAD_OF[("mz", 0)]
            for b in range(NB):
                if b == 4:
                    load_slot(MZ0)
                x = (2 + b) % 3
                if b < 2:
                    sp.wait_ge(o_full, PT)
                else:
                    sp.wait_ge(st_out[x], 16 * (b // 3 + (x == 1)))
                sp.dma_start(St[x], state_gla[0, b].rearrange("(k e) d v -> (e d) k v", e=2))\
                    .then_inc(st_in[x], 16)
            load_slot(MZ0 + 1)
            for x in range(3):
                sp.wait_ge(st_out[x], 48)
            sp.dma_start(w_mq, w_in[0, :, C_MQ:C_MQ + W].rearrange("(k p) n -> p k n", p=P)).then_inc(tm_w[5], 16)
            load_slot(MZ0 + 2)
            load_slot(MZ0 + 3)
            PB0 = LOAD_OF[("pair", 1, 0)]
            for i in range(PB0 + 2, PB0 + 5):
                load_slot(i)
            sp.wait_ge(m_full, PT)
            sp.wait_ge(qm_ready, H)
            for b in range(NB):
                if b >= 2:
                    sp.wait_ge(mtr_full[1], b - 1)
                sp.dma_start(kpageM[b % 2], mem_k[0, b].rearrange("(g t) h d -> t g (h d)", g=2)).then_inc(km_in[b % 2], 16)
                if b >= 2:
                    sp.wait_ge(om_full, PT + b - 1)
                sp.dma_start(vpageM[b % 2], mem_v[0, b].rearrange("(g t) h d -> t g (h d)", g=2)).then_inc(vm_in[b % 2], 16)
                if b in (1, 2, 4, 6):
                    load_slot(PB0 + {1: 5, 2: 6, 4: 7, 6: 8}[b])
            load_slot(PB0 + 9)
            sp.wait_ge(om_full, PT + NB)
            for k0, nk, o in OUT_W:
                sp.dma_start(at(o, [nk, D]), w_o[0, k0 * P:(k0 + nk) * P].rearrange("(k p) n -> p k n", p=P))                    .then_inc(wo_in, 16)
            for i in range(PB0 + 10, len(LOADS)):
                load_slot(i)
            hv_wait_full(sp, STAGE["PM"][-1])
            for r in range(PT + 1):
                if r >= 2:
                    hv_wait_free(sp, STAGE["O"][2 * (r - 2) + 1])
                src = x_prompt[0, r * P:(r + 1) * P, :] if r < PT else xs
                sp.dma_start(x_res[r % 2][0:ROWS_TILE(r), :], src).then_inc(xr_in[r % 2], 16)
            sp.wait_ge(y_out[0], 16 * ((PT + 2) // 2))
            sp.wait_ge(y_out[1], 16 * ((PT + 1) // 2))
            for x in range(3):
                sp.wait_ge(st_out[x], 48)
            sp.wait_ge(out_done, ROWS_OUT_V)
            for i in range(2):
                sp.wait_ge(rows_out[i], ROWS_OUT[i])

        @block.tensor
        def _(pe):
            def tr_begin(*use):
                if TRN[use]:
                    pe.wait_ge(tr_free, TRN[use])

            def hv_begin(n):
                if n >= 2:
                    hv_wait_free(pe, n - 2)

            def split_product(out, terms):
                for x, (a_hi, a_lo, b_hi, b_lo) in enumerate(terms):
                    nc.tensor.matmul(out, a_hi, b_hi, start=(x == 0), stop=False)
                    nc.tensor.matmul(out, a_hi, b_lo, start=False, stop=False)
                    last = nc.tensor.matmul(out, a_lo, b_hi, start=False, stop=(x == len(terms) - 1))
                return last

            def heavy(n):
                job = JOBS[n]
                bank = HV[n % 2]
                hv_begin(n)
                if job[0] == "rows":
                    _, kind, r = job
                    i = {"mk": 0, "mv": 6, "q": 1, "k": 2, "v": 3, "gv": 4, "mq": 5}[kind]
                    pe.wait_ge(tm_w[i], 16)
                    rows = P if kind in ("mk", "mv") else ROWS_TILE(r)
                    if kind in ("mk", "mv"):
                        src, w = hT_mem, w_mem[:, :, W * (kind == "mv"):W * (kind == "mv") + W]
                    else:
                        src, w = hT, {1: None, 2: None, 3: w_av, 4: w_gv, 5: w_mq}[i]
                    if n in STAGE["X"]:
                        t = r + (0 if kind in ("mk", "mv") else NMT)
                        pe.wait_ge(xt_done, 2 * (t + 1))
                    if is_split(n):
                        pe.wait_ge(wx_split, i)
                        pe.wait_ge(x_split, r + 1)
                        last = split_product(bank[0:rows, :], [
                            (xs_hi[:, k, :] if r == PT else x_hi[k // 4][:, k % 4, :], h_lo[k // 2][:, k % 2, r * P:r * P + rows],
                             wx_hi[i - 1][k // 4][:, k % 4, :], wx_lo[i - 1][k // 4][:, k % 4, :])
                            for k in range(KD)])
                        last.then_inc(hv_full[n % 2], 1)
                        return
                    for k in range(KD):
                        last = nc.tensor.matmul(bank[0:rows, :], src[:, k, r * P:r * P + rows],
                                                w[:, k, :], start=(k == 0), stop=(k == KD - 1))
                elif job[0] == "out":
                    _, r, j = job
                    rows = ROWS_TILE(r)
                    pe.wait_ge(wo_in, 16 * len(OUT_W))
                    pe.wait_ge(madd_done, 2 * 3 * KD)
                    if is_split(n):
                        pe.wait_ge(wo_split, KD)
                        pe.wait_ge(mt_split, r - 1)
                        o = slice(j * W, (j + 1) * W)
                        last = split_product(bank[0:rows, :], [(m_hi[r % 2][:, k, 0:rows], m_lo[r % 2][:, k, 0:rows],
                                                                wo_hi[k // 2][:, k % 2, o], wo_lo[k // 2][:, k % 2, o]) for k in range(KD)])
                    else:
                        for k in range(KD):
                            last = nc.tensor.matmul(bank[0:rows, :], merged[:, k, r * P:r * P + rows],
                                                    w_out[k][:, j * W:(j + 1) * W], start=(k == 0), stop=(k == KD - 1))
                else:
                    _, kind, f, c = job
                    c0, cw = CH[c]
                    if job[0] == "cols":
                        i = LOAD_OF[(kind, f // 2)]
                        m = 16 if kind == "gr" else P
                        w = ring[i % 2][:, 0:KD * (16 if kind == "gr" else 256)].rearrange("p (k n) -> p k n", k=KD)
                        w = w[:, :, (f % 2) * P:(f % 2) * P + m]
                        src, kb, loads = hT, KD, 1 + i // 2
                    else:
                        i = LOAD_OF[("pair", kind, f)]
                        m = P
                        if job[0] == "gate":
                            w, src, kb = ring[i % 2][:, 0:1024].rearrange("p (k n) -> p k n", k=KD), hT, KD
                        else:
                            w = ring[i % 2][:, 1024:1536].rearrange("p (k n) -> p k n", k=KW)
                            src, kb = (azT, gzT, mzT)[kind], KW
                    pe.wait_ge(ring_in[i % 2], slot_count(i))
                    if is_split(n):
                        t, gate = slice(c0, c0 + cw), job[0] == "gate"
                        pe.wait_ge(w_split, weights_number(kind, f) + 1)
                        if gate:
                            pe.wait_ge(h_split, (c0 + cw + P - 1) // P)
                        else:
                            pe.wait_ge(mz_split, c + 1)
                        last = split_product(bank[:, 0:cw], [
                            (wg_hi[f % 2][k // 4][:, k % 4, :] if gate else wu_hi[i % 2][:, k, :],
                             (wg_lo if gate else wu_lo)[i % 2][:, k, :],
                             (h_hi if gate else mz_hi)[k // 2][:, k % 2, t],
                             (h_lo if gate else mz_lo)[k // 2][:, k % 2, t]) for k in range(kb)])
                        last.then_inc(hv_full[n % 2], 1)
                        return
                    if job[0] == "up" and f == 0 and c == 0:
                        pe.wait_ge(*((tail_done, PT + 1), (tail_done, 2 * (PT + 1)), (mt_done, PT + 1))[kind])
                    for k in range(kb):
                        last = nc.tensor.matmul(bank[0:m, 0:cw], w[:, k, :], src[:, k, c0:c0 + cw],
                                                start=(k == 0), stop=(k == kb - 1))
                last.then_inc(hv_full[n % 2], 1)

            def x_transposes(t):
                rows = TILES[t][1]
                pe.wait_ge(xn_done, t + 1)
                for j in range(2):
                    if t >= 1:
                        pe.wait_ge(xt_done, 2 * (t - 1) + j + 1)
                    for k in range(4):
                        last = nc.tensor.transpose(sc_all[:, j, k * P:k * P + rows],
                                                   xn[0:rows, (4 * j + k) * P:(4 * j + k + 1) * P],
                                                   ident[0:rows, 0:rows])
                    last.then_inc(xt_full, 1)

            def norm_transposes(n):
                _, rows = norm_dest(n)
                norm_wait(pe, n)
                tr_begin("norm", n)
                for h in range(H):
                    last = nc.tensor.transpose(TR[:, h * P:h * P + rows], nrm_of(n)[0:rows, h * P:(h + 1) * P],
                                               ident[0:rows, 0:rows])
                last.then_inc(tr_full, 1)

            pe.wait_ge(first_in, 48)
            x_transposes(0)
            for n in STAGE["X"]:
                kind, r = JOBS[n][1], JOBS[n][2]
                heavy(n)
                if kind in ("mk", "v") and (t := r + (0 if kind == "mk" else NMT)) + 1 < NT:
                    x_transposes(t + 1)
                if n - 1 in NJ:
                    norm_transposes(n - 1)

            def scores(u):
                i, h = u // H, u % H
                nk = (i + 1) * P
                for c in range(2):
                    if u:
                        pe.wait_ge(sc_read, 2 * (u - 1) + c + 1)
                    for j in range(0, nk, W):
                        w = min(W, nk - j)
                        last = nc.tensor.matmul(sc_all[:, 2 * c + j // W, 0:w],
                                                qT[64 * c:64 * c + 64, h, i * P:(i + 1) * P],
                                                kT[64 * c:64 * c + 64, h, j:j + w], start=True, stop=True)
                    last.then_inc(sc_full, 1)

            def weights_transposed(u, g):
                b0, b1 = groups_A(u)[g]
                tr_begin("a", u, b0)
                for b in range(b0, b1):
                    last = nc.tensor.transpose(TR[:, (b - b0) * P:(b - b0 + 1) * P],
                                               S[u % 2][:, 0, b * P:(b + 1) * P], ident[:, :])
                last.then_inc(tr_full, 1)

            def values(u):
                i, h = u // H, u % H
                if h == 0 and i:
                    pe.wait_ge(o_free, i)
                for b in range(i + 1):
                    if b % 4 == 0:
                        pe.wait_ge(tr_free, TRN["a", u, b] + 1)
                    last = nc.tensor.matmul(OB[:, h * P:(h + 1) * P], vA[:, b, h * P:(h + 1) * P],
                                            aT[u % 2][:, b * P:(b + 1) * P], start=(b == 0), stop=(b == i))
                last.then_inc(pv_done, 1)

            def page_transposes(b, kp, kin, n_in):
                pe.wait_ge(kin[b % 2], n_in * (b // 2 + 1))
                for g in range(2):
                    if b:
                        pe.wait_ge(kts_copied[g], b)
                    for h in range(H):
                        last = nc.tensor.transpose(sc_all[:, g, h * P:(h + 1) * P],
                                                   kp[b % 2][:, g, h * P:(h + 1) * P], ident[:, :])
                    last.then_inc(ktr_full[g], 1)

            def sample_scores(b):
                if b == 0:
                    pe.wait_ge(qpad_ready, 2 * H)
                    pe.wait_ge(new_keys, 2)
                else:
                    pe.wait_ge(ss_read, b)
                for g in range(2):
                    pe.wait_ge(kts_copied[g], b + 1)
                for h in range(H):
                    last = nc.tensor.matmul(sc_all[0:64, 2, 0:NSK], qpadA[:, h, b, :], kTsA[b % 2][:, h, :],
                                            start=(h == 0), stop=(h == H - 1))
                last.then_inc(ss_full, 1)

            def sample_weights(b):
                pe.wait_ge(a_ready, NU + b + 1)
                tr_begin("s", b)
                for j in range(3):
                    m = min(P, NSK - j * P)
                    last = nc.tensor.matmul(TR[0:m, 32 * j:32 * j + 32], Ps[b % 2][0:64, j * P:j * P + m],
                                            comb_t[0:64, :], start=True, stop=True)
                last.then_inc(tr_full, 1)

            def sample_values(b):
                if b == 0:
                    pe.wait_ge(o_free, PT)
                pe.wait_ge(tr_free, TRN["s", b] + 1)
                pe.wait_ge(v_in[b % 2], 32 * (b // 2 + 1))
                for h in range(H):
                    for j in range(3):
                        m = min(P, NSK - j * P)
                        v = vpage[b % 2][:, j, h * P:(h + 1) * P] if j < 2 else vA[0:m, PT, h * P:(h + 1) * P]
                        last = nc.tensor.matmul(OB[0:NS_TOK, h * P:(h + 1) * P], batch_window(aTs, j, h, b)[0:m],
                                                v, start=(b + h + j == 0), stop=(b == NB - 1 and h == H - 1 and j == 2))
                last.then_inc(pv_done, 1)

            def sample_rows_transposed(i):
                pe.wait_ge(otok_ready, i + 1)
                for h in range(H):
                    last = nc.tensor.transpose(OB[:, h * NS_TOK:(h + 1) * NS_TOK],
                                               (otok, otokM)[i][0:NS_TOK, h * P:(h + 1) * P],
                                               ident[0:NS_TOK, 0:NS_TOK])
                last.then_inc(os_full, 1)

            def tail_mean(k):
                n, _ = tail_of(k)
                pe.wait_ge(osq_done, k + 1)
                tr_begin("mean", k)
                nc.tensor.matmul(TR[:, 0:H * n], meanm[:, :], sq[:, 0:H * n], start=True, stop=True)\
                    .then_inc(tr_full, 1)

            pe.wait_ge(tr_free, TRN["norm", K_JOBS[-2]] + 1)
            hv_wait_free(pe, V_JOBS[-1])
            for u in range(STEPS_A + 1):
                jobs = heavy_A(u) if u < STEPS_A else []
                if u < NU:
                    scores(u)
                    if u == 0:
                        norm_transposes(STAGE["X"][-1])
                        pe.wait_ge(x_whole, PT + 1)
                elif u == NU:
                    values(u - 2)
                    pe.wait_ge(sc_read, 2 * NU)
                    page_transposes(0, kpage, k_in, 32)
                elif NU < u < STEPS_A:
                    sample_scores(u - NU)
                    if u - NU + 1 < NB:
                        page_transposes(u - NU + 1, kpage, k_in, 32)
                if 1 <= u <= NU:
                    for n in jobs:
                        heavy(n)
                    pe.wait_ge(a_ready, u)
                    weights_transposed(u - 1, 0)
                    if 2 <= u < NU:
                        values(u - 2)
                    if len(groups_A(u - 1)) > 1:
                        weights_transposed(u - 1, 1)
                    if u == NU:
                        values(u - 1)
                else:
                    for n in jobs:
                        heavy(n)
                if u > NU:
                    sample_weights(u - 1 - NU)
                    sample_values(u - 1 - NU)
                if u == NU:
                    sample_scores(0)
                    page_transposes(1, kpage, k_in, 32)
                if u in MEAN_AT:
                    tail_mean(MEAN_AT[u])

            heavy(STAGE["R"][0])
            sample_rows_transposed(0)
            heavy(STAGE["R"][1])
            tail_mean(PT)
            heavy(STAGE["R"][2])
            heavy(STAGE["V"][0])
            pe.wait_ge(gw_in, 32)
            for c, (c0, cw) in enumerate(CH):
                hv_wait_free(pe, STAGE["R"][c])
                for k in range(2):
                    x = 2 * c + k
                    if x >= 4:
                        pe.wait_ge(lg_read, x - 3)
                    nc.tensor.matmul(sc_all[:, x % 4, 0:cw], wa2[0:16, k * P:(k + 1) * P], gr[0:16, c0:c0 + cw],
                                     start=True, stop=True).then_inc(lg_full, 1)
            for n in list(STAGE["V"])[1:] + list(STAGE["Z"]):
                heavy(n)

            def decayed_transposed(r):
                n = ROWS_TILE(r)
                pe.wait_ge(kd_ready, r + 1)
                tr_begin("kd", r)
                for k in range(2):
                    last = nc.tensor.transpose(TR[0:n, k * P:(k + 1) * P], kd[:, k, 0:n], ident[:, :])
                last.then_inc(tr_full, 1)

            def level(r, lc):
                n, x = ROWS_TILE(r), lc % 2
                pe.wait_ge(lv_ready, lc + 1)
                if lc >= 2:
                    pe.wait_ge(masked, lc - 1)
                for k in range(2):
                    last = nc.tensor.matmul(sc_all[0:n, x, 2 * n * k:2 * n * (k + 1)], kz[x][:, k, 0:n],
                                            qz[x][:, :, k, 0:n], start=True, stop=True)
                last.then_inc(at_full, 1)

            def updates(r, j, count, done, full):
                n = ROWS_TILE(r)
                pe.wait_ge(kdz_ready, count + 1)
                for k in range(2):
                    last = nc.tensor.matmul(sc_all[:, 2 + j, 256 * k:256 * (k + 1)], kdz[j][0:n, k, :],
                                            gv[0:n, r, 256 * k:256 * (k + 1)], start=True, stop=True)
                last.then_inc(full, 1)

            hv_wait_free(pe, STAGE["V"][-1])
            for r in range(PT):
                jobs = STAGE["PA"][5 * r:5 * r + 5]
                heavy(jobs[0])
                decayed_transposed(r)
                heavy(jobs[1])
                if r:
                    tail_mean(PT + r)
                level(r, 3 * r)
                heavy(jobs[2])
                level(r, 3 * r + 1)
                if r:
                    pe.wait_ge(st_ready, 2 * r)
                for j in range(2):
                    updates(r, j, 2 * r + j, None, u_full)
                heavy(jobs[3])
                level(r, 3 * r + 2)
                heavy(jobs[4])
                pe.wait_ge(att_ready, r + 1)
                pe.wait_ge(o_free, PT + 1 + r)
                pe.wait_ge(st_ready, 2 * r + 1)
                pe.wait_ge(st_zero, 2)
                for h in range(H):
                    nc.tensor.matmul(OB[:, h * P:(h + 1) * P], gv[:, r, h * P:(h + 1) * P], att[:, h, :],
                                     start=True, stop=False)
                    for j in range(2):
                        last = nc.tensor.matmul(OB[:, h * P:(h + 1) * P], St[(2 * r + j) % 3][:, h // 2, :],
                                                qe[:, j, h % 2, h // 2, :], start=False, stop=(j == 1))
                last.then_inc(o_full, 1)
            r = PT
            jobs = STAGE["PA"][5 * PT:]
            heavy(jobs[0])
            decayed_transposed(r)
            tail_mean(2 * PT)
            level(r, 3 * PT)
            pe.wait_ge(st_ready, 2 * PT)
            pe.wait_ge(masked, 3 * PT + 1)
            pe.wait_ge(o_free, PT + 1 + r)
            for h in range(H):
                nc.tensor.matmul(OB[:, h * NS_TOK:(h + 1) * NS_TOK], gv[0:NS_TOK, r, h * P:(h + 1) * P],
                                 att[0:NS_TOK, h, 0:NS_TOK], start=(h == 0), stop=False)
            for b in range(NB):
                if b:
                    heavy(jobs[b])
                pe.wait_ge(st_in[(2 + b) % 3], 16 * (b // 3 + 1))
                for h in range(H):
                    o = OB[:, h * NS_TOK + QB * b:h * NS_TOK + QB * (b + 1)]
                    last = nc.tensor.matmul(o, St[(2 + b) % 3][:, h // 2, :],
                                            qe[:, 0, h % 2, h // 2, QB * b:QB * (b + 1)], start=False,
                                            stop=(b == NB - 1 and h == H - 1))
                last.then_inc(vb_done, 1)
                if b >= 2:
                    pe.wait_ge(bst_ready, b - 1)
                updates(r, b % 2, 2 * PT + b, None, bu_full)

            def norm_jobs_Q():
                for n in STAGE["Q"]:
                    heavy(n)
                    if n - 1 in NJ:
                        norm_transposes(n - 1)

            heavy(STAGE["MZ"][0])
            tail_mean(2 * PT + 1)
            for n in list(STAGE["MZ"])[1:]:
                heavy(n)
            norm_jobs_Q()

            def m_scores(i):
                b0 = 2 * (i % 2)
                if i >= 2:
                    pe.wait_ge(m_exp, i - 1)
                for h in range(H):
                    last = nc.tensor.matmul(sc_all[:, b0 + h // 2, NMEM * (h % 2):NMEM * (h % 2 + 1)],
                                            mqT[:, h, i * P:(i + 1) * P], mkT[:, h, :], start=True, stop=True)
                last.then_inc(m_full, 1)

            def m_transposed(i, g):
                tr_begin("m", i, g)
                for x in range(4):
                    h, kb = 2 * g + x // 2, x % 2
                    last = nc.tensor.transpose(TR[:, x * P:(x + 1) * P], Pm[:, h, kb * P:(kb + 1) * P], ident[:, :])
                last.then_inc(tr_full, 1)

            def m_values(i):
                if i:
                    pe.wait_ge(mt_done, i)
                else:
                    pe.wait_ge(o_free, 2 * PT + 2)
                for h in range(H):
                    pe.wait_ge(tr_free, TRN["m", i, h // 2] + 1)
                    for kb in range(2):
                        last = nc.tensor.matmul(OB[:, h * P:(h + 1) * P], mv[:, kb, h * P:(h + 1) * P],
                                                PmT[:, 2 * h + kb, :], start=(kb == 0), stop=(kb == 1))
                last.then_inc(om_full, 1)

            def m_pages(b):
                pe.wait_ge(km_in[b % 2], 16 * (b // 2 + 1))
                for g in range(2):
                    if b:
                        pe.wait_ge(mts_copied[g], b)
                    for h in range(H):
                        last = nc.tensor.transpose(sc_all[:, g, h * P:(h + 1) * P],
                                                   kpageM[b % 2][:, g, h * P:(h + 1) * P], ident[:, :])
                    last.then_inc(mtr_full[g], 1)

            def m_sample_scores(b):
                if b == 0:
                    pe.wait_ge(qm_ready, H)
                else:
                    pe.wait_ge(m_exp, PT + b)
                for g in range(2):
                    pe.wait_ge(mts_copied[g], b + 1)
                for h in range(H):
                    last = nc.tensor.matmul(sc_all[0:32, 2, 0:NMEM], qpadM[:, h, b, :], kTsM[:, h, :],
                                            start=(h == 0), stop=(h == H - 1))
                last.then_inc(ms_full, 1)

            def m_sample_values(b):
                if b == 0:
                    pe.wait_ge(mt_done, PT)
                pe.wait_ge(tr_free, TRN["ms", b] + 1)
                pe.wait_ge(vm_in[b % 2], 16 * (b // 2 + 1))
                for h in range(H):
                    for kb in range(2):
                        last = nc.tensor.matmul(OB[0:NS_TOK, h * P:(h + 1) * P], batch_window(aTsM, kb, h, b),
                                                vpageM[b % 2][:, kb, h * P:(h + 1) * P],
                                                start=(b + h + kb == 0), stop=(b == NB - 1 and h == H - 1 and kb == 1))
                last.then_inc(om_full, 1)

            norm_transposes(STAGE["Q"][-1])
            pe.wait_ge(tr_free, TRN["norm", STAGE["Q"][-1]] + 1)
            m_scores(0)
            for i in range(PT):
                jobs = STAGE["PB"][3 * i:3 * i + 3]
                heavy(jobs[0])
                if i + 1 < PT:
                    m_scores(i + 1)
                pe.wait_ge(m_ready, i + 1)
                m_transposed(i, 0)
                heavy(jobs[1])
                m_transposed(i, 1)
                heavy(jobs[2])
                m_values(i)
            pe.wait_ge(m_exp, PT)
            for b in range(NB):
                jobs = STAGE["PB"][3 * (PT + b):3 * (PT + b) + 3]
                m_pages(b)
                heavy(jobs[0])
                m_sample_scores(b)
                heavy(jobs[1])
                pe.wait_ge(m_ready, PT + b + 1)
                tr_begin("ms", b)
                for kb in range(2):
                    last = nc.tensor.transpose(TR[:, 32 * kb:32 * kb + 32], PsM[0:32, kb * P:(kb + 1) * P],
                                               ident[0:32, 0:32])
                last.then_inc(tr_full, 1)
                heavy(jobs[2])
                m_sample_values(b)
            heavy(STAGE["PM"][0])
            sample_rows_transposed(1)
            for n in [*list(STAGE["PM"])[1:], *STAGE["O"]]:
                heavy(n)

        @block.scalar
        def _(act):
            steps = [0]

            def settle(ins):
                steps[0] += 1
                ins.then_inc(act_step, 1)
                act.wait_ge(act_step, steps[0])

            def tr_wait(*use):
                act.wait_ge(tr_full, TRN[use] + 1)

            def heavy(n):
                job = JOBS[n]
                bank = HV[n % 2]
                if job[0] == "rows":
                    _, kind, r = job
                    rows = P if kind in ("mk", "mv") else ROWS_TILE(r)
                    hv_wait_full(act, n)
                    if kind in NORMED:
                        m, g = NJ.index(n), W // NORMED[kind]
                        if m:
                            act.wait_ge(gsum_done, m)
                        nc.scalar.activation(sq[0:rows, :], bank[0:rows, :], ACT.Square).then_inc(sq_done, 1)
                        act.wait_ge(gsum_done, m + 1)
                        nc.scalar.activation(gstat[0:rows, 1, 0:g], gstat[0:rows, 0, 0:g], ACT.Sqrt,
                                             bias=eps[0:rows, :], scale=float(g) / W).then_inc(groot_done, 1)
                    else:
                        dst = {"v": vA, "mv": mv, "gv": gv}[kind][0:rows, r, :]
                        nc.scalar.copy(dst, bank[0:rows, :]).then_inc(hv_free[n % 2], 1)
                elif job[0] == "out":
                    return
                else:
                    _, kind, f, c = job
                    c0, cw = CH[c]
                    if job[0] == "up":
                        return
                    hv_wait_full(act, n)
                    if n in ZJ:
                        m = ZJ.index(n)
                        if m >= 2:
                            hv_wait_free(act, tanh_reader(ZJ[m - 2]))
                        out = nc.scalar.activation(tanh[m % 2][:, 0:cw], bank[:, 0:cw], ACT.Tanh, scale=0.5)
                        out.then_inc(hv_free[n % 2] if job[0] == "gate" else tanh_done, 1)
                    elif kind == "gr":
                        nc.scalar.copy(gr[0:16, c0:c0 + cw], bank[0:16, 0:cw]).then_inc(hv_free[n % 2], 1)
                    else:
                        dst, s = (gqT, 0.125) if kind == "gq" else (gkT, 1.0)
                        nc.scalar.mul(dst[:, f, c0:c0 + cw], bank[:, 0:cw], s).then_inc(hv_free[n % 2], 1)

            def row_stat(t):
                n = TILES[t][1]
                act.wait_ge(x_loaded[t % 2], 16 * (t // 2 + 1))
                if t >= 1:
                    act.wait_ge(xn_done, t)
                settle(nc.scalar.activation(junk[0:n, :], x_in[t % 2][0:n, :], ACT.Square,
                                            accum_out=rstat[0:n, 0:1]))
                nc.scalar.activation(rstat[0:n, 1:2], rstat[0:n, 0:1], ACT.Sqrt, bias=eps[0:n, :],
                                     scale=1.0 / D).then_inc(root_done, 1)

            def norm_evict(n):
                dst, rows = norm_dest(n)
                tr_wait("norm", n)
                src = TR[:, :].rearrange("p (h t) -> p h t", h=H)[:, :, 0:rows]
                g = {"q": GQA, "mq": GQM}.get(JOBS[n][1])
                if g is None:
                    nc.scalar.copy(dst, src).then_inc(tr_free, 1)
                else:
                    nc.scalar.activation(dst, src, ACT.Copy, scale=gcol[:, g:g + 1]).then_inc(tr_free, 1)

            def high_projection(i):
                act.wait_ge(tm_w[1 + i], 16)
                for x in range(2):
                    last = nc.scalar.copy(wx_hi[i][x], wX[i][:, 4 * x:4 * x + 4, :])
                last.then_inc(wx_high, 1)

            def high_tile(r):
                n = ROWS_TILE(r)
                act.wait_ge(xt_done, 2 * (r + NMT + 1))
                if r == PT:
                    hv_wait_full(act, V_JOBS[-1])
                    nc.scalar.copy(xs_hi, hT[:, :, r * P:r * P + n]).then_inc(x_high, 1)
                    return
                if r:
                    act.wait_ge(x_whole, r)
                for x in range(2):
                    last = nc.scalar.copy(x_hi[x], hT[:, 4 * x:4 * x + 4, r * P:r * P + n])
                last.then_inc(x_high, 1)

            act.wait_ge(eps_ready, 1)
            row_stat(0)
            for n in STAGE["X"]:
                kind, r = JOBS[n][1], JOBS[n][2]
                if kind in ("mk", "v") and (t := r + (0 if kind == "mk" else NMT)) + 1 < NT:
                    row_stat(t + 1)
                if n == NJ[0]:
                    act.wait_ge(consts_ready, 1)
                heavy(n)
                if n - 1 in NJ:
                    norm_evict(n - 1)
                if kind == "mv":
                    high_projection(r)
                if n == V_JOBS[0]:
                    high_tile(0)
                if n == V_JOBS[-1] or kind == "k" and r + 1 < PT:
                    high_tile(PT if n == V_JOBS[-1] else r + 1)
            norm_evict(STAGE["X"][-1])

            def tail_square(k):
                n, _ = tail_of(k)
                act.wait_ge(o_free, k + 1)
                if k:
                    act.wait_ge(tr_full, TRN["mean", k - 1] + 1)
                nc.scalar.activation(sq[:, 0:H * n], og[:, 0:H * n], ACT.Square).then_inc(osq_done, 1)

            def tail_root(k):
                n, _ = tail_of(k)
                tr_wait("mean", k)
                if k:
                    act.wait_ge(tail_done, k)
                nc.scalar.activation(rs_t[:, 0:H * n], TR[:, 0:H * n], ACT.Sqrt, bias=eps[:, :]).then_inc(tr_free, 1)

            def exps(u):
                nk = (u // H + 1) * P
                act.wait_ge(nmx_ready, u + 1)
                for c in range(2):
                    last = nc.scalar.activation(S[u % 2][:, c, 0:nk], S[u % 2][:, c, 0:nk], ACT.Exp,
                                                bias=nmx[:, c:c + 1], accum_out=psum_r[:, c:c + 1])
                last.then_inc(p_ready, 1)

            def weights_evict(u, g):
                b0, b1 = groups_A(u)[g]
                tr_wait("a", u, b0)
                if u >= 2:
                    act.wait_ge(pv_done, u - 1)
                nc.scalar.copy(aT[u % 2][:, b0 * P:b1 * P], TR[:, 0:(b1 - b0) * P]).then_inc(tr_free, 1)

            def page_evict(b, dst, g):
                act.wait_ge(ktr_full[g], b + 1)
                nc.scalar.copy(dst[:, :, g * P:(g + 1) * P], sc_all[:, g, :].rearrange("p (h t) -> p h t", h=H))\
                    .then_inc(kts_copied[g], 1)

            def sample_exp(b):
                act.wait_ge(nmx_ready, NU + b + 1)
                nc.scalar.activation(Ps[b % 2][0:64, :], Ps[b % 2][0:64, :], ACT.Exp, bias=nmx[0:64, 0:1],
                                     accum_out=psum_r[0:64, 0:1]).then_inc(p_ready, 1)

            def sample_evict(b):
                tr_wait("s", b)
                if b:
                    act.wait_ge(pv_done, NU + b)
                else:
                    act.wait_ge(ats_zero, 1)
                for j, m in ((0, P), (1, P), (2, NS_TOK)):
                    last = nc.scalar.copy(batch_columns(aTs, j)[0:m],
                                          TR[0:m, 32 * j:32 * j + 32].rearrange("p (h q) -> p h q", h=H))
                last.then_inc(tr_free, 1)

            nc.scalar.activation(lam_sum[:, 2:4], lam_sum[:, 0:2], ACT.Exp).then_inc(lam_exp, 1)
            for u in range(STEPS_A + 1):
                jobs = heavy_A(u) if u < STEPS_A else []
                if 1 <= u <= NU:
                    if u == NU:
                        act.wait_ge(sc_read, 2 * NU)
                        page_evict(0, kTsA[0], 1)
                    for n in jobs:
                        heavy(n)
                    for g in range(len(groups_A(u - 1))):
                        weights_evict(u - 1, g)
                if u < NU:
                    exps(u)
                elif NU < u < STEPS_A:
                    if u - NU + 1 < NB:
                        if u - NU + 1 >= 2:
                            act.wait_ge(ss_full, u - NU)
                        page_evict(u - NU + 1, kTsA[(u - NU + 1) % 2], 1)
                    sample_exp(u - NU)
                if u == 0 or u > NU:
                    for n in jobs:
                        heavy(n)
                if u > NU:
                    sample_evict(u - 1 - NU)
                if u == NU:
                    page_evict(1, kTsA[1], 1)
                    sample_exp(0)
                if u in COPY_AT:
                    tail_square(COPY_AT[u])
                if u in MEAN_AT:
                    tail_root(MEAN_AT[u])

            act.wait_ge(out_done, ROWS_OUT_V)
            act.wait_ge(pv_done, NU + NB)
            heavy(STAGE["R"][0])
            tail_square(PT)
            heavy(STAGE["R"][1])
            tail_root(PT)
            for n in [*list(STAGE["R"])[2:], *list(STAGE["V"])[:2]]:
                heavy(n)
            act.wait_ge(lg_read, 6)
            settle(nc.scalar.activation(lsig, lsig, ACT.Abs))
            settle(nc.scalar.activation(lsig, lsig, ACT.Exp, scale=-1.0))
            nc.scalar.activation(lsig, lsig, ACT.Ln, bias=1.0).then_inc(lsig_done, 1)
            for n in [*list(STAGE["V"])[2:], *STAGE["Z"]]:
                heavy(n)

            def decays(r):
                n, L = ROWS_TILE(r), (GC if r < PT else QB)
                b = bb[:, :, r * P:r * P + n]
                act.wait_ge(gd_in, r + 1)
                if r:
                    act.wait_ge(st_ready, 2 * r)
                nc.scalar.activation(edel[:, :, 0:n], edel[:, :, 0:n], ACT.Exp, scale=1.0 / 16)
                nc.scalar.activation(dlt[:, :, 0:n], b, ACT.Exp, scale=1.0 / 16)
                nc.scalar.activation(dec[:, :, 0:n // L], b.rearrange("p k (c l) -> p k c l", l=L)[:, :, :, L - 1],
                                     ACT.Exp, scale=1.0 / 16).then_inc(gd_exp, 1)

            def decayed_evict(r):
                n = ROWS_TILE(r)
                tr_wait("kd", r)
                if r:
                    act.wait_ge(kdz_ready, 2 * r)
                nc.scalar.copy(kdt[0:n, :], TR[0:n, 0:256]).then_inc(tr_free, 1)

            def level_exps(r, lc):
                n = ROWS_TILE(r)
                act.wait_ge(lv_in, lc + 1)
                nc.scalar.activation(dk[:, :, 0:n], dk[:, :, 0:n], ACT.Exp, scale=-1.0 / 16)
                nc.scalar.activation(dq[:, :, 0:n], dq[:, :, 0:n], ACT.Exp, scale=1.0 / 16).then_inc(lv_exp, 1)

            level_exps(0, 0)
            decays(0)
            for r in range(PT):
                jobs = STAGE["PA"][5 * r:5 * r + 5]
                heavy(jobs[0])
                decayed_evict(r)
                heavy(jobs[1])
                if r:
                    tail_root(PT + r)
                level_exps(r, 3 * r + 1)
                heavy(jobs[2])
                level_exps(r, 3 * r + 2)
                heavy(jobs[3])
                level_exps(r + 1, 3 * r + 3)
                decays(r + 1)
                heavy(jobs[4])
                tail_square(PT + 1 + r)
            jobs = STAGE["PA"][5 * PT:]
            heavy(jobs[0])
            decayed_evict(PT)
            tail_root(2 * PT)
            for n in jobs[1:]:
                heavy(n)
            tail_square(2 * PT + 1)

            heavy(STAGE["MZ"][0])
            tail_root(2 * PT + 1)
            for k, n in enumerate(list(STAGE["MZ"])[1:]):
                heavy(n)
                if k < KD:
                    if k == KD // 2:
                        for x in range(3):
                            act.wait_ge(st_out[x], 48)
                    nc.scalar.copy(h_hi[k // 2][:, k % 2, :], hT[:, k, :]).then_inc(h_high, 1)

            def high_weights(br, f):
                i = LOAD_OF[("pair", br, f)]
                slot = ring[i % 2]
                act.wait_ge(ring_in[i % 2], slot_count(i))
                if (br, f) == (1, 1):
                    hv_wait_full(act, STAGE["Q"][-1])
                for x in range(2):
                    last = nc.scalar.copy(wg_hi[f % 2][x], slot[:, 512 * x:512 * (x + 1)]
                                          .rearrange("p (k n) -> p k n", k=KD // 2))
                if br == 2 and f:
                    last = nc.scalar.copy(wu_hi[i % 2], slot[:, 1024:1536].rearrange("p (k n) -> p k n", k=KW))
                last.then_inc(wh_high, 1)

            def branch(n):
                heavy(n)
                kind, br, f, c = JOBS[n]
                if kind == "up" and c == 0 and (br, f) != (2, KD - 1):
                    high_weights(*((br, f + 1) if f + 1 < KD else (2, 0)))

            for n in STAGE["Q"]:
                heavy(n)
                if n - 1 in NJ:
                    norm_evict(n - 1)
                if n == STAGE["Q"][2]:
                    high_weights(1, 0)
            norm_evict(STAGE["Q"][-1])

            def m_exps(i):
                act.wait_ge(m_max, i + 1)
                if i:
                    act.wait_ge(tr_full, TRN["m", i - 1, 1] + 1)
                b0 = 2 * (i % 2)
                for h in range(H):
                    last = nc.scalar.activation(Pm[:, h, :], sc_all[:, b0 + h // 2, NMEM * (h % 2):NMEM * (h % 2 + 1)],
                                                ACT.Exp, bias=nmx[:, h:h + 1], accum_out=psum_r[:, h:h + 1])
                last.then_inc(m_exp, 1)

            def m_evict(i, g):
                tr_wait("m", i, g)
                if i:
                    act.wait_ge(om_full, i)
                nc.scalar.copy(PmT[:, 4 * g:4 * g + 4, :], TR[:, :].rearrange("p (x t) -> p x t", x=4)).then_inc(tr_free, 1)

            m_exps(0)
            for i in range(PT):
                jobs = STAGE["PB"][3 * i:3 * i + 3]
                branch(jobs[0])
                m_evict(i, 0)
                branch(jobs[1])
                m_evict(i, 1)
                if i + 1 < PT:
                    m_exps(i + 1)
                branch(jobs[2])
            for b in range(NB):
                jobs = STAGE["PB"][3 * (PT + b):3 * (PT + b) + 3]
                act.wait_ge(mtr_full[1], b + 1)
                if b:
                    act.wait_ge(ms_full, b)
                nc.scalar.copy(kTsM[:, :, P:2 * P], sc_all[:, 1, :].rearrange("p (h t) -> p h t", h=H))\
                    .then_inc(mts_copied[1], 1)
                branch(jobs[0])
                act.wait_ge(m_max, PT + b + 1)
                if b:
                    act.wait_ge(tr_full, TRN["ms", b - 1] + 1)
                nc.scalar.activation(PsM[0:32, :], sc_all[0:32, 2, 0:NMEM], ACT.Exp, bias=nmx[0:32, 0:1],
                                     accum_out=psum_r[0:32, 0:1]).then_inc(m_exp, 1)
                branch(jobs[1])
                tr_wait("ms", b)
                if b:
                    act.wait_ge(om_full, PT + b)
                else:
                    act.wait_ge(atsm_zero, 1)
                for kb in range(2):
                    last = nc.scalar.copy(batch_columns(aTsM, kb),
                                          TR[:, 32 * kb:32 * kb + 32].rearrange("p (h q) -> p h q", h=H))
                last.then_inc(tr_free, 1)
                branch(jobs[2])

            for n in STAGE["PM"]:
                kind, _, f, c = JOBS[n]
                branch(n)
                if kind == "up" and f == 0:
                    hv_wait_full(act, n)
                    t = slice(CH[c][0], CH[c][0] + CH[c][1])
                    for x in range(KW // 2):
                        last = nc.scalar.copy(mz_hi[x][:, :, t], mzT[:, 2 * x:2 * x + 2, t])
                    last.then_inc(mz_high, 1)

            hv_wait_full(act, STAGE["PM"][-1])
            act.wait_ge(wo_in, 16 * len(OUT_W))
            for k in range(KD):
                nc.scalar.copy(wo_hi[k // 2][:, k % 2, :], w_out[k]).then_inc(wo_high, 1)
            act.wait_ge(madd_done, 2 * 3 * KD)
            for r in range(2, PT + 1):
                n = ROWS_TILE(r)
                if r >= 4:
                    hv_wait_full(act, STAGE["O"][2 * (r - 2) + 1])
                    act.wait_ge(mt_split, r - 3)
                nc.scalar.copy(m_hi[r % 2][:, :, 0:n], merged[:, :, r * P:r * P + n]).then_inc(mt_high, 1)

        @block.vector
        def _(dve):
            steps = [0]

            def settle(ins):
                steps[0] += 1
                ins.then_inc(dve_step, 1)
                dve.wait_ge(dve_step, steps[0])

            def heavy(n):
                job = JOBS[n]
                bank = HV[n % 2]
                if job[0] == "rows":
                    _, kind, r = job
                    if kind not in NORMED:
                        return
                    rows = P if kind == "mk" else ROWS_TILE(r)
                    m, wd = NJ.index(n), NORMED[kind]
                    g = W // wd
                    dst = nrm_of(n)[0:rows, :].rearrange("p (g d) -> p g d", g=g)
                    dve.wait_ge(sq_done, m + 1)
                    nc.vector.reduce_sum(gstat[0:rows, 0, 0:g], sq[0:rows, :].rearrange("p (g d) -> p g d", g=g),
                                         axis=AX.X).then_inc(gsum_done, 1)
                    dve.wait_ge(groot_done, m + 1)
                    settle(nc.vector.reciprocal(gstat[0:rows, 2, 0:g], gstat[0:rows, 1, 0:g]))
                    if m >= 2:
                        dve.wait_ge(tr_full, TRN["norm", NJ[m - 2]] + 1)
                        if NJ[m - 2] in KJ:
                            dve.wait_ge(rows_out[m % 2], 16 * sum(1 for x in KJ if x < n and NJ.index(x) % 2 == m % 2))
                    nc.vector.tensor_tensor(out=dst, in0=bank[0:rows, :].rearrange("p (g d) -> p g d", g=g),
                                            in1=bc(gstat[0:rows, 2, 0:g], wd), op=ALU.mult).then_inc(hv_free[n % 2], 1)
                    if n in KJ:
                        hv_wait_free(dve, n)
                        row = (gka_row if kind == "k" else gkm_row)[0:rows, :]
                        nc.vector.tensor_tensor(out=dst, in0=dst,
                                                in1=row.unsqueeze(1).to_broadcast([rows, g, wd]),
                                                op=ALU.mult).then_inc(nrm_done, 1)
                elif job[0] == "cols":
                    _, kind, f, c = job
                    if n not in ZJ:
                        return
                    c0, cw = CH[c]
                    m = ZJ.index(n)
                    dve.wait_ge(tanh_done, sum(1 for x in ZJ[:m + 1] if JOBS[x][0] == "cols"))
                    nc.vector.scalar_tensor_tensor(out=z_of(kind)[:, f, c0:c0 + cw], in0=tanh[m % 2][:, 0:cw],
                                                   scalar=1.0, in1=bank[:, 0:cw], op0=ALU.add, op1=ALU.mult)\
                        .then_inc(hv_free[n % 2], 1)

                elif job[0] == "up":
                    _, br, f, c = job
                    c0, cw = CH[c]
                    hv_wait_full(dve, n)
                    hv_wait_free(dve, n - 1)
                    m = ZJ.index(n - 1)
                    if br == 0:
                        out = merged[:, f, c0:c0 + cw]
                    else:
                        x = 3 * KD * (br - 1) + 3 * f + c
                        if x >= 2:
                            dve.wait_ge(madd_done, x - 1)
                        out = tmp[x % 2][:, 0:cw]
                    nc.vector.scalar_tensor_tensor(out=out, in0=tanh[m % 2][:, 0:cw], scalar=1.0,
                                                   in1=bank[:, 0:cw], op0=ALU.add, op1=ALU.mult)                        .then_inc(hv_free[n % 2], 1)
                elif job[0] == "out":
                    _, r, j = job
                    rows = ROWS_TILE(r)
                    hv_wait_full(dve, n)
                    if j == 0:
                        dve.wait_ge(xr_in[r % 2], 16 * (r // 2 + 1))
                        if r >= 2:
                            dve.wait_ge(y_out[r % 2], 16 * (r // 2))
                    nc.vector.tensor_tensor(out=y_row[r % 2][0:rows, j * W:(j + 1) * W], in0=bank[0:rows, :],
                                            in1=x_res[r % 2][0:rows, j * W:(j + 1) * W], op=ALU.add)                        .then_inc(hv_free[n % 2], 1)

            def x_normed(t):
                rows = TILES[t][1]
                dve.wait_ge(root_done, t + 1)
                settle(nc.vector.reciprocal(rstat[0:rows, 2:3], rstat[0:rows, 1:2]))
                if t:
                    dve.wait_ge(xt_full, 2 * t)
                nc.vector.tensor_scalar(xn[0:rows, :], x_in[t % 2][0:rows, :], rstat[0:rows, 2:3], None,
                                        ALU.mult).then_inc(xn_done, 1)

            def x_evict(t):
                rows = TILES[t][1]
                for j in range(2):
                    dve.wait_ge(xt_full, 2 * t + j + 1)
                    src = sc_all[:, j, :].rearrange("p (k t) -> p k t", k=4)[:, :, 0:rows]
                    g = (gmem if t < NMT else gx)[:, 4 * j:4 * j + 4]
                    dst = (hT_mem[:, 4 * j:4 * j + 4, t * P:(t + 1) * P] if t < NMT else
                           hT[:, 4 * j:4 * j + 4, (t - NMT) * P:(t - NMT) * P + rows])
                    nc.vector.tensor_tensor(out=dst, in0=src, in1=bc(g, rows), op=ALU.mult).then_inc(xt_done, 1)

            nc.vector.memset(eps[:, :], EPS).then_inc(eps_ready, 1)
            x_normed(0)
            dve.wait_ge(first_in, 48)
            x_evict(0)
            dve.wait_ge(consts_in, 16 * N_CONSTS)
            settle(nc.vector.tensor_scalar(gcol[:, GQA:GQA + 1], gcol[:, GQA:GQA + 1], 0.125, None, ALU.mult))
            settle(nc.vector.tensor_scalar(gcol[:, GQM:GQM + 1], gcol[:, GQM:GQM + 1], P ** -0.5, None, ALU.mult))
            settle(nc.vector.tensor_scalar(gcol[:, GOA:GOA + 1], gcol[:, GOA:GOA + 1], 0.25 * (1.0 - LAM_INIT), None, ALU.mult))
            settle(nc.vector.tensor_scalar(gcol[:, GOB:GOB + 1], gcol[:, GOB:GOB + 1], 0.25, None, ALU.mult))
            for i in range(2):
                settle(nc.vector.tensor_tensor(out=nrm[1][:, 0:64], in0=nrm[0][:, 128 * i:128 * i + 64],
                                               in1=nrm[0][:, 128 * i + 64:128 * i + 128], op=ALU.mult))
                settle(nc.vector.reduce_sum(lam_sum[:, i:i + 1], nrm[1][:, 0:64], axis=AX.X))
            nc.vector.tensor_copy(lam_sum[:, 2:4], lam_sum[:, 0:2]).then_inc(consts_ready, 1)

            def low(out, whole, high):
                return nc.vector.tensor_tensor(out=out, in0=whole, in1=high.bitcast(F32), op=ALU.subtract)

            def low_projection(i):
                dve.wait_ge(wx_high, i + 1)
                for x in range(2):
                    last = low(wx_lo[i][x], wX[i][:, 4 * x:4 * x + 4, :], wx_hi[i][x])
                last.then_inc(wx_split, 1)

            def low_tile(r):
                hv_wait_full(dve, V_JOBS[r])
                dve.wait_ge(x_high, r + 1)
                for hi, lo, whole in tile_pairs(r):
                    last = low(lo, whole, hi)
                last.then_inc(x_split, 1)

            def whole_tile(r):
                hv_wait_full(dve, K_JOBS[r])
                for hi, lo, whole in tile_pairs(r):
                    last = nc.vector.tensor_tensor(out=whole, in0=hi.bitcast(F32), in1=lo.bitcast(F32), op=ALU.add)
                last.then_inc(x_whole, 1)

            for n in STAGE["X"]:
                kind, r = JOBS[n][1], JOBS[n][2]
                nxt = kind in ("mk", "v") and (t := r + (0 if kind == "mk" else NMT)) + 1 < NT
                if nxt:
                    x_normed(t + 1)
                if kind == "k":
                    whole_tile(r)
                heavy(n)
                if nxt:
                    x_evict(t + 1)
                if kind == "mv":
                    low_projection(r)
                if n == V_JOBS[0]:
                    low_tile(0)
                if n == V_JOBS[-1] or kind == "k" and r + 1 < PT:
                    low_tile(PT if n == V_JOBS[-1] else r + 1)
                if kind == "q" and r == PT:
                    dve.wait_ge(alibi_in, 16)
                    for h in range(H):
                        nc.vector.tensor_scalar(alibi[:, h, :], distance, 2.0 ** (-8.0 * (h + 1) / H), None,
                                                ALU.mult).then_inc(alibi_ready, 1)

            def o_ready(k):
                if k < PT:
                    dve.wait_ge(pv_done, H * (k + 1))
                elif k == PT:
                    dve.wait_ge(os_full, 1)
                elif k <= 2 * PT:
                    dve.wait_ge(o_full, k - PT)
                else:
                    dve.wait_ge(vb_done, NB)

            def tail_copy(k):
                n, _ = tail_of(k)
                o_ready(k)
                if k:
                    dve.wait_ge(tail_done, k)
                nc.vector.tensor_copy(og[:, 0:H * n], OB[:, 0:H * n]).then_inc(o_free, 1)

            def sample_rows_copy(i, done, count):
                dve.wait_ge(done, count)
                nc.vector.tensor_copy((otok, otokM)[i][0:NS_TOK, :], OB[0:NS_TOK, :]).then_inc(otok_ready, 1)

            def tail_final(k, heads):
                n, z = tail_of(k)
                g = GOA if k <= PT else GOB
                h0, h1 = heads
                roots, out = rs_t[:, h0 * n:h1 * n], og[:, h0 * n:h1 * n]
                if h0 == 0:
                    dve.wait_ge(tr_free, TRN["mean", k] + 1)
                    if k <= PT:
                        c = min((k * P + n - 1) // CHW, 2)
                        for x in range(2):
                            hv_wait_free(dve, STAGE["A"][0] + KW * (c + 1) - 1 - x)
                    else:
                        hv_wait_free(dve, STAGE["Z"][-1])
                settle(nc.vector.reciprocal(roots, roots))
                settle(nc.vector.scalar_tensor_tensor(out=out, in0=out, scalar=gcol[:, g:g + 1], in1=roots,
                                                      op0=ALU.mult, op1=ALU.mult))
                ins = nc.vector.tensor_tensor(out=z[:, h0:h1], in0=z[:, h0:h1],
                                              in1=out.rearrange("p (h t) -> p h t", h=h1 - h0), op=ALU.mult)
                if h1 == H:
                    ins.then_inc(tail_done, 1)

            def softmax_head(u):
                i, h = u // H, u % H
                nk = (i + 1) * P
                if u >= 2:
                    dve.wait_ge(tr_full, TRN["a", u - 2, groups_A(u - 2)[-1][0]] + 1)
                if u:
                    dve.wait_ge(p_ready, u)
                for c in range(2):
                    dve.wait_ge(sc_full, 2 * u + c + 1)
                    nc.vector.tensor_tensor_reduce(
                        out=S[u % 2][:, c, 0:nk], in0=alibi[:, h, NP_TOK - nk:NP_TOK],
                        in1=sc_all[:, 2 * c:2 * c + 2, :].rearrange("p a n -> p (a n)")[:, 0:nk],
                        scale=1.0, scalar=NEG, op0=ALU.add, op1=ALU.max,
                        accum_out=mx[:, c:c + 1]).then_inc(sc_read, 1)
                dve.wait_ge(sc_read, 2 * u + 2)
                nc.vector.tensor_scalar(nmx[:, 0:2], mx[:, 0:2], -1.0, None, ALU.mult).then_inc(nmx_ready, 1)

            def combine(u):
                nk = (u // H + 1) * P
                dve.wait_ge(p_ready, u + 1)
                settle(nc.vector.reciprocal(coef[:, 0:2], psum_r[:, 0:2]))
                settle(nc.vector.tensor_scalar(coef[:, 1:2], coef[:, 1:2], neg_lam[:, :], None, ALU.mult))
                p0, p1 = S[u % 2][:, 0, 0:nk], S[u % 2][:, 1, 0:nk]
                settle(nc.vector.tensor_scalar(p0, p0, coef[:, 0:1], None, ALU.mult))
                nc.vector.scalar_tensor_tensor(out=p0, in0=p1, scalar=coef[:, 1:2], in1=p0, op0=ALU.mult,
                                               op1=ALU.add).then_inc(a_ready, 1)

            def sample_head(b):
                P_ = Ps[b % 2]
                if b >= 2:
                    dve.wait_ge(tr_full, TRN["s", b - 2] + 1)
                else:
                    dve.wait_ge(pv_done, NU - 1)
                dve.wait_ge(p_ready, NU + b)
                dve.wait_ge(ss_full, b + 1)
                settle(nc.vector.tensor_tensor_reduce(
                    out=P_[0:64, 0:PAST], in0=past_t[0:64, :], in1=sc_all[0:64, 2, 0:PAST], scale=1.0, scalar=NEG,
                    op0=ALU.add, op1=ALU.max, accum_out=mx[0:64, 0:1]))
                nc.vector.tensor_tensor_reduce(
                    out=P_[0:64, PAST:NSK], in0=new_t[0:64, b, :], in1=sc_all[0:64, 2, PAST:NSK], scale=1.0,
                    scalar=mx[0:64, 0:1], op0=ALU.add, op1=ALU.max, accum_out=mx[0:64, 1:2]).then_inc(ss_read, 1)
                dve.wait_ge(ss_read, b + 1)
                nc.vector.tensor_scalar(nmx[0:64, 0:1], mx[0:64, 1:2], -1.0, None, ALU.mult).then_inc(nmx_ready, 1)

            def sample_scale(b):
                dve.wait_ge(p_ready, NU + b + 1)
                settle(nc.vector.reciprocal(coef[0:64, 0:1], psum_r[0:64, 0:1]))
                nc.vector.tensor_scalar(Ps[b % 2][0:64, :], Ps[b % 2][0:64, :], coef[0:64, 0:1], wrow[0:64, :],
                                        ALU.mult, ALU.mult).then_inc(a_ready, 1)

            def page_evict(b, dst, g):
                dve.wait_ge(ktr_full[g], b + 1)
                nc.vector.tensor_copy(dst[:, :, g * P:(g + 1) * P], sc_all[:, g, :].rearrange("p (h t) -> p h t", h=H))\
                    .then_inc(kts_copied[g], 1)

            def lambdas():
                dve.wait_ge(lam_exp, 1)
                settle(nc.vector.tensor_tensor(out=lam_sum[:, 0:1], in0=lam_sum[:, 3:4], in1=lam_sum[:, 2:3], op=ALU.subtract))
                settle(nc.vector.tensor_scalar(neg_lam[:, :], lam_sum[:, 0:1], LAM_INIT, None, ALU.subtract))
                nc.vector.scalar_tensor_tensor(out=wrow[:, :], in0=small["map"][:, 1:2], scalar=neg_lam[:, :],
                                               in1=small["map"][:, 0:1], op0=ALU.mult, op1=ALU.add)

            dve.wait_ge(alibi_ready, H)
            for u in range(STEPS_A + 1):
                jobs = heavy_A(u) if u < STEPS_A else []
                if u < NU:
                    softmax_head(u)
                elif u == NU:
                    page_evict(0, kTsA[0], 0)
                elif u < STEPS_A:
                    sample_head(u - NU)
                    if u - NU + 1 < NB:
                        page_evict(u - NU + 1, kTsA[(u - NU + 1) % 2], 0)
                for n in jobs:
                    heavy(n)
                if u == 0:
                    lambdas()
                if u < NU:
                    combine(u)
                elif NU < u < STEPS_A:
                    sample_scale(u - NU)
                for x, heads in enumerate(((0, 1), (1, 2), (2, H))):
                    if u - x in MEAN_AT:
                        tail_final(MEAN_AT[u - x], heads)
                if u in COPY_AT:
                    tail_copy(COPY_AT[u])
                if u == NU:
                    dve.wait_ge(tabs_in, 32)
                    sample_head(0)
                    page_evict(1, kTsA[1], 0)
                    sample_scale(0)
            sample_rows_copy(0, pv_done, NU + NB)
            tail_copy(PT)

            dve.wait_ge(pv_done, NU + NB)
            tail_final(PT, (0, H))
            for c, (c0, cw) in enumerate(CH):
                for k in range(2):
                    x = 2 * c + k
                    dve.wait_ge(lg_full, x + 1)
                    nc.vector.tensor_scalar(bb[:, k, c0:c0 + cw], sc_all[:, x % 4, 0:cw], ba_col[:, k:k + 1], 0.0,
                                            ALU.add, ALU.min)
                    nc.vector.tensor_scalar(lsig[:, k, c0:c0 + cw], sc_all[:, x % 4, 0:cw], ba_col[:, k:k + 1],
                                            None, ALU.add).then_inc(lg_read, 1)
            dve.wait_ge(lsig_done, 1)
            settle(nc.vector.tensor_tensor(out=bb, in0=bb, in1=lsig, op=ALU.subtract))
            dve.wait_ge(gw_in, 32)
            for k in range(2):
                settle(nc.vector.tensor_tensor_scan(out=bb[:, k, :], data0=keep, data1=bb[:, k, :], initial=0.0,
                                                    op0=ALU.mult, op1=ALU.add))

            def tile_views(r):
                n, L = ROWS_TILE(r), (GC if r < PT else QB)
                t = slice(r * P, r * P + n)
                return n, L, bb[:, :, t], gqT[:, :, t], gkT[:, :, t]

            def decay_start(r):
                n, L, b, _, _ = tile_views(r)
                b4 = b.rearrange("p k (c l) -> p k c l", l=L)
                for k in range(2):
                    last = nc.vector.tensor_tensor(out=edel[:, k, 0:n].rearrange("p (c l) -> p c l", l=L),
                                                   in0=bc(b4[:, k, :, L - 1], L), in1=b4[:, k], op=ALU.subtract)
                last.then_inc(gd_in, 1)

            def decay_apply(r):
                n, L, b, q, kk = tile_views(r)
                dve.wait_ge(gd_exp, r + 1)
                if r:
                    dve.wait_ge(tr_full, TRN["kd", r - 1] + 1)
                nc.vector.tensor_tensor(out=kd[:, :, 0:n], in0=kk, in1=edel[:, :, 0:n], op=ALU.mult).then_inc(kd_ready, 1)
                if r:
                    dve.wait_ge(o_full, r)
                for x in range(2):
                    for j in range((n + GC - 1) // GC):
                        t = slice(GC * j, GC * (j + 1))
                        last = nc.vector.scalar_tensor_tensor(out=qe[:, j, x, :, t], in0=q[:, :, t],
                                                              scalar=half_t[:, x:x + 1], in1=dlt[:, :, t],
                                                              op0=ALU.mult, op1=ALU.mult)
                settle(last)

            def level_operands(r, lc, L, ref, diag):
                n, _, b, q, kk = tile_views(r)
                x = lc % 2
                b4 = b.rearrange("p k (c l) -> p k c l", l=L)
                for k in range(2):
                    last = nc.vector.tensor_tensor(out=dlt[:, k, 0:n].rearrange("p (c l) -> p c l", l=L), in0=b4[:, k],
                                                   in1=bc(b4[:, k, :, ref], L), op=ALU.subtract)
                settle(last)
                d = dlt[:, :, 0:n]
                if diag:
                    nc.vector.tensor_scalar(dq[:, :, 0:n], d, CLIP, -CLIP, ALU.min, ALU.max)
                    nc.vector.tensor_scalar(dk[:, :, 0:n], d, CLIP, -CLIP, ALU.min, ALU.max).then_inc(lv_in, 1)
                else:
                    nc.vector.tensor_scalar(dq[:, :, 0:n], d, 0.0, None, ALU.min)
                    nc.vector.tensor_scalar(dk[:, :, 0:n], d, 0.0, None, ALU.max).then_inc(lv_in, 1)
                dve.wait_ge(lv_exp, lc + 1)
                if lc >= 2:
                    dve.wait_ge(at_full, lc - 1)
                nc.vector.tensor_tensor(out=kz[x][:, :, 0:n], in0=kk, in1=dk[:, :, 0:n], op=ALU.mult)
                for y in range(2):
                    last = nc.vector.scalar_tensor_tensor(out=qz[x][:, y, :, 0:n], in0=q, scalar=half_t[:, y:y + 1],
                                                          in1=dq[:, :, 0:n], op0=ALU.mult, op1=ALU.mult)
                last.then_inc(lv_ready, 1)

            def masked_add(r, lc, mask, first, final):
                n = ROWS_TILE(r)
                dve.wait_ge(at_full, lc + 1)
                if first and r:
                    dve.wait_ge(o_full, r)
                src = sc_all[0:n, lc % 2, 0:H * n].rearrange("p (h t) -> p h t", h=H)
                mk_ = gmask[0:n, mask, 0:n].unsqueeze(1).to_broadcast([n, H, n])
                dst = att if first else atm
                nc.vector.tensor_tensor(out=dst[0:n, :, 0:n], in0=src, in1=mk_, op=ALU.mult).then_inc(masked, 1)
                dve.wait_ge(masked, lc + 1)
                if not first:
                    ins = nc.vector.tensor_tensor(out=att[:, :, :], in0=att[:, :, :], in1=atm[:, :, :], op=ALU.add)
                    if final:
                        ins.then_inc(att_ready, 1)
                    else:
                        settle(ins)

            def split_keys(r, j, count, sel):
                n = ROWS_TILE(r)
                if count >= 2 * PT + 2:
                    dve.wait_ge(bu_full, count - 2 * PT - 1)
                nc.vector.tensor_scalar(kdz[j][0:n, :, :].rearrange("p k d -> p (k d)"), kdt[0:n, :], sel, None,
                                        ALU.mult).then_inc(kdz_ready, 1)

            def state_step(new, old, c, bank, done):
                for k in range(2):
                    for x in range(2):
                        p = slice(64 * x, 64 * x + 64)
                        last = nc.vector.scalar_tensor_tensor(
                            out=new[p, k, :], in0=old[p, k, :], scalar=dec[p, k, c:c + 1],
                            in1=sc_all[p, bank, 256 * k + P * x:256 * k + P * (x + 1)], op0=ALU.mult, op1=ALU.add)
                last.then_inc(done, 1)

            nc.vector.memset(St[0], 0.0).then_inc(st_zero, 1)
            nc.vector.memset(qe, 0.0).then_inc(st_zero, 1)
            for n in STAGE["Z"]:
                heavy(n)
            dve.wait_ge(st_zero, 2)
            level_operands(0, 0, *LEVELS[0][:2], True)
            decay_start(0)
            for r in range(PT):
                jobs = STAGE["PA"][5 * r:5 * r + 5]
                decay_apply(r)
                heavy(jobs[0])
                heavy(jobs[1])
                dve.wait_ge(tr_free, TRN["kd", r] + 1)
                if r:
                    dve.wait_ge(u_full, 2 * r)
                for j in range(2):
                    split_keys(r, j, 2 * r + j, half_t[:, j:j + 1])
                level_operands(r, 3 * r + 1, *LEVELS[1][:2], False)
                heavy(jobs[2])
                masked_add(r, 3 * r, 0, True, False)
                level_operands(r, 3 * r + 2, *LEVELS[2][:2], False)
                if r:
                    tail_final(PT + r, (0, 2))
                heavy(jobs[3])
                for j in range(2):
                    c = 2 * r + j
                    dve.wait_ge(u_full, c + 1)
                    if c:
                        dve.wait_ge(st_ready, c)
                    state_step(St[(c + 1) % 3], St[c % 3], j, 2 + j, st_ready)
                masked_add(r, 3 * r + 1, 1, False, False)
                masked_add(r, 3 * r + 2, 2, False, True)
                level_operands(r + 1, 3 * r + 3, *(LEVELS if r + 1 < PT else LEVELS_S)[0][:2], True)
                decay_start(r + 1)
                if r:
                    tail_final(PT + r, (2, H))
                heavy(jobs[4])
                tail_copy(PT + 1 + r)
            jobs = STAGE["PA"][5 * PT:]
            r = PT
            decay_apply(r)
            heavy(jobs[0])
            masked_add(r, 3 * PT, 3, True, False)
            dve.wait_ge(tr_free, TRN["kd", r] + 1)
            dve.wait_ge(u_full, 2 * PT)
            for b in range(2):
                split_keys(r, b, 2 * PT + b, batch_t[0:NS_TOK, b:b + 1])
            for b in range(NB):
                if b:
                    heavy(jobs[b])
                dve.wait_ge(bu_full, b + 1)
                dve.wait_ge(st_in[(2 + b) % 3], 16 * (b // 3 + 1))
                state_step(St[(2 + b) % 3], St[(2 + b) % 3], b, 2 + b % 2, bst_ready)
                if b + 2 < NB:
                    split_keys(r, b % 2, 2 * PT + b + 2, batch_t[0:NS_TOK, b + 2:b + 3])
                if b < 2:
                    tail_final(2 * PT, (2 * b, 2 * b + 2))
            tail_copy(2 * PT + 1)

            heavy(STAGE["MZ"][0])
            tail_final(2 * PT + 1, (0, H))
            for n in list(STAGE["MZ"])[1:]:
                heavy(n)

            def low_weights(br, f):
                i = LOAD_OF[("pair", br, f)]
                slot = ring[i % 2]
                dve.wait_ge(wh_high, weights_number(br, f) + 1)
                for x in range(2):
                    last = low(wg_lo[i % 2][:, 4 * x:4 * x + 4, :], slot[:, 512 * x:512 * (x + 1)]
                               .rearrange("p (k n) -> p k n", k=KD // 2), wg_hi[f % 2][x])
                if br == 2 and f:
                    last = low(wu_lo[i % 2], slot[:, 1024:1536].rearrange("p (k n) -> p k n", k=KW), wu_hi[i % 2])
                last.then_inc(w_split, 1)

            def branch(n):
                heavy(n)
                kind, br, f, c = JOBS[n]
                if kind == "up" and c == 0 and (br, f) != (2, KD - 1):
                    low_weights(*((br, f + 1) if f + 1 < KD else (2, 0)))

            dve.wait_ge(h_high, KD)
            for r, n in enumerate(STAGE["Q"]):
                heavy(n)
                if r == PT:
                    hv_wait_full(dve, n)
                t = slice(r * P, r * P + ROWS_TILE(r))
                for x in range(KD // 2):
                    last = low(h_lo[x][:, :, t], hT[:, 2 * x:2 * x + 2, t], h_hi[x][:, :, t])
                last.then_inc(h_split, 1)
                if r == 2:
                    low_weights(1, 0)

            def m_maxima(i, src, rows, k):
                if i:
                    dve.wait_ge(m_exp, i)
                settle(nc.vector.reduce_max(mx[0:rows, 0:k], src, axis=AX.X))
                nc.vector.tensor_scalar(nmx[0:rows, 0:k], mx[0:rows, 0:k], -1.0, None, ALU.mult).then_inc(m_max, 1)

            def m_max_of(i):
                dve.wait_ge(m_full, i + 1)
                m_maxima(i, sc_all[:, 2 * (i % 2):2 * (i % 2) + 2, :].rearrange("p a n -> p (a n)")
                         .rearrange("p (h m) -> p h m", h=H), P, H)

            def m_weights(i):
                dve.wait_ge(m_exp, i + 1)
                settle(nc.vector.reciprocal(coef[:, :], psum_r[:, :]))
                for h in range(H):
                    last = nc.vector.tensor_scalar(Pm[:, h, :], Pm[:, h, :], coef[:, h:h + 1], None, ALU.mult)
                last.then_inc(m_ready, 1)

            def m_tail(k):
                n = ROWS_TILE(k)
                if k < PT:
                    dve.wait_ge(om_full, k + 1)
                else:
                    dve.wait_ge(os_full, 2)
                z = mzT[:, :, k * P:k * P + n]
                nc.vector.scalar_tensor_tensor(out=z, in0=o_view(OB, n), scalar=0.25, in1=z, op0=ALU.mult,
                                               op1=ALU.mult).then_inc(mt_done, 1)

            m_max_of(0)
            for i in range(PT):
                jobs = STAGE["PB"][3 * i:3 * i + 3]
                m_weights(i)
                branch(jobs[0])
                if i + 1 < PT:
                    m_max_of(i + 1)
                branch(jobs[1])
                branch(jobs[2])
                m_tail(i)
            nc.vector.memset(aTsM, 0.0).then_inc(atsm_zero, 1)
            for b in range(NB):
                jobs = STAGE["PB"][3 * (PT + b):3 * (PT + b) + 3]
                dve.wait_ge(mtr_full[0], b + 1)
                if b:
                    dve.wait_ge(ms_full, b)
                nc.vector.tensor_copy(kTsM[:, :, 0:P], sc_all[:, 0, :].rearrange("p (h t) -> p h t", h=H))\
                    .then_inc(mts_copied[0], 1)
                branch(jobs[0])
                dve.wait_ge(ms_full, b + 1)
                m_maxima(PT + b, sc_all[0:32, 2, 0:NMEM], 32, 1)
                dve.wait_ge(m_exp, PT + b + 1)
                settle(nc.vector.reciprocal(coef[0:32, 0:1], psum_r[0:32, 0:1]))
                nc.vector.tensor_scalar(PsM[0:32, :], PsM[0:32, :], coef[0:32, 0:1], None, ALU.mult).then_inc(m_ready, 1)
                branch(jobs[1])
                branch(jobs[2])
            sample_rows_copy(1, om_full, PT + NB)
            m_tail(PT)

            for n in STAGE["PM"]:
                kind, _, f, c = JOBS[n]
                branch(n)
                if kind == "up" and f == 0:
                    t = slice(CH[c][0], CH[c][0] + CH[c][1])
                    dve.wait_ge(mz_high, c + 1)
                    for x in range(KW // 2):
                        last = low(mz_lo[x][:, :, t], mzT[:, 2 * x:2 * x + 2, t], mz_hi[x][:, :, t])
                    last.then_inc(mz_split, 1)

            for k in range(KD // 2):
                dve.wait_ge(wo_high, k + 1)
                low(wo_lo[k // 2][:, k % 2, :], w_out[k], wo_hi[k // 2][:, k % 2, :]).then_inc(wo_split, 1)
            heavy(STAGE["O"][0])
            for k in range(KD // 2, KD):
                dve.wait_ge(wo_high, k + 1)
                low(wo_lo[k // 2][:, k % 2, :], w_out[k], wo_hi[k // 2][:, k % 2, :]).then_inc(wo_split, 1)
            heavy(STAGE["O"][1])
            for r in range(1, PT + 1):
                if r < PT:
                    n = ROWS_TILE(r + 1)
                    dve.wait_ge(mt_high, r)
                    low(m_lo[(r + 1) % 2][:, :, 0:n], merged[:, :, (r + 1) * P:(r + 1) * P + n],
                        m_hi[(r + 1) % 2][:, :, 0:n]).then_inc(mt_split, 1)
                heavy(STAGE["O"][2 * r])
                heavy(STAGE["O"][2 * r + 1])


_INS = ["x_prompt", "x_sample", "cache_k_a", "cache_v_a", "page_table", "state_gla", "cache_mem_k",
        "cache_mem_v", "mem_prompt", "norm_x", "w_in", "g_qa", "g_ka", "lam", "g_oa", "w_a2", "b_a",
        "g_ob", "g_qm", "g_km", "norm_mem", "w_mkv", "w_branch", "w_o"]
_OUTS = [(1, NP_TOK, D), (NB, QB, D), (1, 1, NP_TOK, H, P), (1, 1, NP_TOK, H, P),
         (1, NB, QB, H, P), (1, NB, QB, H, P), (1, 1, H, 64, P), (1, NB, H, 64, P),
         (1, 1, NMEM, H, P), (1, 1, NMEM, H, P)]


def kernel(**inputs):
    import concourse.bacc as bacc
    from concourse.bass_utils import run_bass_kernel_spmd

    nc = bacc.Bacc("TRN2", target_bir_lowering=False, num_devices=1)
    arrays, args, outs = {}, [], []
    for name in _INS:
        a = np.ascontiguousarray(inputs[name])
        arrays[name] = a
        args.append(nc.dram_tensor(name, a.shape, mybir.dt.from_np(a.dtype), kind="ExternalInput").ap())
    tabs = {}
    for name, a in shape_tables().items():
        arrays["tab_" + name] = a
        tabs[name] = nc.dram_tensor("tab_" + name, a.shape, F32, kind="ExternalInput").ap()
    for i, shape in enumerate(_OUTS):
        outs.append(nc.dram_tensor(f"out_{i}", shape, F32, kind="ExternalOutput").ap())
    hybrid_step(nc, *args, tabs, *outs)
    r = run_bass_kernel_spmd(nc, [arrays], core_ids=[0])
    return tuple(r.results[0][f"out_{i}"] for i in range(len(_OUTS)))
```
